# Optimizing a Trainium2 kernel written in Bass

```python
import jax
import jax.numpy as jnp
from jax import lax
import numpy as np
import math
import jax, jax.numpy as jnp

D_MODEL = 1024
BATCH = 1
SEQ = 256
DEPTH = 1

ATT_HEADS = 8
ATT_KV_HEADS = 2
ATT_GROUP = ATT_HEADS // ATT_KV_HEADS
ATT_HEAD_DIM = 64
WINDOW = 128
ATT_BLOCK = 128
ROPE_DIM = ATT_HEAD_DIM // 4
ROPE_THETA = 500000.0

RET_HEADS = 4
RET_KEY_DIM = 128
RET_VAL_DIM = 256
RET_CHUNK = 128
RET_ROT_BASE = 10000.0

D_FF = 4 * D_MODEL

NORM_EPS = 1e-6
GN_EPS = 1e-6
NEG_INF = -1e30

ATT_Q_W = ATT_HEADS * ATT_HEAD_DIM
ATT_KV_W = ATT_KV_HEADS * ATT_HEAD_DIM
RET_QK_W = RET_HEADS * RET_KEY_DIM
RET_V_W = RET_HEADS * RET_VAL_DIM
IN_SPLITS = (ATT_Q_W, ATT_KV_W, ATT_KV_W, RET_QK_W, RET_QK_W, RET_V_W, RET_V_W, D_MODEL, D_MODEL)
IN_WIDTH = sum(IN_SPLITS)
IN_OFFSETS = tuple(int(v) for v in np.cumsum(IN_SPLITS)[:-1])


def rmsnorm(x, gain):
    xf = x.astype(jnp.float32)
    y = xf * lax.rsqrt(jnp.mean(xf * xf, axis=-1, keepdims=True) + NORM_EPS)
    return (y * gain.astype(jnp.float32)).astype(x.dtype)

def rope_tables(seq_len, dim, theta):
    pos = jnp.arange(seq_len, dtype=jnp.float32)
    inv_freq = theta ** (-jnp.arange(0, dim, 2, dtype=jnp.float32) / dim)
    ang = pos[:, None] * inv_freq[None, :]
    return jnp.cos(ang)[:, None, :], jnp.sin(ang)[:, None, :]

def apply_rope(x, cos, sin):
    xf = x.astype(jnp.float32)
    x1, x2 = jnp.split(xf, 2, axis=-1)
    out = jnp.concatenate([x1 * cos - x2 * sin, x2 * cos + x1 * sin], axis=-1)
    return out.astype(x.dtype)

def partial_rope(x, cos, sin):
    return jnp.concatenate([apply_rope(x[..., :ROPE_DIM], cos, sin), x[..., ROPE_DIM:]], axis=-1)

def sliding_window_sink_attention(q, k, v, sinks):
    b, s, _, dh = q.shape
    c = ATT_BLOCK
    nb = s // c
    qb = q.reshape(b, nb, c, ATT_KV_HEADS, ATT_GROUP, dh)
    kb = k.reshape(b, nb, c, ATT_KV_HEADS, dh)
    vb = v.reshape(b, nb, c, ATT_KV_HEADS, dh)

    def with_prev(t):
        prev = jnp.concatenate([jnp.zeros_like(t[:, :1]), t[:, :-1]], axis=1)
        return jnp.concatenate([prev, t], axis=2)

    kw, vw = with_prev(kb), with_prev(vb)
    scores = jnp.einsum('bnqhgd,bnkhd->bnhgqk', qb, kw,
                        preferred_element_type=jnp.float32) * (dh ** -0.5)
    qi = jnp.arange(c)[:, None] + c
    kj = jnp.arange(2 * c)[None, :]
    delta = qi - kj
    in_window = (delta >= 0) & (delta < WINDOW)
    has_prev = (jnp.arange(nb) > 0)[:, None, None] | (kj >= c)[None]
    mask = in_window[None] & has_prev
    scores = jnp.where(mask[None, :, None, None], scores, NEG_INF)
    sink = sinks.astype(jnp.float32).reshape(ATT_KV_HEADS, ATT_GROUP)[None, None, :, :, None, None]
    sink = jnp.broadcast_to(sink, scores.shape[:-1] + (1,))
    probs = jax.nn.softmax(jnp.concatenate([scores, sink], axis=-1), axis=-1)[..., :-1]
    out = jnp.einsum('bnhgqk,bnkhd->bnqhgd', probs.astype(v.dtype), vw)
    return out.reshape(b, s, ATT_HEADS * dh)

def chunkwise_retention(q, k, v):
    b, s, h, dk = q.shape
    dv = v.shape[-1]
    c = RET_CHUNK
    nc = s // c
    log_gamma = jnp.log1p(-jnp.exp2(-5.0 - jnp.arange(h, dtype=jnp.float32)))
    idx = jnp.arange(c, dtype=jnp.float32)
    diff = idx[:, None] - idx[None, :]
    intra = jnp.where(diff >= 0, jnp.exp(jnp.maximum(diff, 0.0) * log_gamma[:, None, None]), 0.0)
    q_decay = jnp.exp((idx + 1.0)[None, :] * log_gamma[:, None])[..., None]
    k_decay = jnp.exp((c - 1.0 - idx)[None, :] * log_gamma[:, None])[..., None]
    chunk_decay = jnp.exp(c * log_gamma)[:, None, None]

    def to_chunks(t):
        return t.astype(jnp.float32).reshape(b, nc, c, h, t.shape[-1]).transpose(1, 0, 3, 2, 4)

    qc, kc, vc = to_chunks(q), to_chunks(k), to_chunks(v)

    def step(state, inp):
        qi, ki, vi = inp
        att = jnp.einsum('bhqd,bhkd->bhqk', qi, ki) * intra
        inner = jnp.einsum('bhqk,bhkv->bhqv', att, vi)
        cross = jnp.einsum('bhqd,bhdv->bhqv', qi * q_decay, state)
        new_state = state * chunk_decay + jnp.einsum('bhkd,bhkv->bhdv', ki * k_decay, vi)
        return new_state, inner + cross

    state0 = jnp.zeros((b, h, dk, dv), jnp.float32)
    _, out = lax.scan(step, state0, (qc, kc, vc))
    return out.transpose(1, 0, 3, 2, 4).reshape(b, s, h, dv)

def head_groupnorm(y, gain):
    b, s, h, dv = y.shape
    mu = jnp.mean(y, axis=-1, keepdims=True)
    var = jnp.mean(jnp.square(y - mu), axis=-1, keepdims=True)
    yn = (y - mu) * lax.rsqrt(var + GN_EPS)
    return yn.reshape(b, s, h * dv) * gain.astype(jnp.float32)

def mixer_block(xn, w_in, b_gates, attn_sinks, ret_gn_gain, w_att_up, w_ret_up, w_out, att_rope, ret_rope):
    b, s, _ = xn.shape
    proj = jnp.einsum('bsd,dn->bsn', xn, w_in)
    q_a, k_a, v_a, q_r, k_r, v_r, g_r, gate_a, gate_r = jnp.split(proj, IN_OFFSETS, axis=-1)

    q_a = partial_rope(q_a.reshape(b, s, ATT_HEADS, ATT_HEAD_DIM), *att_rope)
    k_a = partial_rope(k_a.reshape(b, s, ATT_KV_HEADS, ATT_HEAD_DIM), *att_rope)
    v_a = v_a.reshape(b, s, ATT_KV_HEADS, ATT_HEAD_DIM)
    y_a = sliding_window_sink_attention(q_a, k_a, v_a, attn_sinks) @ w_att_up

    q_r = apply_rope(q_r.reshape(b, s, RET_HEADS, RET_KEY_DIM), *ret_rope)
    k_r = apply_rope(k_r.reshape(b, s, RET_HEADS, RET_KEY_DIM), *ret_rope) * (RET_KEY_DIM ** -0.5)
    ret = chunkwise_retention(q_r, k_r, v_r.reshape(b, s, RET_HEADS, RET_VAL_DIM))
    ret = head_groupnorm(ret, ret_gn_gain)
    y_r = (jax.nn.silu(g_r.astype(jnp.float32)) * ret).astype(xn.dtype) @ w_ret_up

    bg = b_gates.astype(jnp.float32)
    ga = jax.nn.sigmoid(gate_a.astype(jnp.float32) + bg[:D_MODEL])
    gr = jax.nn.sigmoid(gate_r.astype(jnp.float32) + bg[D_MODEL:])
    merged = (ga * y_a.astype(jnp.float32) + gr * y_r.astype(jnp.float32)).astype(xn.dtype)
    return merged @ w_out

def squared_relu_mlp(xn, w_ff1, w_ff2):
    hdn = jnp.square(jax.nn.relu(xn @ w_ff1))
    return hdn @ w_ff2

def first_inputs(seed: int = 0) -> dict:
    key = jax.random.key(seed)
    ks = jax.random.split(key, 14)
    f32 = jnp.float32

    def normal(k, shape, scale):
        return jax.random.normal(k, shape, f32) * scale

    def gain(k, shape):
        return 1.0 + 0.02 * jax.random.normal(k, shape, f32)

    return {
        'x': normal(ks[0], (BATCH, SEQ, D_MODEL), 1.0),
        'norm_mix_gain': gain(ks[1], (DEPTH, D_MODEL)),
        'w_in': normal(ks[2], (DEPTH, D_MODEL, IN_WIDTH), D_MODEL ** -0.5),
        'b_gates': normal(ks[3], (DEPTH, 2 * D_MODEL), 0.1),
        'attn_sinks': normal(ks[4], (DEPTH, ATT_HEADS), 0.5),
        'ret_gn_gain': gain(ks[5], (DEPTH, RET_V_W)),
        'w_att_up': normal(ks[6], (DEPTH, ATT_Q_W, D_MODEL), ATT_Q_W ** -0.5),
        'w_ret_up': normal(ks[7], (DEPTH, RET_V_W, D_MODEL), RET_V_W ** -0.5),
        'w_out': normal(ks[8], (DEPTH, D_MODEL, D_MODEL), D_MODEL ** -0.5),
        'norm_mlp_gain': gain(ks[9], (DEPTH, D_MODEL)),
        'w_ff1': normal(ks[10], (DEPTH, D_MODEL, D_FF), D_MODEL ** -0.5),
        'w_ff2': normal(ks[11], (DEPTH, D_FF, D_MODEL), D_FF ** -0.5),
        'norm_final_gain': gain(ks[12], (D_MODEL,)),
    }

def first_block(x, norm_mix_gain, w_in, b_gates, attn_sinks, ret_gn_gain, w_att_up, w_ret_up, w_out,
              norm_mlp_gain, w_ff1, w_ff2, norm_final_gain):
    s = x.shape[1]
    att_rope = rope_tables(s, ROPE_DIM, ROPE_THETA)
    ret_rope = rope_tables(s, RET_KEY_DIM, RET_ROT_BASE)
    h = x
    for l in range(DEPTH):
        h = h + mixer_block(rmsnorm(h, norm_mix_gain[l]), w_in[l], b_gates[l], attn_sinks[l],
                            ret_gn_gain[l], w_att_up[l], w_ret_up[l], w_out[l], att_rope, ret_rope)
        h = h + squared_relu_mlp(rmsnorm(h, norm_mlp_gain[l]), w_ff1[l], w_ff2[l])
    return rmsnorm(h, norm_final_gain)


HEAD_DIM = 64
BLOCK = 128
N_META = 16
META_PAD = BLOCK - N_META
ROPE_THETA_2 = 10000.0
RMS_EPS = 1e-6
NEG_INF_2 = -1e30

SWA_Q_HEADS = 16
SWA_KV_HEADS = 4
SWA_GROUP = SWA_Q_HEADS // SWA_KV_HEADS
SWA_WIDTH = SWA_Q_HEADS * HEAD_DIM

DIFF_HEADS = 8
DIFF_V_DIM = 2 * HEAD_DIM
DIFF_WIDTH = DIFF_HEADS * DIFF_V_DIM

D_FF_2 = ((8 * D_MODEL // 3 + 255) // 256) * 256

QA_COLS = SWA_Q_HEADS * HEAD_DIM
KA_COLS = SWA_KV_HEADS * HEAD_DIM
VA_COLS = SWA_KV_HEADS * HEAD_DIM
QB_COLS = DIFF_HEADS * 2 * HEAD_DIM
KB_COLS = DIFF_HEADS * 2 * HEAD_DIM
VB_COLS = DIFF_WIDTH
GATE_COLS = 2 * D_MODEL
IN_COLS = QA_COLS + KA_COLS + VA_COLS + QB_COLS + KB_COLS + VB_COLS + GATE_COLS
SPLITS = (
    QA_COLS,
    QA_COLS + KA_COLS,
    QA_COLS + KA_COLS + VA_COLS,
    QA_COLS + KA_COLS + VA_COLS + QB_COLS,
    QA_COLS + KA_COLS + VA_COLS + QB_COLS + KB_COLS,
    QA_COLS + KA_COLS + VA_COLS + QB_COLS + KB_COLS + VB_COLS,
)


def rms_norm(x, g):
    xf = x.astype(jnp.float32)
    y = xf * lax.rsqrt(jnp.mean(xf * xf, axis=-1, keepdims=True) + RMS_EPS)
    return (y * g.astype(jnp.float32)).astype(x.dtype)

def rope(x, pos):
    d = x.shape[-1]
    half = d // 2
    inv_freq = ROPE_THETA_2 ** (-jnp.arange(0, d, 2, dtype=jnp.float32) / d)
    ang = pos.astype(jnp.float32)[:, None] * inv_freq[None, :]
    shape = (1, x.shape[1]) + (1,) * (x.ndim - 3) + (half,)
    cos = jnp.cos(ang).reshape(shape)
    sin = jnp.sin(ang).reshape(shape)
    xf = x.astype(jnp.float32)
    x1, x2 = xf[..., :half], xf[..., half:]
    return jnp.concatenate([x1 * cos - x2 * sin, x2 * cos + x1 * sin], axis=-1).astype(x.dtype)

def windowed_gqa_sink_attention(q, k, v, sink, pos, is_real):
    B, Lp = q.shape[0], q.shape[1]
    nb = Lp // BLOCK
    scale = HEAD_DIM ** -0.5
    k_meta = k[:, META_PAD:BLOCK]
    v_meta = v[:, META_PAD:BLOCK]
    padw = ((0, 0), (BLOCK, BLOCK), (0, 0), (0, 0))
    k_p = jnp.pad(k, padw)
    v_p = jnp.pad(v, padw)
    pos_p = jnp.pad(pos, (BLOCK, BLOCK))
    real_p = jnp.pad(is_real, (BLOCK, BLOCK))
    qb = q.reshape(B, nb, BLOCK, SWA_KV_HEADS, SWA_GROUP, HEAD_DIM).transpose(1, 0, 2, 3, 4, 5)
    sink_g = sink.astype(jnp.float32).reshape(SWA_KV_HEADS, SWA_GROUP)

    def one_block(args):
        i, qi = args
        start = i * BLOCK
        kb = lax.dynamic_slice_in_dim(k_p, start, 3 * BLOCK, axis=1)
        vb = lax.dynamic_slice_in_dim(v_p, start, 3 * BLOCK, axis=1)
        kpos = lax.dynamic_slice_in_dim(pos_p, start, 3 * BLOCK)
        kreal = lax.dynamic_slice_in_dim(real_p, start, 3 * BLOCK)
        qpos = lax.dynamic_slice_in_dim(pos, start, BLOCK)
        mask = kreal[None, :] & (jnp.abs(qpos[:, None] - kpos[None, :]) <= WINDOW)
        s_band = jnp.einsum('bqhgd,bkhd->bhgqk', qi, kb).astype(jnp.float32) * scale
        s_band = jnp.where(mask, s_band, NEG_INF_2)
        s_meta = jnp.einsum('bqhgd,bmhd->bhgqm', qi, k_meta).astype(jnp.float32) * scale
        s_sink = jnp.broadcast_to(sink_g[None, :, :, None, None], s_meta.shape[:-1] + (1,))
        p = jax.nn.softmax(jnp.concatenate([s_band, s_meta, s_sink], axis=-1), axis=-1)
        p_band = p[..., :3 * BLOCK].astype(v.dtype)
        p_meta = p[..., 3 * BLOCK:3 * BLOCK + N_META].astype(v.dtype)
        return (jnp.einsum('bhgqk,bkhd->bqhgd', p_band, vb)
                + jnp.einsum('bhgqm,bmhd->bqhgd', p_meta, v_meta))

    o = lax.map(one_block, (jnp.arange(nb), qb))
    return o.transpose(1, 0, 2, 3, 4, 5).reshape(B, Lp, SWA_WIDTH)

def differential_attention(q, k, v, lam, lambda_init, subln_gain, is_key):
    B, Lp = q.shape[0], q.shape[1]
    nb = Lp // BLOCK
    scale = HEAD_DIM ** -0.5
    key_bias = jnp.where(is_key, 0.0, NEG_INF_2).astype(jnp.float32)
    qb = q.reshape(B, nb, BLOCK, DIFF_HEADS, 2, HEAD_DIM).transpose(1, 0, 2, 3, 4, 5)

    def one_block(qi):
        s = jnp.einsum('bqhcd,bkhcd->bhcqk', qi, k).astype(jnp.float32) * scale + key_bias
        p = jax.nn.softmax(s, axis=-1)
        a = (p[:, :, 0] - lam * p[:, :, 1]).astype(v.dtype)
        return jnp.einsum('bhqk,bkhe->bqhe', a, v)

    o = lax.map(one_block, qb)
    o = o.transpose(1, 0, 2, 3, 4).reshape(B, Lp, DIFF_HEADS, DIFF_V_DIM)
    o = rms_norm(o, subln_gain) * (1.0 - lambda_init)
    return o.reshape(B, Lp, DIFF_WIDTH).astype(v.dtype)

def second_inputs(seed: int = 0) -> dict:
    key = jax.random.key(seed)
    ks = jax.random.split(key, 20)
    f32 = jnp.float32

    def nrm(k, shape, scale):
        return jax.random.normal(k, shape, f32) * scale

    def gain(k, shape):
        return 1.0 + 0.02 * jax.random.normal(k, shape, f32)

    return {
        "x": nrm(ks[0], (BATCH, SEQ, D_MODEL), 1.0),
        "meta_tokens": nrm(ks[1], (N_META, D_MODEL), 1.0),
        "pre_mix_gain": gain(ks[2], (DEPTH, D_MODEL)),
        "w_in": nrm(ks[3], (DEPTH, D_MODEL, IN_COLS), D_MODEL ** -0.5),
        "b_gate": nrm(ks[4], (DEPTH, GATE_COLS), 0.1),
        "attn_sink": nrm(ks[5], (DEPTH, SWA_Q_HEADS), 0.5),
        "lambda_q1": nrm(ks[6], (DEPTH, HEAD_DIM), 0.1),
        "lambda_k1": nrm(ks[7], (DEPTH, HEAD_DIM), 0.1),
        "lambda_q2": nrm(ks[8], (DEPTH, HEAD_DIM), 0.1),
        "lambda_k2": nrm(ks[9], (DEPTH, HEAD_DIM), 0.1),
        "diff_subln_gain": gain(ks[10], (DEPTH, DIFF_V_DIM)),
        "w_branch_swa": nrm(ks[11], (DEPTH, SWA_WIDTH, D_MODEL), SWA_WIDTH ** -0.5),
        "w_branch_diff": nrm(ks[12], (DEPTH, DIFF_WIDTH, D_MODEL), DIFF_WIDTH ** -0.5),
        "w_out": nrm(ks[13], (DEPTH, D_MODEL, D_MODEL), D_MODEL ** -0.5),
        "post_mix_gain": gain(ks[14], (DEPTH, D_MODEL)),
        "pre_ffn_gain": gain(ks[15], (DEPTH, D_MODEL)),
        "w_ffn_in": nrm(ks[16], (DEPTH, D_MODEL, 2 * D_FF_2), D_MODEL ** -0.5),
        "w_ffn_out": nrm(ks[17], (DEPTH, D_FF_2, D_MODEL), D_FF_2 ** -0.5),
        "post_ffn_gain": gain(ks[18], (DEPTH, D_MODEL)),
    }

def second_block(x, meta_tokens, pre_mix_gain, w_in, b_gate, attn_sink, lambda_q1, lambda_k1,
              lambda_q2, lambda_k2, diff_subln_gain, w_branch_swa, w_branch_diff, w_out,
              post_mix_gain, pre_ffn_gain, w_ffn_in, w_ffn_out, post_ffn_gain):
    B = x.shape[0]
    filler = jnp.zeros((B, META_PAD, D_MODEL), x.dtype)
    meta = jnp.broadcast_to(meta_tokens[None].astype(x.dtype), (B, N_META, D_MODEL))
    h = jnp.concatenate([filler, meta, x], axis=1)
    Lp = h.shape[1]
    pos = jnp.arange(Lp, dtype=jnp.int32) - META_PAD
    is_real = pos >= N_META
    is_key = pos >= 0

    for l in range(DEPTH):
        lambda_init = 0.8 - 0.6 * math.exp(-0.3 * l)
        u = rms_norm(h, pre_mix_gain[l])
        proj = u @ w_in[l]
        qa, ka, va, qb, kb, vb, g = jnp.split(proj, SPLITS, axis=-1)
        qa = rope(qa.reshape(B, Lp, SWA_Q_HEADS, HEAD_DIM), pos)
        ka = rope(ka.reshape(B, Lp, SWA_KV_HEADS, HEAD_DIM), pos)
        va = va.reshape(B, Lp, SWA_KV_HEADS, HEAD_DIM)
        qb = rope(qb.reshape(B, Lp, DIFF_HEADS, 2, HEAD_DIM), pos)
        kb = rope(kb.reshape(B, Lp, DIFF_HEADS, 2, HEAD_DIM), pos)
        vb = vb.reshape(B, Lp, DIFF_HEADS, DIFF_V_DIM)

        o_swa = windowed_gqa_sink_attention(qa, ka, va, attn_sink[l], pos, is_real)
        lam = (jnp.exp(jnp.sum(lambda_q1[l].astype(jnp.float32) * lambda_k1[l].astype(jnp.float32)))
               - jnp.exp(jnp.sum(lambda_q2[l].astype(jnp.float32) * lambda_k2[l].astype(jnp.float32)))
               + lambda_init)
        o_diff = differential_attention(qb, kb, vb, lam, lambda_init, diff_subln_gain[l], is_key)

        gates = jax.nn.sigmoid(g + b_gate[l])
        g_swa, g_diff = gates[..., :D_MODEL], gates[..., D_MODEL:]
        merged = g_swa * (o_swa @ w_branch_swa[l]) + g_diff * (o_diff @ w_branch_diff[l])
        h = h + rms_norm(merged @ w_out[l], post_mix_gain[l])

        u = rms_norm(h, pre_ffn_gain[l])
        gate_up = u @ w_ffn_in[l]
        f = (jax.nn.silu(gate_up[..., :D_FF_2]) * gate_up[..., D_FF_2:]) @ w_ffn_out[l]
        h = h + rms_norm(f, post_ffn_gain[l])

    return h[:, BLOCK:]


def setup_inputs(seed=0):
    out = dict(first_inputs(seed))
    for name, value in second_inputs(seed + 1).items():
        if name != "x":
            out[name + "_2"] = value
    return out


def reference(
    x, norm_mix_gain, w_in, b_gates, attn_sinks, ret_gn_gain, w_att_up, w_ret_up, w_out,
    norm_mlp_gain, w_ff1, w_ff2, norm_final_gain, meta_tokens_2, pre_mix_gain_2, w_in_2,
    b_gate_2, attn_sink_2, lambda_q1_2, lambda_k1_2, lambda_q2_2, lambda_k2_2,
    diff_subln_gain_2, w_branch_swa_2, w_branch_diff_2, w_out_2, post_mix_gain_2,
    pre_ffn_gain_2, w_ffn_in_2, w_ffn_out_2, post_ffn_gain_2,
):
    x = first_block(
        x, norm_mix_gain, w_in, b_gates, attn_sinks, ret_gn_gain, w_att_up, w_ret_up, w_out,
        norm_mlp_gain, w_ff1, w_ff2, norm_final_gain,
    )
    return second_block(
        x, meta_tokens_2, pre_mix_gain_2, w_in_2, b_gate_2, attn_sink_2, lambda_q1_2,
        lambda_k1_2, lambda_q2_2, lambda_k2_2, diff_subln_gain_2, w_branch_swa_2,
        w_branch_diff_2, w_out_2, post_mix_gain_2, pre_ffn_gain_2, w_ffn_in_2, w_ffn_out_2,
        post_ffn_gain_2,
    )


_drawn_inputs = setup_inputs


def setup_inputs(seed=0):
    import zlib

    import numpy as np

    out = dict(_drawn_inputs(seed))
    spreads = {}
    factors = {'norm_mix_gain': 3.626,
     'b_gates': 4.217,
     'attn_sinks': 8.0,
     'ret_gn_gain': 8.0,
     'norm_mlp_gain': 3.228,
     'pre_mix_gain_2': 3.163,
     'attn_sink_2': 64.0,
     'lambda_q1_2': 3.784,
     'lambda_k1_2': 2.708,
     'diff_subln_gain_2': 10.998,
     'post_mix_gain_2': 3.594,
     'pre_ffn_gain_2': 3.339,
     'post_ffn_gain_2': 17.004}
    for name, (base, spread) in spreads.items():
        noise = np.random.default_rng([zlib.crc32(name.encode()), seed]).standard_normal(out[name].shape)
        drawn = base * np.exp(spread * noise) if base else spread * noise
        out[name] = jnp.asarray(drawn.astype(out[name].dtype))
    for name, factor in factors.items():
        out[name] = (out[name] * factor).astype(out[name].dtype)
    return out
```

```python
from contextlib import ExitStack

import numpy as np

import concourse.bass as bass
from concourse import mybir

F32 = mybir.dt.float32
F32R = mybir.dt.float32r
ALU = mybir.AluOpType
ACT = mybir.ActivationFunctionType
AX = mybir.AxisListType

P = 128
D = 1024
TOK = 256
NT = TOK // P
KC = D // P
BANK = 512
BLOB = 2048
EPS = 1e-6
NEG = -1e30

A_HEADS, A_DIM, A_ROPE, A_WINDOW = 8, 64, 16, 128
R_HEADS, R_KEY, R_VAL = 4, 128, 256
FF1 = 4096
N_META = 16
S_HEADS, S_KV, DH = 16, 4, 64
F_HEADS = 8
FF2 = 2816
LAMBDA = 0.8 - 0.6
KEYS = TOK + N_META

MIX1 = 2 + 1 + 2 + 2 + 4 + 4 + 4 + 4 + 2 + 4 + 4
STEP1 = FF1 // 512
N1 = MIX1 + 4 * STEP1
OUT2 = 34
U0, S_UNITS, UNITS = 22, 16, 32
MIX2 = 2 + 4 + 4 + 4 + 4 + 4 + 4 + 4 + 4 + 4
STEP2 = FF2 // 256
F2 = N1 + MIX2
NBLOB = F2 + 3 * STEP2

CONST = {}
for _name, _width in (("ident", P), ("neghalf", 2), ("a_cos", NT * A_ROPE), ("a_sin", NT * A_ROPE),
                      ("ge", P), ("zero", P), ("diag2", P), ("negone", 6),
                      ("h_cos", (NT + 1) * DH), ("h_sin", (NT + 1) * DH),
                      ("gt", P), ("diag1", P), ("ret_cos", NT * P), ("ret_sin", NT * P),
                      ("decay", R_HEADS * 3 * P)):
    CONST[_name] = (sum(w for _, w in CONST.values()), _width)
NCONST = sum(w for _, w in CONST.values())

COLS = {}
for _name, _width in (("norm_mix", KC), ("norm_mlp", KC), ("ret_gn", KC), ("b_gates", 2 * KC),
                      ("pre_mix", KC), ("b_gate_2", 2 * KC), ("pre_ffn", KC), ("subln", 1)):
    COLS[_name] = (sum(w for _, w in COLS.values()), _width)
NCOLS = sum(w for _, w in COLS.values())

ROWS = {}
for _name, _width in (("sinks", A_HEADS * 2), ("sinks_2", S_HEADS), ("lambdas", 4 * DH)):
    ROWS[_name] = (sum(w for _, w in ROWS.values()), _width)
NROWS = sum(w for _, w in ROWS.values())


def slot_of(n):
    return n % 4 if n < N1 else 1 + (n - N1) % 3


def depth_of(n):
    return 4 if n < N1 else 3


def used_before(n):
    return n - 3 if n < N1 + 3 else n - 2


def fills(n):
    if n < N1:
        return n // 4 + 1
    return (N1 - 1) // 4 + 1 + (n - N1) // 3


def build(nc, w, x, meta, consts, cols, rows, grow, out):
    with ExitStack() as ctx:
        def sem(name):
            return ctx.enter_context(nc.semaphore(name))

        base = (nc.sbuf_base + 127) // 128 * 128
        top = [0]

        def at(name, shape, dt, offset):
            return nc.alloc_sbuf_tensor_at(name, shape, dt, offset=base + 4 * offset)

        def new(name, shape, dt=F32):
            size = (int(np.prod(shape[1:])) + 7) // 8 * 8
            top[0] += size
            assert base + 4 * top[0] <= nc.sbuf_usable_end, (name, top[0])
            return at(name, shape, dt, top[0] - size)

        raw, whi, wlo = [None] * 4, [None] * 4, [None] * 4
        for s in range(4):
            raw[s] = new(f"raw{s}", [P, BLOB])
            whi[s] = new(f"whi{s}", [P, BLOB], F32R)
            wlo[s] = new(f"wlo{s}", [P, BLOB], F32R)
        xT_h = new("xT_h", [P, KC, TOK], F32R)
        xT_l = new("xT_l", [P, KC, TOK], F32R)
        h = new("h", [P, NT, D])
        cst_at = top[0]
        cst = new("cst", [P, NCONST])
        col = new("col", [P, NCOLS])
        row = new("row", [P, NROWS])
        stat = new("stat", [P, 8])
        soft = new("soft", [P, 2, 5, 4])
        gn_stat = new("gn_stat", [P, 2, NT, 6])
        gn_mv = new("gn_mv", [P, 2, NT, 2])
        gn_mid = new("gn_mid", [P, 2, NT])
        gn_r = new("gn_r", [P, 2, NT])
        metaT_h = new("metaT_h", [P, KC, N_META], F32R)
        metaT_l = new("metaT_l", [P, KC, N_META], F32R)
        metaT = new("metaT", [P, KC, N_META])
        mstat = new("mstat", [N_META, 4])
        usoft = new("usoft", [P, 2, 6, 2])
        lam = new("lam", [P, 4])
        neglam = new("neglam", [P, 1])
        subgain = new("subgain", [P, 1])
        ostat = new("ostat", [P, 2, 3])
        negsink = new("negsink", [P, 2 * A_HEADS + S_HEADS])
        region = top[0]

        def c(name):
            a, n = CONST[name]
            return cst[:, a:a + n]

        def cl(name, i=0, n=1):
            a = COLS[name][0] + i
            return col[:, a:a + n]

        xn = at("xn", [P, NT, D], F32, region)

        tok = [new("tok0", [P, NT, 512]), new("tok1", [P, NT, 512])]
        ka_tok = new("ka_tok", [P, NT, P])
        qaT = new("qaT", [P, 4, TOK])
        kaT = new("kaT", [P, 2, TOK])
        va = new("va", [P, NT, 2, P])
        qrT = new("qrT", [P, R_HEADS, TOK])
        krT = new("krT", [P, R_HEADS, TOK])
        vr_at = top[0]
        vr = new("vr", [P, R_HEADS, NT, R_VAL])
        gr_at = top[0]
        gr = new("gr", [P, R_HEADS, NT, R_VAL])
        gate_a = new("gate_a", [P, KC, TOK])
        gate_r = at("gate_r", [P, KC, TOK], F32, region)
        retT_h = at("retT_h", [P, KC, TOK], F32R, vr_at)
        retT_l = at("retT_l", [P, KC, TOK], F32R, gr_at)
        aT_h = new("aT_h", [P, 4, TOK], F32R)
        aT_l = new("aT_l", [P, 4, TOK], F32R)
        s1 = [new("s1a", [P, 2, TOK]), new("s1b", [P, 2, TOK])]
        s0 = [new("s0a", [P, 2, P]), new("s0b", [P, 2, P])]
        pT = new("pT", [P, 6, P])
        decayed_at = top[0]
        decayed = new("decayed", [P, 3 * P])
        scratch = new("scratch", [P, 512])
        end1 = top[0]

        top[0] = region + NT * D
        f_sq = [new("f_sq0", [P, 2, TOK]), new("f_sq1", [P, 2, TOK])]
        fT_h = [new("fT_h0", [P, 2, TOK], F32R), new("fT_h1", [P, 2, TOK], F32R)]
        fT_l = [new("fT_l0", [P, 2, TOK], F32R), new("fT_l1", [P, 2, TOK], F32R)]

        gain_row = new("gain_row", [P, D])
        meta_tok = new("meta_tok", [N_META, D])

        dead = cst_at + CONST["gt"][0]
        gate_s = at("gate_s", [P, KC, TOK], F32, dead)
        o_tok = [at("o_tok0", [P, P], F32, dead + KC * TOK), at("o_tok1", [P, P], F32, dead + KC * TOK + P)]
        top[0] = 0
        kbT = new("kbT", [P, 2 * F_HEADS, KEYS])
        ksT = new("ksT", [P, S_KV, KEYS])
        vs_meta = new("vs_meta", [N_META, 2, 2, P])
        o_junk = new("o_junk", [P, P])
        assert top[0] <= 3 * BLOB
        top[0] = region
        gate_d = at("gate_d", [P, KC, TOK], F32, region)
        tok2 = [new("tok2a", [P, NT, 512]), new("tok2b", [P, NT, 512])]
        dT_l = at("dT_l", [P, KC, TOK], F32R, top[0])
        ks_tok = new("ks_tok", [P, NT, 256])
        mk = [new("mk0", [N_META, 512]), new("mk1", [N_META, 512])]
        vs = new("vs", [P, NT, 2, 2, P])
        vb = new("vb", [P, NT, D])
        vb_meta = new("vb_meta", [N_META, D])
        dT_h = at("dT_h", [P, KC, TOK], F32R, top[0])
        qsT = new("qsT", [P, KC, TOK])
        gain_rows = at("gain_rows2", [P, 2, D], F32, top[0])
        qbT = new("qbT", [P, KC, TOK])
        sT_h = new("sT_h", [P, KC, TOK], F32R)
        sT_l = new("sT_l", [P, KC, TOK], F32R)
        sc = [new("sc0", [P, 2, KEYS]), new("sc1", [P, 2, KEYS])]
        puT = new("puT", [P, 4, P])
        pmT = new("pmT", [N_META, 2, P])
        scratch2 = new("scratch2", [P, 512])

        top[0] = region + NT * D
        g_act = new("g_act", [P, 2, TOK])
        gT_h = new("gT_h", [P, 2, TOK], F32R)
        gT_l = new("gT_l", [P, 2, TOK], F32R)

        ps = ctx.enter_context(nc.psum_tensor("ps", [P, 8, BANK], F32))
        acc = [ps[:, 4:6, :].rearrange("p a b -> p (a b)"), ps[:, 6:8, :].rearrange("p a b -> p (a b)")]

        raw_in = [sem(f"raw_in{s}") for s in range(4)]
        split_hi = sem("split_hi")
        split_lo = sem("split_lo")
        blob_used = sem("blob_used")
        x_in = sem("x_in")
        const_in = sem("const_in")
        row_in = sem("row_in")
        dve_step = sem("dve_step")
        act_step = sem("act_step")
        pool_step = sem("pool_step")
        init_ok = sem("init_ok")
        out_done = sem("out_done")
        sq0 = sem("sq0")
        sq1 = sem("sq1")
        rstd_ok = sem("rstd_ok")
        xn_a = sem("xn_a")
        xn_d = sem("xn_d")
        xt_ps = sem("xt_ps")
        xt_hi = sem("xt_hi")
        xt_lo = sem("xt_lo")
        h_ok = sem("h_ok")
        taken_a = sem("taken_a")
        taken_d = sem("taken_d")
        rope_ok = sem("rope_ok")
        q_ps = sem("q_ps")
        q_ok = sem("q_ok")
        sc_ps = sem("sc_ps")
        sc_ok = sem("sc_ok")
        ex_ok = sem("ex_ok")
        pr_ok = sem("pr_ok")
        pt_ps = sem("pt_ps")
        pt_a = sem("pt_a")
        pt_d = sem("pt_d")
        o_ps = sem("o_ps")
        o_hi = sem("o_hi")
        o_lo = sem("o_lo")
        at_ps = sem("at_ps")
        at_ok = sem("at_ok")
        ro_ps = sem("ro_ps")
        rv_ok = sem("rv_ok")
        rr_ok = sem("rr_ok")
        rn_ok = sem("rn_ok")
        rt_ps = sem("rt_ps")
        rt_hi = sem("rt_hi")
        rt_lo = sem("rt_lo")
        e_ok = sem("e_ok")
        mg_ok = sem("mg_ok")
        mg_hi = sem("mg_hi")
        mg_lo = sem("mg_lo")
        ff_relu = sem("ff_relu")
        ff_sq = sem("ff_sq")
        ff_hi = sem("ff_hi")
        ff_lo = sem("ff_lo")

        meta_in = sem("meta_in")
        meta_sq = sem("meta_sq")
        meta_r = sem("meta_r")
        meta_n = sem("meta_n")
        meta_ps = sem("meta_ps")
        meta_g = sem("meta_g")
        meta_hi = sem("meta_hi")
        meta_lo = sem("meta_lo")
        zero2 = sem("zero2")
        mtaken_a = sem("mtaken_a")
        mtaken_d = sem("mtaken_d")
        kt_ps = sem("kt_ps")
        kt_ok = sem("kt_ok")
        sv_ok = sem("sv_ok")
        lam_s = sem("lam_s")
        lam_ok = sem("lam_ok")
        lam_e = sem("lam_e")
        u_sc = sem("u_sc")
        u_max = sem("u_max")
        u_exp = sem("u_exp")
        u_pr = sem("u_pr")
        u_pt = sem("u_pt")
        u_ptd = sem("u_ptd")
        u_ptm = sem("u_ptm")
        u_o = sem("u_o")
        s_hi = sem("s_hi")
        s_lo = sem("s_lo")
        d_o = sem("d_o")
        d_n = sem("d_n")
        d_ps = sem("d_ps")
        d_hi = sem("d_hi")
        d_lo = sem("d_lo")
        rows_in = sem("rows_in")
        gs_ok = sem("gs_ok")
        g_one = sem("g_one")
        g_two = sem("g_two")
        g_hi = sem("g_hi")
        g_lo = sem("g_lo")

        steps = {"act": 0, "dve": 0, "pool": 0}
        chain = {"act": act_step, "dve": dve_step, "pool": pool_step}

        def link(eng, name, ins):
            steps[name] += 1
            ins.then_inc(chain[name], 1)
            eng.wait_ge(chain[name], steps[name])

        TAKERS = "aadd" + "aa" + "dd" + "aaaa" + "dd" + "dd" + "dddd" + "aa" + "ddd" + "aaaa" + "dd" + "dd"

        def wait_pair_free(pe, group):
            if group >= 2:
                who = TAKERS[group - 2]
                pe.wait_ge(taken_a if who == "a" else taken_d, 2 * TAKERS[:group - 1].count(who))

        def product(pe, o, lh, ll, rh, rl, first, last):
            pe.matmul(o, lh, rh, start=first, stop=False)
            pe.matmul(o, lh, rl, start=False, stop=False)
            return pe.matmul(o, ll, rh, start=False, stop=last)

        def multiply_tokens(pe, slot, k0, nk, width, bank0, first, last, xh, xl, chunk_wait=None, part=None,
                            meta_bank=None):
            vh = whi[slot][:].rearrange("p (k c) -> p k c", k=nk)
            vl = wlo[slot][:].rearrange("p (k c) -> p k c", k=nk)
            halves = max(1, width // BANK)
            wd = min(width, BANK)
            for k in range(nk) if part is None else range(part * nk // 2, (part + 1) * nk // 2):
                if chunk_wait is not None:
                    pe.wait_ge(xt_lo, chunk_wait + max(2, k0 + k + 1))
                for t in range(NT):
                    for half in range(halves):
                        m = product(pe, ps[:, bank0 + t * halves + half, 0:wd],
                                    xh[:, k0 + k, t * P:(t + 1) * P], xl[:, k0 + k, t * P:(t + 1) * P],
                                    vh[:, k, half * BANK:half * BANK + wd],
                                    vl[:, k, half * BANK:half * BANK + wd],
                                    first and k == 0, last and k == nk - 1)
            if meta_bank is not None:
                if chunk_wait is not None and part != 0:
                    pe.wait_ge(xt_lo, chunk_wait + KC)
                for k in range(nk) if part else []:
                    m = product(pe, ps[0:N_META, meta_bank, :], metaT_h[:, k0 + k, :], metaT_l[:, k0 + k, :],
                                vh[:, k, :], vl[:, k, :], first and k == 0, last and k == nk - 1)
            if part != 0:
                m.then_inc(blob_used, 1)

        def multiply_features(pe, slot, nk, ntile, bank0, xh, xl, chunk_wait=None, part=None):
            vh = whi[slot][:].rearrange("p (k c) -> p k c", k=nk)
            vl = wlo[slot][:].rearrange("p (k c) -> p k c", k=nk)
            for j in range(ntile) if part is None else range(part * ntile // 2, (part + 1) * ntile // 2):
                o = ps[:, bank0 + j // 2, (j % 2) * TOK:(j % 2 + 1) * TOK]
                for k in range(nk):
                    if chunk_wait is not None and j == 0:
                        pe.wait_ge(xt_lo, chunk_wait + max(2, k + 1))
                    m = product(pe, o, vh[:, k, j * P:(j + 1) * P], vl[:, k, j * P:(j + 1) * P],
                                xh[:, k, :], xl[:, k, :], k == 0, k == nk - 1)
            if part != 0:
                m.then_inc(blob_used, 1)

        block = ctx.enter_context(nc.Block())

        @block.sync
        def _(sp):
            def load(n, src, made):
                if made is not None:
                    sp.wait_ge(split_lo, made)
                sp.dma_start(raw[slot_of(n)][:], src).then_inc(raw_in[slot_of(n)], 16)

            for n in range(4):
                load(n, w[n], None)
            with sp.Fori(4, N1 - 4, 4) as i:
                for j in range(4):
                    load(j, w[bass.ds(i + j, 1)].rearrange("a p c -> (a p) c"), i + (j - 3))
            load(N1 - 1, w[N1 - 1], N1 - 1 - 3)
            whole = (NBLOB - N1) // 3 * 3
            with sp.Fori(N1, N1 + whole - 2, 3) as i:
                for j in range(3):
                    load(N1 + j, w[bass.ds(i + j, 1)].rearrange("a p c -> (a p) c"), i + (j - 2))
            for n in range(N1 + whole, NBLOB):
                load(n, w[n], n - 2)

        @block.scalar
        def _(act):
            act.dma_start(h[:], x).then_inc(x_in, 16)
            act.dma_start(cst[:], consts).then_inc(const_in, 16)
            act.dma_start(col[:], cols).then_inc(const_in, 16)
            act.dma_start(row[:], rows.partition_broadcast(P)).then_inc(const_in, 16)

            def hi(n, i=0, per=0):
                s, depth = slot_of(n), depth_of(n)
                act.wait_ge(raw_in[s], i * (16 * per // depth) + 16 * fills(n))
                if n >= 4:
                    act.wait_ge(blob_used, i * per + used_before(n))
                act.activation(whi[s][:], raw[s][:], ACT.Copy).then_inc(split_hi, 1)

            def square(src):
                act.activation(xn[:, 0, :], src, ACT.Square, accum_out=stat[:, 0:1]).then_inc(sq0, 1)

            def to_features(norm, r, gain):
                act.wait_ge(rstd_ok, norm)
                act.activation(xn[:, 0, :], h[:, 0, :], ACT.Copy, scale=stat[:, 4:5]).then_inc(xn_a, 1)
                for k in range(KC):
                    act.wait_ge(xt_ps, r * KC + k + 1)
                    act.activation(xT_h[:, k, :], ps[:, k, 0:TOK], ACT.Copy, scale=cl(gain, k)).then_inc(xt_hi, 1)

            def exp_pairs(j):
                act.wait_ge(sc_ok, j + 1)
                st = soft[:, j % 2]
                for u in range(2):
                    act.activation(s1[j % 2][:, u, :], s1[j % 2][:, u, :], ACT.Exp, bias=st[:, 1, u:u + 1],
                                   accum_out=st[:, 3, u:u + 1])
                for u in range(2):
                    act.activation(s0[j % 2][:, u, :], s0[j % 2][:, u, :], ACT.Exp, bias=st[:, 1, 2 + u:3 + u],
                                   accum_out=st[:, 3, 2 + u:3 + u])
                act.activation(st[:, 2, :], st[:, 2, :], ACT.Exp).then_inc(ex_ok, 1)

            def gate(bank, dst, func, scale, bias):
                for b in range(2):
                    for j in range(2):
                        m = act.activation(dst[:, 2 * b + j, :], ps[:, bank + b, j * TOK:(j + 1) * TOK],
                                           func, scale=scale, bias=bias(2 * b + j))
                    m.then_inc(taken_a, 1)

            def merged_hi(count, merged=gate_a):
                act.wait_ge(mg_ok, count + 1)
                i = count % 4
                act.activation(xT_h[:, 2 * i:2 * i + 2, :], merged[:, 2 * i:2 * i + 2, :],
                               ACT.Copy).then_inc(mg_hi, 1)

            act.wait_ge(x_in, 16)
            square(h[:, 0, :])
            act.wait_ge(const_in, 48)
            to_features(1, 0, "norm_mix")
            for n in range(3):
                hi(n)

            for n in range(MIX1):
                hi(n + 3)
                if n == 2:
                    act.wait_ge(blob_used, 2)
                    for t in range(NT):
                        act.activation(tok[0][:, t, :], ps[:, t, :], ACT.Copy).then_inc(taken_a, 1)
                if n == 3:
                    act.wait_ge(blob_used, 3)
                    act.wait_ge(init_ok, 3)
                    for t in range(NT):
                        act.activation(ka_tok[:, t, :], ps[:, 2 + t, 0:P], ACT.Copy)
                        act.activation(va[:, t, 0, 0:A_DIM], ps[:, 2 + t, P:P + A_DIM], ACT.Copy)
                        act.activation(va[:, t, 1, A_DIM:P], ps[:, 2 + t, P + A_DIM:2 * P],
                                       ACT.Copy).then_inc(taken_a, 1)
                if n == 4:
                    act.wait_ge(q_ps, 1)
                    for t in range(NT):
                        m = act.activation(qaT[:, :, t * P:(t + 1) * P],
                                           ps[:, 4 + t, :].rearrange("p (j q) -> p j q", j=4), ACT.Copy)
                    m.then_inc(q_ok, 1)
                    act.wait_ge(q_ps, 2)
                    act.activation(kaT[0:A_DIM, 0, :], ps[0:A_DIM, 6, 0:TOK], ACT.Copy)
                    act.activation(kaT[A_DIM:P, 1, :], ps[A_DIM:P, 6, 0:TOK], ACT.Copy).then_inc(q_ok, 1)
                if n in (7, 9):
                    dst, bank = (qrT, 4) if n == 7 else (krT, 6)
                    act.wait_ge(q_ps, 3 if n == 7 else 4)
                    for t in range(NT):
                        m = act.activation(dst[:, :, t * P:(t + 1) * P],
                                           ps[:, bank + t, :].rearrange("p (j q) -> p j q", j=4), ACT.Copy)
                    m.then_inc(q_ok, 1)
                if n in (9, 11):
                    act.wait_ge(blob_used, n)
                    hh = n - 9
                    for t in range(NT):
                        act.activation(vr[:, hh:hh + 2, t, :],
                                       ps[:, (n - 9) + t, :].rearrange("p (a v) -> p a v", a=2),
                                       ACT.Copy).then_inc(taken_a, 1)
                if n in (13, 15):
                    act.wait_ge(blob_used, n)
                    hh = n - 13
                    for t in range(NT):
                        act.activation(gr[:, hh:hh + 2, t, :],
                                       ps[:, (n - 13) + t, :].rearrange("p (a v) -> p a v", a=2),
                                       ACT.Sigmoid).then_inc(e_ok, 1)
                if n in (17, 19, 21, 23):
                    act.wait_ge(blob_used, n)
                    g = (n - 17) // 2
                    gate(2 * (g % 2), (gate_a if g < 2 else gate_r)[:, 4 * (g % 2):4 * (g % 2) + 4, :],
                         ACT.Sigmoid, 1.0, lambda j: cl("b_gates", 4 * g + j))
                if 12 <= n < 16:
                    j = n - 12
                    act.wait_ge(pt_ps, j + 1)
                    act.activation(pT[:, 4:6, :], ps[:, 7, 0:TOK].rearrange("p (a q) -> p a q", a=2),
                                   ACT.Copy).then_inc(pt_a, 1)
                if 13 <= n < 17:
                    j = n - 13
                    act.wait_ge(o_ps, j + 1)
                    act.activation(aT_h[:, j, :], ps[:, 7, TOK:2 * TOK], ACT.Copy).then_inc(o_hi, 1)
                if 10 <= n < 14:
                    exp_pairs(n - 10)
                if 18 <= n < 22:
                    r = n - 18
                    act.wait_ge(rt_ps, r + 1)
                    for j in range(2):
                        act.activation(retT_h[:, 2 * r + j, :], ps[:, 6, j * TOK:(j + 1) * TOK], ACT.Copy,
                                       scale=cl("ret_gn", 2 * r + j)).then_inc(rt_hi, 1)
                if 26 <= n < 30:
                    merged_hi(n - 26)
            act.wait_ge(h_ok, 1)
            square(h[:, 0, :])
            to_features(2, 1, "norm_mlp")

            def hidden_relu(k, used, made=None):
                if made is not None:
                    act.wait_ge(ff_lo, made)
                act.wait_ge(blob_used, used)
                act.activation(f_sq[k][:], ps[:, k, :].rearrange("p (a q) -> p a q", a=2), ACT.Relu).then_inc(ff_relu, 1)

            def hidden_hi(k, count):
                act.wait_ge(ff_sq, count)
                act.activation(fT_h[k][:], f_sq[k][:], ACT.Copy).then_inc(ff_hi, 1)

            act.dma_start(gain_row[:], grow[0].partition_broadcast(P)).then_inc(row_in, 16)
            act.dma_start(meta_tok[:], meta).then_inc(meta_in, 16)
            b = MIX1
            hi(b + 3)
            hi(b + 4)
            hidden_relu(0, b + 1)
            hidden_relu(1, b + 2)
            hidden_hi(0, 1)
            with act.Fori(0, STEP1 - 1) as i:
                b = MIX1 + 2
                hi(b + 3, i, 4)
                hidden_hi(1, i * 2 + 2)
                hi(b + 4, i, 4)
                hidden_relu(0, i * 4 + (b + 1), i * 2 + 1)
                hi(b + 5, i, 4)
                hidden_relu(1, i * 4 + (b + 2), i * 2 + 2)
                hi(b + 6, i, 4)
                hidden_hi(0, i * 2 + 3)
            b = N1 - 2
            hi(b + 3)
            hidden_hi(1, 2 * STEP1)
            act.wait_ge(meta_in, 16)
            act.activation(xn[0:N_META, 0, :], meta_tok[:], ACT.Square, accum_out=mstat[:, 0:1]).then_inc(meta_sq, 1)
            act.wait_ge(meta_r, 1)
            act.activation(meta_tok[:], meta_tok[:], ACT.Copy, scale=mstat[:, 2:3]).then_inc(meta_n, 1)
            hi(b + 4)
            act.wait_ge(meta_g, 1)
            act.activation(metaT_h[:], metaT[:], ACT.Copy).then_inc(meta_hi, 1)

            act.wait_ge(h_ok, 3)
            square(h[:, 0, :])

            act.wait_ge(h_ok, 5)
            square(h[:, 0, :])
            to_features(4, 2, "pre_mix")

            def copy_halves(dst, variant, bank):
                act.activation(dst[0:DH, variant, :], ps[0:DH, bank, 0:KEYS], ACT.Copy)
                return act.activation(dst[DH:P, variant + 1, :], ps[DH:P, bank, 0:KEYS], ACT.Copy)

            for q in range(2 * OUT2):
                m = q // 2
                if q == 4:
                    act.wait_ge(blob_used, N1 + 2)
                    act.wait_ge(zero2, 1)
                    for u in range(2):
                        for t in range(NT):
                            v = ps[:, t, 256:512].rearrange("p (a u d) -> p a u d", a=2, u=2)
                            act.activation(vs[:, t, :, u, u * DH:(u + 1) * DH], v[:, :, u, :], ACT.Copy)
                        v = ps[0:N_META, 6, 256:512].rearrange("p (a u d) -> p a u d", a=2, u=2)
                        ins = act.activation(vs_meta[:, :, u, u * DH:(u + 1) * DH], v[:, :, u, :], ACT.Copy)
                    ins.then_inc(sv_ok, 1)
                if q in (6, 10, 11, 14, 15):
                    r = (6, 10, 11, 14, 15).index(q)
                    act.wait_ge(kt_ps, r + 1)
                    for cc in range(2):
                        ins = copy_halves(*((ksT, 2 * cc) if r == 0 else (kbT, 4 * (r - 1) + 2 * cc)), 4 + cc)
                    ins.then_inc(kt_ok, 1)
                if q in (18, 30, 34, 38):
                    r = (18, 30, 34, 38).index(q)
                    g = (3, 6, 7, 8)[r]
                    act.wait_ge(q_ps, 5 + r)
                    for t in range(NT):
                        ins = act.activation(
                            (qsT if r < 2 else qbT)[:, 4 * (r % 2):4 * (r % 2) + 4, t * P:(t + 1) * P],
                            ps[:, 2 * (g % 2) + t, :].rearrange("p (j q) -> p j q", j=4), ACT.Copy)
                    ins.then_inc(q_ok, 1)
                if q in (20, 24):
                    half = (q - 20) // 4
                    act.wait_ge(blob_used, N1 + m)
                    for t in range(NT):
                        act.activation(vb[:, t, half * BANK:(half + 1) * BANK], ps[:, 2 * half + t, :],
                                       ACT.Copy).then_inc(taken_a, 1)
                    act.activation(vb_meta[:, half * BANK:(half + 1) * BANK], ps[0:N_META, 7 - half, :],
                                   ACT.Copy).then_inc(mtaken_a, 1)
                if q in (40, 44, 48, 52):
                    g = (q - 40) // 4
                    act.wait_ge(blob_used, N1 + m)
                    gate(2 * ((g + 1) % 2), (gate_s if g < 2 else gate_d)[:, 4 * (g % 2):4 * (g % 2) + 4, :],
                         ACT.Sigmoid, 1.0, lambda j: cl("b_gate_2", 4 * g + j))
                U = q - U0 - 3
                if 0 <= U < UNITS:
                    act.wait_ge(u_pt, U + 1)
                    heads = 2 if U < S_UNITS else 1
                    act.activation(pmT[:, 0:heads, :], ps[0:N_META, 7, 32:32 + heads * P].rearrange(
                        "p (a q) -> p a q", a=heads), ACT.Copy).then_inc(u_ptm, 1)
                U = q - U0 - 4
                if 0 <= U < UNITS:
                    act.wait_ge(u_o, U + 1)
                    cc, t = U % S_UNITS // 2, U % 2
                    if U < S_UNITS:
                        act.activation(sT_h[:, cc, t * P:(t + 1) * P], ps[:, 7, 288:288 + P],
                                       ACT.Copy).then_inc(s_hi, 1)
                    else:
                        if U - S_UNITS >= 2:
                            act.wait_ge(d_ps, U - S_UNITS - 1)
                        act.activation(o_junk[:], ps[:, 7, 288:288 + P], ACT.Square,
                                       accum_out=ostat[:, U % 2, 0:1])
                        act.activation(o_tok[U % 2][:], ps[:, 7, 288:288 + P], ACT.Copy).then_inc(d_o, 1)
                V = q - U0 - 6 - S_UNITS
                if 0 <= V < UNITS - S_UNITS:
                    act.wait_ge(d_ps, V + 1)
                    act.wait_ge(u_sc, min(UNITS, q - U0))
                    act.activation(dT_h[:, V // 2, V % 2 * P:(V % 2 + 1) * P], ps[:, 5, P:2 * P], ACT.Copy,
                                   scale=subgain[:]).then_inc(d_hi, 1)
                if q == 2:
                    act.wait_ge(lam_s, 1)
                    act.activation(lam[:, 2:4], lam[:, 0:2], ACT.Exp).then_inc(lam_e, 1)
                U = q - U0 - 1
                if 0 <= U < UNITS:
                    act.wait_ge(u_max, U + 1)
                    st = usoft[:, U % 2]
                    for u in range(2):
                        ins = act.activation(sc[U % 2][:, u, :], sc[U % 2][:, u, :], ACT.Exp,
                                             bias=st[:, 2, u:u + 1], accum_out=st[:, 4, u:u + 1])
                    if U < S_UNITS:
                        ins = act.activation(st[:, 3, :], st[:, 3, :], ACT.Exp)
                    ins.then_inc(u_exp, 1)
                if q == 2 * OUT2 - 8:
                    act.wait_ge(u_sc, UNITS)
                    act.dma_start(gain_rows[:], grow[1:3].partition_broadcast(P)).then_inc(rows_in, 16)
                if q % 2 == 0 and m:
                    hi(N1 + m + 2)
                if q % 2 == 0 and m > OUT2 - 4:
                    merged_hi(4 + m - (OUT2 - 3), gate_s)
            for m in range(OUT2, MIX2):
                if m == OUT2:
                    merged_hi(7, gate_s)
                hi(N1 + m + 2)

            def square_acc(norm):
                act.activation(xn[:, 0, :], acc[0], ACT.Square, accum_out=stat[:, 0:1]).then_inc(sq0, 1)
                act.activation(xn[:, 1, :], acc[1], ACT.Square, accum_out=stat[:, 1:2]).then_inc(sq1, 1)

            act.wait_ge(blob_used, F2)
            square_acc(5)
            hi(F2 + 2)
            act.wait_ge(h_ok, 7)
            square(h[:, 0, :])
            to_features(6, 3, "pre_ffn")

            def silu_one(j, used, i=0):
                act.wait_ge(blob_used, used)
                act.activation(g_act[:], ps[:, 0, :].rearrange("p (a q) -> p a q", a=2),
                               ACT.Sigmoid).then_inc(gs_ok, 1)

            def hidden2_hi(made):
                act.wait_ge(g_two, made)
                act.activation(gT_h[:], g_act[:], ACT.Copy).then_inc(g_hi, 1)

            hi(F2 + 3)
            silu_one(0, F2 + 1)
            hi(F2 + 4)
            hidden2_hi(1)
            with act.Fori(0, STEP2 - 2) as i:
                hi(F2 + 5, i, 3)
                act.wait_ge(g_lo, i + 1)
                silu_one(0, i * 3 + (F2 + 3))
                hi(F2 + 6, i, 3)
                hi(F2 + 7, i, 3)
                hidden2_hi(i + 2)
            hi(NBLOB - 1)
            act.wait_ge(g_lo, STEP2 - 1)
            silu_one(0, F2 + 3 * STEP2 - 3)
            act.wait_ge(blob_used, NBLOB - 1)
            hidden2_hi(STEP2)

            act.wait_ge(blob_used, NBLOB)
            square_acc(7)
            for t in range(NT):
                act.wait_ge(h_ok, 9 + t)
                act.dma_start(out[:, t, :], h[:, t, :]).then_inc(out_done, 16)
            act.wait_ge(out_done, 32)

        @block.gpsimd
        def _(pool):
            def rsqrt(dst, mid, src, scale, rows=P):
                link(pool, "pool", pool.tensor_scalar(mid, src, scale, EPS, ALU.mult, ALU.add))
                return pool.tensor_tensor(dst, mid, c("neghalf")[0:rows, 0:dst.shape[-1]], ALU.pow)

            def rms(norm):
                pool.wait_ge(sq0, norm)
                pool.wait_ge(sq1, norm)
                rsqrt(stat[:, 4:6], stat[:, 2:4], stat[:, 0:2], 1.0 / D).then_inc(rstd_ok, 1)

            pool.wait_ge(const_in, 48)
            rms(1)
            for r in range(R_HEADS):
                pool.wait_ge(rv_ok, r + 1)
                rsqrt(gn_r[:, r % 2, :], gn_mid[:, r % 2, :], gn_mv[:, r % 2, :, 1], 1.0).then_inc(rr_ok, 1)
            rms(2)
            pool.wait_ge(meta_sq, 1)
            rsqrt(mstat[:, 2:3], mstat[:, 1:2], mstat[:, 0:1], 1.0 / D, N_META).then_inc(meta_r, 1)
            rms(3)
            rms(4)

            pool.wait_ge(blob_used, N1)
            pool.wait_ge(h_ok, 6)
            pool.memset(ksT[:], 0.0)
            pool.memset(vs[:], 0.0)
            pool.memset(vs_meta[:], 0.0)
            pool.memset(kbT[:], 0.0).then_inc(zero2, 1)

            for q in range(U0 + 1, U0 + 5 + UNITS):
                V = q - U0 - 4 - S_UNITS
                if 0 <= V < UNITS - S_UNITS:
                    pool.wait_ge(d_o, V + 1)
                    st = ostat[:, V % 2]
                    link(pool, "pool", rsqrt(st[:, 2:3], st[:, 1:2], st[:, 0:1], 1.0 / P))
                    pool.tensor_scalar(o_tok[V % 2][:], o_tok[V % 2][:], st[:, 2:3], None, ALU.mult).then_inc(d_n, 1)
                U = q - U0 - 1
                if 0 <= U < UNITS:
                    pool.wait_ge(u_exp, U + 1)
                    st, s = usoft[:, U % 2], sc[U % 2]
                    if U < S_UNITS:
                        link(pool, "pool", pool.tensor_tensor(st[:, 4, :], st[:, 4, :], st[:, 3, :], ALU.add))
                    link(pool, "pool", pool.tensor_tensor(st[:, 5, :], st[:, 4, :], c("negone")[:, 0:2], ALU.pow))
                    if U < S_UNITS:
                        for u in range(2):
                            ins = pool.tensor_scalar(s[:, u, :], s[:, u, :], st[:, 5, u:u + 1], None, ALU.mult)
                    else:
                        if U == S_UNITS:
                            pool.wait_ge(lam_ok, 1)
                        link(pool, "pool", pool.tensor_tensor(st[:, 5, 1:2], st[:, 5, 1:2], neglam[:], ALU.mult))
                        pool.tensor_scalar(s[:, 0, :], s[:, 0, :], st[:, 5, 0:1], None, ALU.mult)
                        link(pool, "pool", pool.tensor_scalar(s[:, 1, :], s[:, 1, :], st[:, 5, 1:2], None, ALU.mult))
                        ins = pool.tensor_tensor(s[:, 0, :], s[:, 0, :], s[:, 1, :], ALU.add)
                    ins.then_inc(u_pr, 1)
            for norm in (5, 6, 7):
                rms(norm)

        @block.tensor
        def _(pe):
            ident = c("ident")

            def features(norm, r):
                pe.wait_ge(xn_a, r + 1)
                pe.wait_ge(xn_d, r + 1)
                for k in range(KC):
                    for t in range(NT):
                        m = pe.transpose(ps[:, k, t * P:(t + 1) * P], xn[:, t, k * P:(k + 1) * P], ident)
                    m.then_inc(xt_ps, 1)

            def transpose4(bank, src, signal):
                for t in range(NT):
                    for j in range(4):
                        m = pe.transpose(ps[:, bank + t, j * P:(j + 1) * P], src(t, j), ident)
                m.then_inc(signal, 1)

            features(1, 0)
            for n in range(MIX1):
                pe.wait_ge(split_lo, n + 1)
                if n < 2:
                    multiply_tokens(pe, n % 4, 4 * n, 4, BANK, 0, n == 0, n == 1, xT_h, xT_l, 0)
                elif n == 2:
                    multiply_tokens(pe, n % 4, 0, KC, TOK, 2, True, True, xT_h, xT_l)
                elif n < 15:
                    g = 2 + (n - 3) // 2
                    first = n % 2 == 1
                    if first:
                        wait_pair_free(pe, g)
                    multiply_tokens(pe, n % 4, 0 if first else 4, 4, BANK, 2 * (g % 2), first, not first, xT_h, xT_l)
                elif n < 23:
                    g = 8 + (n - 15) // 2
                    if n % 2 == 1:
                        wait_pair_free(pe, g)
                    multiply_features(pe, n % 4, KC, 2, 2 * (g % 2) + (n - 15) % 2, xT_h, xT_l)
                elif n < 25:
                    g = 12 + n - 23
                    wait_pair_free(pe, g)
                    pe.wait_ge(o_lo, 4)
                    multiply_features(pe, n % 4, 4, 4, 2 * (g % 2), aT_h, aT_l)
                elif n < 29:
                    g = 14 + (n - 25) // 2
                    if n % 2 == 1:
                        wait_pair_free(pe, g)
                    pe.wait_ge(rt_lo, KC)
                    multiply_features(pe, n % 4, KC, 2, 2 * (g % 2) + (n - 25) % 2, retT_h, retT_l)
                else:
                    pe.wait_ge(mg_lo, n - 29 + 1)
                    multiply_tokens(pe, n % 4, 2 * (n - 29), 2, D, 4, n == 29, n == 32, xT_h, xT_l)

                if n == 3:
                    pe.wait_ge(rope_ok, 1)
                    transpose4(4, lambda t, j: tok[0][:, t, j * P:(j + 1) * P], q_ps)
                    pe.wait_ge(rope_ok, 2)
                    for t in range(NT):
                        m = pe.transpose(ps[:, 6, t * P:(t + 1) * P], ka_tok[:, t, :], ident)
                    m.then_inc(q_ps, 1)
                if n == 6:
                    pe.wait_ge(rope_ok, 3)
                    pe.wait_ge(q_ok, 1)
                    transpose4(4, lambda t, j: tok[1][:, t, j * P:(j + 1) * P], q_ps)
                if n == 8:
                    pe.wait_ge(rope_ok, 4)
                    pe.wait_ge(q_ok, 2)
                    transpose4(6, lambda t, j: tok[0][:, t, j * P:(j + 1) * P], q_ps)
                if 12 <= n < 16:
                    j = n - 12
                    pe.wait_ge(pt_a, j + 1)
                    pe.wait_ge(pt_d, j + 1)
                    if j >= 1:
                        pe.wait_ge(o_lo, j)
                    for u in range(2):
                        pe.matmul(ps[:, 7, TOK:TOK + P], va[:, 0, u, :], pT[:, 4 + u, :], start=u == 0, stop=u == 1)
                    for u in range(2):
                        for kt in range(NT):
                            m = pe.matmul(ps[:, 7, TOK + P:2 * TOK], va[:, kt, u, :], pT[:, 2 * u + kt, :],
                                          start=u + kt == 0, stop=u + kt == 2)
                    m.then_inc(o_ps, 1)
                if 11 <= n < 15:
                    j = n - 11
                    pe.wait_ge(pr_ok, j + 1)
                    if j == 0:
                        pe.wait_ge(q_ok, 4)
                    else:
                        pe.wait_ge(pt_d, j)
                        pe.wait_ge(pt_a, j)
                    if j >= 2:
                        pe.wait_ge(o_lo, j - 1)
                    for u in range(2):
                        for kt in range(NT):
                            pe.transpose(ps[:, 6, (2 * u + kt) * P:(2 * u + kt + 1) * P],
                                         s1[j % 2][:, u, kt * P:(kt + 1) * P], ident)
                    for u in range(2):
                        m = pe.transpose(ps[:, 7, u * P:(u + 1) * P], s0[j % 2][:, u, :], ident)
                    m.then_inc(pt_ps, 1)
                if 9 <= n < 13:
                    j = n - 9
                    if j == 0:
                        pe.wait_ge(q_ok, 3)
                    else:
                        pe.wait_ge(sc_ok, j)
                    for u in range(2):
                        pe.matmul(ps[:, 4, u * TOK:(u + 1) * TOK], qaT[:, j, P:TOK], kaT[:, u, :], start=True, stop=True)
                        m = pe.matmul(ps[:, 5, u * P:(u + 1) * P], qaT[:, j, 0:P], kaT[:, u, 0:P], start=True, stop=True)
                    m.then_inc(sc_ps, 1)
                if 17 <= n < 21:
                    r = n - 17
                    pe.wait_ge(rn_ok, r + 1)
                    if r == 0:
                        pe.wait_ge(pt_d, 4)
                    else:
                        pe.wait_ge(rt_lo, 2 * r)
                    for j in range(2):
                        for t in range(NT):
                            m = pe.transpose(ps[:, 6, j * TOK + t * P:j * TOK + (t + 1) * P],
                                             gr[:, r, t, j * P:(j + 1) * P], ident)
                    m.then_inc(rt_ps, 1)
                if 15 <= n < 19:
                    r = n - 15
                    pe.wait_ge(at_ok, r + 1)
                    if r == 0:
                        pe.wait_ge(taken_a, 8)
                    else:
                        pe.wait_ge(rn_ok, r)
                    pe.matmul(ps[:, 5, 0:TOK], decayed[:, 0:P], vr[:, r, 0, :], start=True, stop=True)
                    pe.matmul(ps[:, 5, TOK:2 * TOK], decayed[:, P:2 * P], vr[:, r, 0, :], start=True, stop=False)
                    pe.matmul(ps[:, 5, TOK:2 * TOK], decayed[:, 2 * P:3 * P], vr[:, r, 1, :],
                              start=False, stop=True).then_inc(ro_ps, 1)
                if 14 <= n < 18:
                    r = n - 14
                    if r == 0:
                        pe.wait_ge(sc_ok, 4)
                    else:
                        pe.wait_ge(at_ok, r)
                    pe.matmul(ps[:, 4, 0:TOK], krT[:, r, 0:P], qrT[:, r, :], start=True, stop=True)
                    pe.matmul(ps[:, 4, TOK:TOK + P], krT[:, r, P:TOK], qrT[:, r, P:TOK],
                              start=True, stop=True).then_inc(at_ps, 1)

            features(2, 1)

            def hidden(n, k, i=0, last_read=None, chunk_wait=None, per=4):
                pe.wait_ge(split_lo, i * per + n + 1)
                if last_read is not None:
                    pe.wait_ge(ff_relu, last_read)
                multiply_features(pe, slot_of(n), KC, 2, k, xT_h, xT_l, chunk_wait)

            def down(n, k, made, i=0, first=False, last=False, per=4):
                pe.wait_ge(split_lo, i * per + n + 1)
                pe.wait_ge(ff_lo, made)
                multiply_tokens(pe, slot_of(n), 0, 2, D, 4, first, last, fT_h[k], fT_l[k])

            hidden(MIX1, 0, chunk_wait=KC)
            hidden(MIX1 + 1, 1)
            b = MIX1 + 2
            hidden(b, 0, last_read=1)
            hidden(b + 1, 1, last_read=2)
            down(b + 2, 0, 1, first=True)
            down(b + 3, 1, 2)
            with pe.Fori(1, STEP1 - 1) as i:
                hidden(b, 0, i, i * 2 + 1)
                hidden(b + 1, 1, i, i * 2 + 2)
                down(b + 2, 0, i * 2 + 1, i)
                down(b + 3, 1, i * 2 + 2, i)
            down(N1 - 2, 0, 2 * STEP1 - 1)
            pe.wait_ge(meta_n, 1)
            for k in range(KC):
                m = pe.transpose(ps[:, 2, k * N_META:(k + 1) * N_META], meta_tok[:, k * P:(k + 1) * P],
                                 ident[0:N_META, 0:N_META])
            m.then_inc(meta_ps, 1)
            down(N1 - 1, 1, 2 * STEP1, last=True)

            features(4, 2)

            def slot(q):
                if q in (5, 9, 10, 13, 14):
                    r = (5, 9, 10, 13, 14).index(q)
                    pe.wait_ge(rope_ok, (5, 6, 6, 7, 7)[r])
                    if r:
                        pe.wait_ge(kt_ok, r)
                    for cc in range(2):
                        if r == 0:
                            src, mt, a = ks_tok, mk[0], cc * P
                        else:
                            src, mt, a = tok2[(r - 1) // 2], mk[(1, 0)[(r - 1) // 2]], ((r - 1) % 2 * 2 + cc) * P
                        for t in range(NT):
                            pe.transpose(ps[:, 4 + cc, t * P:(t + 1) * P], src[:, t, a:a + P], ident)
                        m = pe.transpose(ps[:, 4 + cc, TOK:KEYS], mt[:, a:a + P], ident[0:N_META, 0:N_META])
                    m.then_inc(kt_ps, 1)
                if q in (17, 29, 33, 37):
                    r = (17, 29, 33, 37).index(q)
                    g, buf = (3, 6, 7, 8)[r], tok2[r % 2]
                    pe.wait_ge(rope_ok, 8 + r)
                    transpose4(2 * (g % 2), lambda t, j: buf[:, t, j * P:(j + 1) * P], q_ps)
                U = q - U0 - 3
                if 0 <= U < UNITS:
                    pe.wait_ge(u_ptd, U + 1)
                    pe.wait_ge(u_ptm, U + 1)
                    if 0 < U <= S_UNITS:
                        pe.wait_ge(s_lo, U)
                    elif U > S_UNITS:
                        pe.wait_ge(d_o, U - S_UNITS)
                    cc, o = U % S_UNITS // 2, ps[:, 7, 288:288 + P]
                    if U < S_UNITS:
                        for u in range(2):
                            for kt in range(NT):
                                pe.matmul(o, vs[:, kt, cc // 4, u, :], puT[:, 2 * u + kt, :], start=u + kt == 0,
                                          stop=False)
                            m = pe.matmul(o, vs_meta[:, cc // 4, u, :], pmT[:, u, :], start=False, stop=u == 1)
                    else:
                        for kt in range(NT):
                            pe.matmul(o, puT[:, kt, :], vb[:, kt, cc * P:(cc + 1) * P], start=kt == 0, stop=False)
                        m = pe.matmul(o, pmT[:, 0, :], vb_meta[:, cc * P:(cc + 1) * P], start=False, stop=True)
                    m.then_inc(u_o, 1)
                U = q - U0 - 2
                if 0 <= U < UNITS:
                    pe.wait_ge(u_pr, U + 1)
                    if U == 0:
                        pe.wait_ge(mtaken_a, 2)
                    else:
                        pe.wait_ge(u_ptd, U)
                        pe.wait_ge(u_ptm, U)
                    heads = 2 if U < S_UNITS else 1
                    for u in range(heads):
                        for kt in range(NT):
                            pe.transpose(ps[:, 6, (2 * u + kt) * P:(2 * u + kt + 1) * P],
                                         sc[U % 2][:, u, kt * P:(kt + 1) * P], ident)
                    for u in range(heads):
                        m = pe.transpose(ps[0:N_META, 7, 32 + u * P:32 + (u + 1) * P], sc[U % 2][:, u, TOK:KEYS],
                                         ident)
                    m.then_inc(u_pt, 1)
                V = q - U0 - 5 - S_UNITS
                if 0 <= V < UNITS - S_UNITS:
                    pe.wait_ge(d_n, V + 1)
                    pe.wait_ge(u_max, min(UNITS, q - U0))
                    if V:
                        pe.wait_ge(d_lo, V)
                    pe.transpose(ps[:, 5, P:2 * P], o_tok[V % 2][:], ident).then_inc(d_ps, 1)
                U = q - U0
                if 0 <= U < UNITS:
                    cc, t = U % S_UNITS // 2, U % 2
                    pe.wait_ge(q_ok, 5 + U // 8)
                    if U == 0:
                        pe.wait_ge(kt_ok, 5)
                    else:
                        pe.wait_ge(u_max, U)
                    if q - U0 - 6 - S_UNITS >= 0:
                        pe.wait_ge(d_lo, q - U0 - 5 - S_UNITS)
                    qT = qsT if U < S_UNITS else qbT
                    for u in range(2):
                        kT = ksT[:, 2 * (cc // 4) + u, :] if U < S_UNITS else kbT[:, 2 * cc + u, :]
                        pe.matmul(ps[:, 4, u * TOK:(u + 1) * TOK], qT[:, cc, t * P:(t + 1) * P], kT[:, 0:TOK],
                                  start=True, stop=True)
                        m = pe.matmul(ps[:, 5, u * N_META:(u + 1) * N_META], qT[:, cc, t * P:(t + 1) * P],
                                      kT[:, TOK:KEYS], start=True, stop=True)
                    m.then_inc(u_sc, 1)

            for m2 in range(OUT2):
                n = N1 + m2
                pe.wait_ge(split_lo, n + 1)
                for part in range(2):
                    if m2 < 18:
                        g, first = m2 // 2, m2 % 2 == 0
                        meta_bank = {0: 6, 1: 7, 2: 6, 4: 7, 5: 6}.get(g)
                        if first and part == 0:
                            if g >= 2:
                                wait_pair_free(pe, 16 + g)
                            if g - 2 in (3, 6, 7, 8):
                                pe.wait_ge(q_ok, 5 + (3, 6, 7, 8).index(g - 2))
                        if first and part == 1 and g in (2, 4, 5):
                            pe.wait_ge(mtaken_d, {2: 1, 4: 2, 5: 3}[g])
                        if m2 == 0 and part == 0:
                            pe.wait_ge(meta_lo, 1)
                        multiply_tokens(pe, slot_of(n), 0 if first else 4, 4, BANK, 2 * (g % 2), first, not first,
                                        xT_h, xT_l, 2 * KC if g == 0 else None, part, meta_bank)
                    else:
                        g = 9 + (m2 - 18) // 2
                        if m2 % 2 == 0 and part == 0:
                            wait_pair_free(pe, 16 + g)
                            if g - 2 in (7, 8):
                                pe.wait_ge(q_ok, g - 2)
                            if m2 == 26:
                                pe.wait_ge(s_lo, S_UNITS)
                            if m2 == 30:
                                pe.wait_ge(d_lo, UNITS - S_UNITS)
                        xh, xl = (xT_h, xT_l) if m2 < 26 else (sT_h, sT_l) if m2 < 30 else (dT_h, dT_l)
                        multiply_features(pe, slot_of(n), KC, 2, 2 * (g % 2) + m2 % 2, xh, xl, None, part)
                    slot(2 * m2 + part)
            for i in range(4):
                n = N1 + OUT2 + i
                pe.wait_ge(split_lo, n + 1)
                pe.wait_ge(mg_lo, 4 + i + 1)
                multiply_tokens(pe, slot_of(n), 2 * i, 2, D, 4, i == 0, i == 3, xT_h, xT_l)

            features(6, 3)

            def hidden2(n, bank, signal, read, i=0, chunk_wait=None):
                pe.wait_ge(split_lo, i * 3 + n + 1)
                if signal is not None:
                    pe.wait_ge(signal, read)
                multiply_features(pe, slot_of(n), KC, 2, bank, xT_h, xT_l, chunk_wait)

            def down2(n, made, i=0, first=False, last=False):
                pe.wait_ge(split_lo, i * 3 + n + 1)
                pe.wait_ge(g_lo, made)
                multiply_tokens(pe, slot_of(n), 0, 2, D, 4, first, last, gT_h, gT_l)

            hidden2(F2, 0, None, 0, chunk_wait=3 * KC)
            hidden2(F2 + 1, 1, None, 0)
            hidden2(F2 + 2, 0, g_one, 1)
            hidden2(F2 + 3, 1, g_two, 1)
            down2(F2 + 4, 1, first=True)
            with pe.Fori(0, STEP2 - 2) as i:
                hidden2(F2 + 5, 0, g_one, i + 2, i)
                hidden2(F2 + 6, 1, g_two, i + 2, i)
                down2(F2 + 7, i + 2, i)
            down2(NBLOB - 1, STEP2, last=True)

        @block.vector
        def _(dve):
            freed, mfreed, rotated = [0], [0], [0]

            def free(ins):
                freed[0] += 1
                ins.then_inc(taken_d, 1)
                dve.wait_ge(taken_d, freed[0])

            def lo(n, i=0, per=0):
                s = slot_of(n)
                dve.wait_ge(split_hi, i * per + n + 1)
                dve.tensor_tensor(wlo[s][:], raw[s][:], whi[s][:], ALU.subtract).then_inc(split_lo, 1)

            def square(src):
                dve.tensor_tensor_reduce(out=xn[:, 1, :], in0=src, in1=src, scale=1.0, scalar=0.0, op0=ALU.mult,
                                         op1=ALU.add, accum_out=stat[:, 1:2]).then_inc(sq1, 1)

            def to_features(norm, r, gain):
                dve.wait_ge(rstd_ok, norm)
                dve.tensor_scalar(xn[:, 1, :], h[:, 1, :], stat[:, 5:6], None, ALU.mult).then_inc(xn_d, 1)
                for k in range(KC):
                    dve.wait_ge(xt_hi, r * KC + k + 1)
                    dve.scalar_tensor_tensor(out=xT_l[:, k, :], in0=ps[:, k, 0:TOK], scalar=cl(gain, k),
                                             in1=xT_h[:, k, :], op0=ALU.mult, op1=ALU.subtract).then_inc(xt_lo, 1)

            def rope_window(buf, heads, t, signal):
                v = buf.rearrange("p (a d) -> p a d", d=A_DIM)
                cs = c("a_cos")[:, t * A_ROPE:(t + 1) * A_ROPE].unsqueeze(1).to_broadcast([P, heads, A_ROPE])
                sn = c("a_sin")[:, t * A_ROPE:(t + 1) * A_ROPE]
                half = A_ROPE // 2
                tmp = scratch[:, 0:heads * A_ROPE].rearrange("p (a d) -> p a d", a=heads)
                dve.tensor_tensor(tmp[:, :, 0:half], v[:, :, half:A_ROPE],
                                  sn[:, 0:half].unsqueeze(1).to_broadcast([P, heads, half]), ALU.mult)
                link(dve, "dve", dve.tensor_tensor(
                    tmp[:, :, half:A_ROPE], v[:, :, 0:half],
                    sn[:, half:A_ROPE].unsqueeze(1).to_broadcast([P, heads, half]), ALU.mult))
                link(dve, "dve", dve.tensor_tensor(v[:, :, 0:A_ROPE], v[:, :, 0:A_ROPE], cs, ALU.mult))
                m = dve.tensor_tensor(v[:, :, 0:A_ROPE], v[:, :, 0:A_ROPE], tmp, ALU.add)
                if signal is None:
                    link(dve, "dve", m)
                else:
                    m.then_inc(signal, 1)
                    rotated[0] += 1
                    dve.wait_ge(signal, rotated[0])

            def rope_whole(dst, bank, heads, d, cs, sn, signal, spare=scratch, rows=P):
                v = ps[0:rows, bank, 0:heads * d].rearrange("p (a d) -> p a d", a=heads)
                o = dst.rearrange("p (a d) -> p a d", a=heads)
                tmp = spare[0:rows, 0:heads * d].rearrange("p (a d) -> p a d", a=heads)
                half = d // 2
                dve.tensor_tensor(tmp[:, :, 0:half], v[:, :, half:d],
                                  sn[:, 0:half].unsqueeze(1).to_broadcast([rows, heads, half]), ALU.mult)
                dve.tensor_tensor(tmp[:, :, half:d], v[:, :, 0:half],
                                  sn[:, half:d].unsqueeze(1).to_broadcast([rows, heads, half]), ALU.mult)
                m = dve.tensor_tensor(o, v, cs.unsqueeze(1).to_broadcast([rows, heads, d]), ALU.mult)
                if rows == P:
                    free(m)
                else:
                    mfreed[0] += 1
                    m.then_inc(mtaken_d, 1)
                    dve.wait_ge(mtaken_d, mfreed[0])
                m = dve.tensor_tensor(o, o, tmp, ALU.add)
                if signal is None:
                    link(dve, "dve", m)
                else:
                    m.then_inc(signal, 1)
                    rotated[0] += 1
                    dve.wait_ge(signal, rotated[0])

            def merge(i, n, first=gate_a, second=gate_r, spare=scratch, bank=0, before=0):
                a = first[:, 2 * i:2 * i + 2, :].rearrange("p a q -> p (a q)")
                r = second[:, 2 * i:2 * i + 2, :].rearrange("p a q -> p (a q)")
                dve.wait_ge(blob_used, n)
                free(dve.tensor_tensor(spare[:], ps[:, (bank + i) % 4, :], r, ALU.mult))
                dve.tensor_tensor(a, spare[:], a, ALU.add).then_inc(mg_ok, 1)
                dve.wait_ge(mg_hi, before + i + 1)
                dve.tensor_tensor(xT_l[:, 2 * i:2 * i + 2, :], first[:, 2 * i:2 * i + 2, :],
                                  xT_h[:, 2 * i:2 * i + 2, :], ALU.subtract).then_inc(mg_lo, 1)

            def softmax_front(j):
                dve.wait_ge(sc_ps, j + 1)
                if j >= 2:
                    dve.wait_ge(pt_ps, j - 1)
                st = soft[:, j % 2]
                m1 = cst[:, CONST["gt"][0]:CONST["gt"][0] + 2 * P]
                dve.scalar_tensor_tensor(out=s1[j % 2][:], in0=ps[:, 4, :].rearrange("p (a k) -> p a k", a=2),
                                         scalar=A_DIM ** -0.5, in1=m1.unsqueeze(1).to_broadcast([P, 2, 2 * P]),
                                         op0=ALU.mult, op1=ALU.add)
                link(dve, "dve", dve.scalar_tensor_tensor(
                    out=s0[j % 2][:], in0=ps[:, 5, 0:TOK].rearrange("p (a k) -> p a k", a=2), scalar=A_DIM ** -0.5,
                    in1=c("diag1").unsqueeze(1).to_broadcast([P, 2, P]), op0=ALU.mult, op1=ALU.add))
                dve.tensor_reduce(st[:, 0, 0:2], s1[j % 2][:], AX.X, ALU.max)
                link(dve, "dve", dve.tensor_reduce(st[:, 0, 2:4], s0[j % 2][:], AX.X, ALU.max))
                link(dve, "dve", dve.scalar_tensor_tensor(out=st[:, 1, :], in0=st[:, 0, :], scalar=-1.0,
                                                          in1=negsink[:, 4 * j:4 * j + 4], op0=ALU.mult, op1=ALU.min))
                dve.tensor_tensor(st[:, 2, :], st[:, 1, :], negsink[:, 4 * j:4 * j + 4],
                                  ALU.subtract).then_inc(sc_ok, 1)

            def softmax_back(j):
                dve.wait_ge(ex_ok, j + 1)
                st = soft[:, j % 2]
                link(dve, "dve", dve.tensor_tensor(st[:, 3, :], st[:, 3, :], st[:, 2, :], ALU.add))
                link(dve, "dve", dve.reciprocal(st[:, 4, :], st[:, 3, :]))
                for u in range(2):
                    dve.tensor_scalar(s1[j % 2][:, u, :], s1[j % 2][:, u, :], st[:, 4, u:u + 1], None, ALU.mult)
                for u in range(2):
                    m = dve.tensor_scalar(s0[j % 2][:, u, :], s0[j % 2][:, u, :], st[:, 4, 2 + u:3 + u], None, ALU.mult)
                m.then_inc(pr_ok, 1)

            def step_lambda():
                a = ROWS["lambdas"][0]
                for v in range(2):
                    m = dve.tensor_tensor_reduce(
                        out=scratch2[:, v * DH:(v + 1) * DH], in0=row[:, a + 2 * v * DH:a + (2 * v + 1) * DH],
                        in1=row[:, a + (2 * v + 1) * DH:a + (2 * v + 2) * DH], scale=1.0, scalar=0.0, op0=ALU.mult,
                        op1=ALU.add, accum_out=lam[:, v:v + 1])
                m.then_inc(lam_s, 1)
                dve.tensor_scalar(subgain[:], cl("subln"), 1.0 - LAMBDA, None, ALU.mult)
                dve.wait_ge(lam_e, 1)
                dve.scalar_tensor_tensor(out=neglam[:], in0=lam[:, 3:4], scalar=-LAMBDA, in1=lam[:, 2:3],
                                         op0=ALU.add, op1=ALU.subtract).then_inc(lam_ok, 1)

            def unit_front(U):
                dve.wait_ge(u_sc, U + 1)
                if U >= 2:
                    dve.wait_ge(u_pt, U - 1)
                st, s = usoft[:, U % 2], sc[U % 2]
                if U < S_UNITS:
                    a = CONST["ge" if U % 2 else "zero"][0]
                    mask = cst[:, a:a + TOK]
                else:
                    mask = None
                for u in range(2):
                    for part, (src, a, b) in enumerate(((ps[:, 4, u * TOK:(u + 1) * TOK], 0, TOK),
                                                        (ps[:, 5, u * N_META:(u + 1) * N_META], TOK, KEYS))):
                        if part == 0 and mask is not None:
                            add = mask
                        elif part == 0:
                            add = c("zero").unsqueeze(1).to_broadcast([P, 2, P])
                            src = src.rearrange("p (a k) -> p a k", a=2)
                        else:
                            add = c("zero")[:, 0:N_META]
                        o = s[:, u, a:b]
                        if part == 0 and mask is None:
                            o = o.rearrange("p (a k) -> p a k", a=2)
                        m = dve.tensor_tensor_reduce(out=o, in0=src, in1=add, scale=DH ** -0.5, scalar=NEG,
                                                     op0=ALU.add, op1=ALU.max, accum_out=st[:, part, u:u + 1])
                link(dve, "dve", m)
                link(dve, "dve", dve.tensor_tensor(st[:, 0, :], st[:, 0, :], st[:, 1, :], ALU.max))
                if U < S_UNITS:
                    sink = negsink[:, 2 * A_HEADS + U // 2 * 2:2 * A_HEADS + U // 2 * 2 + 2]
                    link(dve, "dve", dve.scalar_tensor_tensor(out=st[:, 2, :], in0=st[:, 0, :], scalar=-1.0, in1=sink,
                                                              op0=ALU.mult, op1=ALU.min))
                    dve.tensor_tensor(st[:, 3, :], st[:, 2, :], sink, ALU.subtract).then_inc(u_max, 1)
                else:
                    dve.tensor_scalar(st[:, 2, :], st[:, 0, :], -1.0, None, ALU.mult).then_inc(u_max, 1)

            dve.memset(kaT[:], 0.0).then_inc(init_ok, 1)
            dve.memset(va[:], 0.0).then_inc(init_ok, 1)
            dve.wait_ge(x_in, 16)
            square(h[:, 1, :])
            dve.wait_ge(const_in, 48)
            dve.tensor_scalar(negsink[:], row[:, 0:2 * A_HEADS + S_HEADS], -1.0, None, ALU.mult).then_inc(init_ok, 1)
            to_features(1, 0, "norm_mix")
            for n in range(3):
                lo(n)

            for n in range(MIX1):
                lo(n + 3)
                if n == 2:
                    dve.wait_ge(taken_a, 2)
                    rope_window(tok[0][:, 0, :], A_HEADS, 0, None)
                    rope_window(tok[0][:, 1, :], A_HEADS, 1, rope_ok)
                if n == 3:
                    dve.wait_ge(taken_a, 4)
                    rope_window(ka_tok[:, 0, :], 2, 0, None)
                    rope_window(ka_tok[:, 1, :], 2, 1, rope_ok)
                if n in (5, 7):
                    dve.wait_ge(blob_used, n)
                    if n == 7:
                        dve.wait_ge(q_ps, 1)
                    for t in range(NT):
                        rope_whole(tok[1 if n == 5 else 0][:, t, :], (n - 5) + t, R_HEADS, R_KEY,
                                   c("ret_cos")[:, t * P:(t + 1) * P], c("ret_sin")[:, t * P:(t + 1) * P],
                                   rope_ok if t == 1 else None)
                if n in (13, 15):
                    hh = n - 13
                    v = gr[:, hh:hh + 2]
                    for t in range(NT):
                        dve.wait_ge(e_ok, 2 * (hh // 2) + t + 1)
                        free(dve.tensor_tensor(v[:, :, t, :], ps[:, (n - 13) + t, :].rearrange("p (a v) -> p a v", a=2),
                                               v[:, :, t, :], ALU.mult))
                if 12 <= n < 16:
                    j = n - 12
                    dve.wait_ge(pt_ps, j + 1)
                    dve.tensor_copy(pT[:, 0:4, :], ps[:, 6, :].rearrange("p (a q) -> p a q", a=4)).then_inc(pt_d, 1)
                if 13 <= n < 17:
                    j = n - 13
                    dve.wait_ge(o_hi, j + 1)
                    dve.wait_ge(pt_a, min(4, j + 2))
                    dve.tensor_tensor(aT_l[:, j, :], ps[:, 7, TOK:2 * TOK], aT_h[:, j, :],
                                      ALU.subtract).then_inc(o_lo, 1)
                if 11 <= n < 15:
                    softmax_back(n - 11)
                if 10 <= n < 14:
                    softmax_front(n - 10)
                if 18 <= n < 22:
                    r = n - 18
                    dve.wait_ge(rt_hi, 2 * r + 2)
                    for j in range(2):
                        dve.scalar_tensor_tensor(out=retT_l[:, 2 * r + j, :], in0=ps[:, 6, j * TOK:(j + 1) * TOK],
                                                 scalar=cl("ret_gn", 2 * r + j), in1=retT_h[:, 2 * r + j, :],
                                                 op0=ALU.mult, op1=ALU.subtract).then_inc(rt_lo, 1)
                if 16 <= n < 20:
                    r = n - 16
                    b = r % 2
                    dve.wait_ge(ro_ps, r + 1)
                    for t in range(NT):
                        m = dve.bn_stats(gn_stat[:, b, t, :], ps[:, 5, t * TOK:(t + 1) * TOK])
                    link(dve, "dve", m)
                    for t in range(NT):
                        m = dve.bn_aggr(gn_mv[:, b, t, :], gn_stat[:, b, t, :])
                    m.then_inc(rv_ok, 1)
                    dve.wait_ge(rv_ok, r + 1)
                    for t in range(NT):
                        m = dve.scalar_tensor_tensor(out=gr[:, r, t, :], in0=ps[:, 5, t * TOK:(t + 1) * TOK],
                                                     scalar=gn_mv[:, b, t, 0:1], in1=gr[:, r, t, :],
                                                     op0=ALU.subtract, op1=ALU.mult)
                    link(dve, "dve", m)
                    dve.wait_ge(rr_ok, r + 1)
                    for t in range(NT):
                        m = dve.tensor_scalar(gr[:, r, t, :], gr[:, r, t, :], gn_r[:, b, t:t + 1], None, ALU.mult)
                    m.then_inc(rn_ok, 1)
                if 15 <= n < 19:
                    r = n - 15
                    dve.wait_ge(at_ps, r + 1)
                    if r:
                        dve.wait_ge(ro_ps, r)
                    dve.tensor_tensor(decayed[:], ps[:, 4, 0:3 * P], c("decay")[:, r * 3 * P:(r + 1) * 3 * P],
                                      ALU.mult).then_inc(at_ok, 1)
                if n in (24, 25):
                    v = gate_a[:, 4 * (n - 24):4 * (n - 24) + 4, :].rearrange("p a q -> p (a q)")
                    dve.wait_ge(blob_used, n)
                    for b in range(2):
                        free(dve.tensor_tensor(v[:, b * BANK:(b + 1) * BANK], ps[:, 2 * (n - 24) + b, :],
                                               v[:, b * BANK:(b + 1) * BANK], ALU.mult))
                if 26 <= n < 30:
                    merge(n - 26, n)
            for t in range(NT):
                dve.wait_ge(blob_used, MIX1)
                dve.tensor_tensor(h[:, t, :], acc[t], h[:, t, :], ALU.add).then_inc(h_ok, 1)
            dve.wait_ge(h_ok, 2)
            square(h[:, 1, :])
            to_features(2, 1, "norm_mlp")

            def hidden_square(k, count):
                dve.wait_ge(ff_relu, count)
                dve.tensor_tensor(f_sq[k][:], f_sq[k][:], f_sq[k][:], ALU.mult).then_inc(ff_sq, 1)

            def hidden_lo(k, count):
                dve.wait_ge(ff_hi, count)
                dve.tensor_tensor(fT_l[k][:], f_sq[k][:], fT_h[k][:], ALU.subtract).then_inc(ff_lo, 1)

            b = MIX1
            lo(b + 3)
            lo(b + 4)
            hidden_square(0, 1)
            hidden_square(1, 2)
            hidden_lo(0, 1)
            with dve.Fori(0, STEP1 - 1) as i:
                b = MIX1 + 2
                lo(b + 3, i, 4)
                hidden_lo(1, i * 2 + 2)
                lo(b + 4, i, 4)
                hidden_square(0, i * 2 + 3)
                lo(b + 5, i, 4)
                hidden_square(1, i * 2 + 4)
                lo(b + 6, i, 4)
                hidden_lo(0, i * 2 + 3)
            b = N1 - 2
            lo(b + 3)
            hidden_lo(1, 2 * STEP1)
            dve.wait_ge(meta_ps, 1)
            dve.tensor_tensor(metaT[:], ps[:, 2, 0:KC * N_META].rearrange("p (a q) -> p a q", a=KC),
                              cl("pre_mix", 0, KC).unsqueeze(2).to_broadcast([P, KC, N_META]),
                              ALU.mult).then_inc(meta_g, 1)
            lo(b + 4)
            dve.wait_ge(meta_hi, 1)
            dve.tensor_tensor(metaT_l[:], metaT[:], metaT_h[:], ALU.subtract).then_inc(meta_lo, 1)

            for t in range(NT):
                dve.wait_ge(blob_used, N1)
                dve.tensor_tensor(h[:, t, :], acc[t], h[:, t, :], ALU.add).then_inc(h_ok, 1)
            dve.wait_ge(h_ok, 4)
            square(h[:, 1, :])
            dve.wait_ge(rstd_ok, 3)
            dve.wait_ge(row_in, 16)
            for t in range(NT):
                dve.scalar_tensor_tensor(out=h[:, t, :], in0=h[:, t, :], scalar=stat[:, 4 + t:5 + t], in1=gain_row[:],
                                         op0=ALU.mult, op1=ALU.mult).then_inc(h_ok, 1)

            dve.wait_ge(h_ok, 6)
            square(h[:, 1, :])
            to_features(4, 2, "pre_mix")

            for q in range(2 * OUT2):
                m2 = q // 2
                if q == 1:
                    step_lambda()
                U = q - U0 - 3
                if 0 <= U < UNITS:
                    dve.wait_ge(u_pt, U + 1)
                    if U:
                        dve.wait_ge(u_o, U)
                    n = 4 if U < S_UNITS else 2
                    dve.tensor_copy(puT[:, 0:n, :], ps[:, 6, 0:n * P].rearrange("p (a q) -> p a q", a=n)).then_inc(
                        u_ptd, 1)
                U = q - U0 - 4
                if 0 <= U < S_UNITS:
                    cc, t = U // 2, U % 2
                    dve.wait_ge(s_hi, U + 1)
                    dve.tensor_tensor(sT_l[:, cc, t * P:(t + 1) * P], ps[:, 7, 288:288 + P],
                                      sT_h[:, cc, t * P:(t + 1) * P], ALU.subtract).then_inc(s_lo, 1)
                V = q - U0 - 6 - S_UNITS
                if 0 <= V < UNITS - S_UNITS:
                    cc, t = V // 2, V % 2
                    dve.wait_ge(d_hi, V + 1)
                    dve.scalar_tensor_tensor(out=dT_l[:, cc, t * P:(t + 1) * P], in0=ps[:, 5, P:2 * P],
                                             scalar=subgain[:], in1=dT_h[:, cc, t * P:(t + 1) * P], op0=ALU.mult,
                                             op1=ALU.subtract).then_inc(d_lo, 1)
                U = q - U0 - 1
                if 0 <= U < UNITS:
                    unit_front(U)
                if q in (4, 8, 12, 16, 28, 32, 36):
                    r = (4, 8, 12, 16, 28, 32, 36).index(q)
                    g = (0, 1, 2, 3, 6, 7, 8)[r]
                    dve.wait_ge(blob_used, N1 + m2)
                    if r == 0:
                        dve.wait_ge(sv_ok, 1)
                        dst, heads = ks_tok, S_KV
                    else:
                        dst, heads = tok2[(0, 1, 0, 1, 0, 1)[r - 1]], F_HEADS
                    if r in (2, 3, 4):
                        dve.wait_ge(kt_ps, {2: 1, 3: 3, 4: 5}[r])
                    if r in (5, 6):
                        dve.wait_ge(q_ps, r)
                    for t in range(NT + 1 if r < 3 else NT):
                        cs, sn = (c(name)[:, t * DH:(t + 1) * DH] for name in ("h_cos", "h_sin"))
                        if t < NT:
                            last = t == NT - 1 and r >= 3
                            rope_whole(dst[:, t, :], 2 * (g % 2) + t, heads, DH, cs, sn, rope_ok if last else None,
                                       scratch2)
                        else:
                            rope_whole(mk[r % 2][:, 0:heads * DH], 6 + r % 2, heads, DH, cs[0:N_META],
                                       sn[0:N_META], rope_ok, scratch2, N_META)
                if q in (56, 60):
                    g = (q - 56) // 4
                    dve.wait_ge(blob_used, N1 + m2)
                    for b in range(2):
                        v = gate_s[:, 4 * g + 2 * b:4 * g + 2 * b + 2, :].rearrange("p a q -> p (a q)")
                        free(dve.tensor_tensor(v, ps[:, (2 + 2 * g + b) % 4, :], v, ALU.mult))
                if q % 2 == 0 and m2:
                    lo(N1 + m2 + 2)
                if q % 2 == 0 and m2 > OUT2 - 4:
                    merge(m2 - (OUT2 - 3), N1 + m2, gate_s, gate_d, scratch2, 2, 4)
            for m2 in range(OUT2, MIX2):
                if m2 == OUT2:
                    merge(3, N1 + OUT2, gate_s, gate_d, scratch2, 2, 4)
                lo(N1 + m2 + 2)

            def add_normalised(norm, k, made):
                dve.wait_ge(rstd_ok, norm)
                for t in range(NT):
                    link(dve, "dve", dve.scalar_tensor_tensor(
                        out=xn[:, t, :], in0=acc[t], scalar=stat[:, 4 + t:5 + t], in1=gain_rows[:, k, :],
                        op0=ALU.mult, op1=ALU.mult))
                    dve.tensor_tensor(h[:, t, :], xn[:, t, :], h[:, t, :], ALU.add).then_inc(h_ok, 1)

            lo(F2 + 2)
            dve.wait_ge(rows_in, 16)
            add_normalised(5, 0, 7)
            dve.wait_ge(h_ok, 8)
            square(h[:, 1, :])
            to_features(6, 3, "pre_ffn")

            def gate_product(made):
                dve.wait_ge(gs_ok, made)
                v = g_act[:].rearrange("p a q -> p (a q)")
                dve.tensor_tensor(v, ps[:, 0, :], v, ALU.mult).then_inc(g_one, 1)

            def up_product(made, used):
                dve.wait_ge(g_one, made)
                dve.wait_ge(blob_used, used)
                v = g_act[:].rearrange("p a q -> p (a q)")
                dve.tensor_tensor(v, ps[:, 1, :], v, ALU.mult).then_inc(g_two, 1)

            def hidden2_lo(made):
                dve.wait_ge(g_hi, made)
                dve.tensor_tensor(gT_l[:], g_act[:], gT_h[:], ALU.subtract).then_inc(g_lo, 1)

            lo(F2 + 3)
            gate_product(1)
            up_product(1, F2 + 2)
            lo(F2 + 4)
            hidden2_lo(1)
            with dve.Fori(0, STEP2 - 2) as i:
                lo(F2 + 5, i, 3)
                gate_product(i + 2)
                lo(F2 + 6, i, 3)
                up_product(i + 2, i * 3 + (F2 + 4))
                lo(F2 + 7, i, 3)
                hidden2_lo(i + 2)
            lo(NBLOB - 1)
            gate_product(STEP2)
            up_product(STEP2, F2 + 3 * STEP2 - 2)
            hidden2_lo(STEP2)
            add_normalised(7, 1, 9)



def blob_tokens(w, c0, width=BANK):
    nk = BLOB // width
    v = w[:, c0:c0 + width].reshape(-1, nk, P, width)
    return [v[i].transpose(1, 0, 2).reshape(P, BLOB) for i in range(v.shape[0])]


def head_pairs(w, first, axis):
    n = w.shape[axis] // DH
    order = [8 * p + 4 * u + a for p in range(n // 8) for a in range(4) for u in range(2)]
    v = np.moveaxis(w, axis, 0).reshape((n, DH) + tuple(np.delete(w.shape, axis)))
    return np.moveaxis(v[order].reshape((n * DH,) + v.shape[2:]), 0, axis)


def weight_stream(i):
    w = np.asarray(i["w_in"])[0]
    at = np.cumsum([0, 512, 128, 128, 512, 512, 1024, 1024, 1024, 1024])
    out = []
    out += blob_tokens(head_pairs(w[:, 0:512], 0, 1), 0)
    out += blob_tokens(w, at[1], 256)
    for a in range(3, 5):
        out += blob_tokens(w, at[a])
    for a in range(5, 7):
        out += blob_tokens(w, at[a]) + blob_tokens(w, at[a] + BANK)
    for a in range(7, 9):
        for q in range(4):
            out += blob_tokens(w, at[a] + 256 * q, 256)
    att = head_pairs(np.asarray(i["w_att_up"])[0], 0, 0)
    out += blob_tokens(att, 0) + blob_tokens(att, BANK)
    up = np.asarray(i["w_ret_up"])[0]
    for q in range(4):
        out += blob_tokens(up, 256 * q, 256)
    out += blob_tokens(np.asarray(i["w_out"])[0], 0, D)
    ff1, ff2 = np.asarray(i["w_ff1"])[0], np.asarray(i["w_ff2"])[0]
    down = blob_tokens(ff2, 0, D)
    for j in range(STEP1):
        out += blob_tokens(ff1, 512 * j, 256) + blob_tokens(ff1, 512 * j + 256, 256)
        if j:
            out += down[2 * j - 2:2 * j]
    out += down[-2:]
    assert len(out) == N1

    w = np.asarray(i["w_in_2"])[0]
    at = np.cumsum([0, 1024, 256, 256, 1024, 1024, 1024])
    qa = head_pairs(w[:, 0:1024], 0, 1)
    out += blob_tokens(w, at[1])
    out += blob_tokens(w, at[4]) + blob_tokens(w, at[4] + BANK)
    out += blob_tokens(qa, 0)
    out += blob_tokens(w, at[5]) + blob_tokens(w, at[5] + BANK)
    out += blob_tokens(qa, BANK)
    out += blob_tokens(w, at[3]) + blob_tokens(w, at[3] + BANK)
    for q in range(8):
        out += blob_tokens(w, at[6] + 256 * q, 256)
    for up in (head_pairs(np.asarray(i["w_branch_swa_2"])[0], 0, 0), np.asarray(i["w_branch_diff_2"])[0]):
        for q in range(4):
            out += blob_tokens(up, 256 * q, 256)
    out += blob_tokens(np.asarray(i["w_out_2"])[0], 0, D)
    assert len(out) == F2
    up, down = np.asarray(i["w_ffn_in_2"])[0], blob_tokens(np.asarray(i["w_ffn_out_2"])[0], 0, D)
    for j in range(STEP2):
        out += blob_tokens(up, 256 * j, 256) + blob_tokens(up, FF2 + 256 * j, 256)
        if j:
            out += down[j - 1:j]
    out += down[-1:]
    assert len(out) == NBLOB
    return out


def constants():
    out = np.zeros((P, NCONST), np.float32)

    def put(name, v):
        a, n = CONST[name]
        out[:v.shape[0], a:a + n] = v.reshape(v.shape[0], n)

    f = np.float32
    q, k = np.arange(P)[:, None], np.arange(P)[None, :]
    put("ident", np.eye(P, dtype=f))
    put("gt", np.where(k > q, 0, NEG))
    put("diag1", np.where(k <= q, 0, NEG))
    put("ge", np.where(k >= q, 0, NEG))
    put("diag2", np.where(k <= q, 0, NEG))
    lg = np.log1p(-np.exp2(-5.0 - np.arange(R_HEADS)))
    dec = np.zeros((P, R_HEADS, 3, P))
    kk, qq = np.arange(P)[:, None], np.arange(P)[None, :]
    for r in range(R_HEADS):
        dec[:, r, 0] = np.where(qq >= kk, np.exp(np.maximum(qq - kk, 0) * lg[r]), 0)
        dec[:, r, 1] = np.exp((P + qq - kk) * lg[r])
        dec[:, r, 2] = dec[:, r, 0]
    put("decay", dec * R_KEY ** -0.5)

    def rope(pos, dim, theta):
        inv = f(theta) ** (-np.arange(0, dim, 2, dtype=f) / f(dim))
        ang = pos.astype(f)[:, None] * inv[None, :].astype(f)
        cs, sn = np.cos(ang.astype(np.float64)), np.sin(ang.astype(np.float64))
        return np.concatenate([cs, cs], 1), np.concatenate([-sn, sn], 1)

    for name, dim, theta in (("a", A_ROPE, 500000.0), ("ret", R_KEY, 10000.0)):
        for part, v in zip(("_cos", "_sin"), rope(np.arange(TOK), dim, theta)):
            put(name + part, v.reshape(NT, P, dim).transpose(1, 0, 2).copy())
    for part, v in zip(("_cos", "_sin"), rope(np.arange(KEYS), DH, 10000.0)):
        a, n = CONST["h" + part]
        t = out[:, a:a + n].reshape(P, NT + 1, DH)
        t[:, 0:NT] = v[N_META:].reshape(NT, P, DH).transpose(1, 0, 2)
        t[:N_META, NT] = v[:N_META]
        out[:, a:a + n] = t.reshape(P, n)
    put("neghalf", np.full((P, 2), -0.5))
    put("negone", np.full((P, 6), -1.0))
    return out


def kernel(**inputs):
    import concourse.bacc as bacc
    from concourse.bass_utils import run_bass_kernel_spmd

    i = {k: np.asarray(v) for k, v in inputs.items()}
    x = i["x"][0].reshape(NT, P, D).transpose(1, 0, 2)
    cols = np.zeros((P, NCOLS), np.float32)
    for name, key in (("norm_mix", "norm_mix_gain"), ("norm_mlp", "norm_mlp_gain"), ("ret_gn", "ret_gn_gain"),
                      ("b_gates", "b_gates"), ("pre_mix", "pre_mix_gain_2"), ("b_gate_2", "b_gate_2"),
                      ("pre_ffn", "pre_ffn_gain_2"), ("subln", "diff_subln_gain_2")):
        a, n = COLS[name]
        cols[:, a:a + n] = i[key].reshape(n, P).T
    s = i["attn_sinks"][0]
    s2 = i["attn_sink_2"][0]
    rows = np.concatenate(
        [np.concatenate([s[[j, j + 4, j, j + 4]] for j in range(4)]),
         s2[[8 * p + 4 * u + a for p in range(2) for a in range(4) for u in range(2)]],
         i["lambda_q1_2"][0], i["lambda_k1_2"][0], i["lambda_q2_2"][0], i["lambda_k2_2"][0]])
    grow = np.stack([i["norm_final_gain"], i["post_mix_gain_2"][0], i["post_ffn_gain_2"][0]])
    arrays = {
        "weights": np.stack(weight_stream(i)),
        "x_tiles": x,
        "meta": i["meta_tokens_2"],
        "consts": constants(),
        "cols": cols,
        "rows": rows,
        "gain_rows": grow,
    }
    arrays = {k: np.ascontiguousarray(v) for k, v in arrays.items()}
    nc = bacc.Bacc("TRN2", target_bir_lowering=False, num_devices=1)
    args = [nc.dram_tensor(k, v.shape, mybir.dt.from_np(v.dtype), kind="ExternalInput").ap() for k, v in arrays.items()]
    y = nc.dram_tensor("y", (P, NT, D), F32, kind="ExternalOutput").ap()
    build(nc, *args, y)
    r = run_bass_kernel_spmd(nc, [arrays], core_ids=[0])
    return r.results[0]["y"].transpose(1, 0, 2).reshape(1, TOK, D)
```

```python
from contextlib import ExitStack

import numpy as np

import concourse.bass as bass
from concourse import mybir

F32 = mybir.dt.float32
F32R = mybir.dt.float32r
ALU = mybir.AluOpType
ACT = mybir.ActivationFunctionType
AX = mybir.AxisListType

P = 128
D = 1024
TOK = 256
NT = TOK // P
KC = D // P
BANK = 512
BLOB = 2048
EPS = 1e-6
NEG = -1e30

A_HEADS, A_DIM, A_ROPE, A_WINDOW = 8, 64, 16, 128
R_HEADS, R_KEY, R_VAL = 4, 128, 256
FF1 = 4096
N_META = 16
S_HEADS, S_KV, DH = 16, 4, 64
F_HEADS = 8
FF2 = 2816
LAMBDA = 0.8 - 0.6
KEYS = TOK + N_META

MIX1 = 2 + 1 + 2 + 2 + 4 + 4 + 4 + 4 + 2 + 4 + 4
STEP1 = FF1 // 512
N1 = MIX1 + 4 * STEP1
OUT2 = 34
U0, S_UNITS, UNITS = 22, 16, 32
MIX2 = 2 + 4 + 4 + 4 + 4 + 4 + 4 + 4 + 4 + 4
STEP2 = FF2 // 256
F2 = N1 + MIX2
NBLOB = F2 + 3 * STEP2

CONST = {}
for _name, _width in (("ident", P), ("neghalf", 2), ("a_cos", NT * A_ROPE), ("a_sin", NT * A_ROPE),
                      ("ge", P), ("zero", P), ("diag2", P), ("pad", 6),
                      ("h_cos", (NT + 1) * DH), ("h_sin", (NT + 1) * DH),
                      ("gt", P), ("diag1", P), ("ret_cos", NT * P), ("ret_sin", NT * P),
                      ("decay", R_HEADS * 3 * P)):
    CONST[_name] = (sum(w for _, w in CONST.values()), _width)
NCONST = sum(w for _, w in CONST.values())
EARLY = P + 2

COLS = {}
for _name, _width in (("norm_mix", KC), ("norm_mlp", KC), ("ret_gn", KC), ("b_gates", 2 * KC),
                      ("pre_mix", KC), ("b_gate_2", 2 * KC), ("pre_ffn", KC), ("subln", 1)):
    COLS[_name] = (sum(w for _, w in COLS.values()), _width)
NCOLS = sum(w for _, w in COLS.values())

ROWS = {}
for _name, _width in (("sinks", A_HEADS * 2), ("sinks_2", S_HEADS), ("lambdas", 4 * DH)):
    ROWS[_name] = (sum(w for _, w in ROWS.values()), _width)
NROWS = sum(w for _, w in ROWS.values())


def slot_of(n):
    return n % 4 if n < N1 else 1 + (n - N1) % 3


def depth_of(n):
    return 4 if n < N1 else 3


def used_before(n):
    return n - 3 if n < N1 + 3 else n - 2


def fills(n):
    if n < N1:
        return n // 4 + 1
    return (N1 - 1) // 4 + 1 + (n - N1) // 3


def build(nc, w, x, meta, consts, cols, rows, grow, out):
    with ExitStack() as ctx:
        def sem(name):
            return ctx.enter_context(nc.semaphore(name))

        base = (nc.sbuf_base + 127) // 128 * 128
        top = [0]

        def at(name, shape, dt, offset):
            return nc.alloc_sbuf_tensor_at(name, shape, dt, offset=base + 4 * offset)

        def new(name, shape, dt=F32):
            size = (int(np.prod(shape[1:])) + 7) // 8 * 8
            top[0] += size
            assert base + 4 * top[0] <= nc.sbuf_usable_end, (name, top[0])
            return at(name, shape, dt, top[0] - size)

        raw, whi, wlo = [None] * 4, [None] * 4, [None] * 4
        for s in range(4):
            raw[s] = new(f"raw{s}", [P, BLOB])
            whi[s] = new(f"whi{s}", [P, BLOB], F32R)
            wlo[s] = new(f"wlo{s}", [P, BLOB], F32R)
        xT_h = new("xT_h", [P, KC, TOK], F32R)
        xT_l = new("xT_l", [P, KC, TOK], F32R)
        h = new("h", [P, NT, D])
        cst_at = top[0]
        cst = new("cst", [P, NCONST])
        col = new("col", [P, NCOLS])
        row = new("row", [P, NROWS])
        stat = new("stat", [P, NT, 4])
        soft = new("soft", [P, 2, 5, 4])
        gn_stat = new("gn_stat", [P, 2, NT, 6])
        gn_mv = new("gn_mv", [P, 2, NT, 2])
        gn_mid = new("gn_mid", [P, 2, NT])
        gn_r = new("gn_r", [P, 2, NT])
        metaT_h = new("metaT_h", [P, KC, N_META], F32R)
        metaT_l = new("metaT_l", [P, KC, N_META], F32R)
        metaT = new("metaT", [P, KC, N_META])
        mstat = new("mstat", [N_META, 4])
        usoft = new("usoft", [P, 2, 6, 2])
        lam = new("lam", [P, 4])
        neglam = new("neglam", [P, 1])
        subgain = new("subgain", [P, 1])
        ostat = new("ostat", [P, 2, 3])
        negsink = new("negsink", [P, 2 * A_HEADS + S_HEADS])
        region = top[0]

        def c(name):
            a, n = CONST[name]
            return cst[:, a:a + n]

        def cl(name, i=0, n=1):
            a = COLS[name][0] + i
            return col[:, a:a + n]

        xn = at("xn", [P, NT, D], F32, region)

        tok = [new("tok0", [P, NT, 512]), new("tok1", [P, NT, 512])]
        ka_tok = new("ka_tok", [P, NT, P])
        qaT = new("qaT", [P, 4, TOK])
        kaT = new("kaT", [P, 2, TOK])
        va = new("va", [P, NT, 2, P])
        qrT = new("qrT", [P, R_HEADS, TOK])
        krT = new("krT", [P, R_HEADS, TOK])
        vr_at = top[0]
        vr = new("vr", [P, R_HEADS, NT, R_VAL])
        gr_at = top[0]
        gr = new("gr", [P, R_HEADS, NT, R_VAL])
        gate_a = new("gate_a", [P, KC, TOK])
        gate_r = at("gate_r", [P, KC, TOK], F32, region)
        retT_h = at("retT_h", [P, KC, TOK], F32R, vr_at)
        retT_l = at("retT_l", [P, KC, TOK], F32R, gr_at)
        aT_h = new("aT_h", [P, 4, TOK], F32R)
        aT_l = new("aT_l", [P, 4, TOK], F32R)
        s1 = [new("s1a", [P, 2, TOK]), new("s1b", [P, 2, TOK])]
        s0 = [new("s0a", [P, 2, P]), new("s0b", [P, 2, P])]
        pT = new("pT", [P, 6, P])
        decayed_at = top[0]
        decayed = new("decayed", [P, 3 * P])
        scratch = new("scratch", [P, 512])
        end1 = top[0]

        top[0] = region + NT * D
        f_sq = [new("f_sq0", [P, 2, TOK]), new("f_sq1", [P, 2, TOK])]
        fT_h = [new("fT_h0", [P, 2, TOK], F32R), new("fT_h1", [P, 2, TOK], F32R)]
        fT_l = [new("fT_l0", [P, 2, TOK], F32R), new("fT_l1", [P, 2, TOK], F32R)]

        gain_row = new("gain_row", [P, D])
        meta_tok = new("meta_tok", [N_META, D])

        dead = cst_at + CONST["gt"][0]
        gate_s = at("gate_s", [P, KC, TOK], F32, dead)
        o_tok = [at("o_tok0", [P, P], F32, dead + KC * TOK), at("o_tok1", [P, P], F32, dead + KC * TOK + P)]
        top[0] = 0
        kbT = new("kbT", [P, 2 * F_HEADS, KEYS])
        ksT = new("ksT", [P, S_KV, KEYS])
        vs_meta = new("vs_meta", [N_META, 2, 2, P])
        o_junk = new("o_junk", [P, P])
        assert top[0] <= 3 * BLOB
        top[0] = region
        gate_d = at("gate_d", [P, KC, TOK], F32, region)
        tok2 = [new("tok2a", [P, NT, 512]), new("tok2b", [P, NT, 512])]
        dT_l = at("dT_l", [P, KC, TOK], F32R, top[0])
        ks_tok = new("ks_tok", [P, NT, 256])
        mk = [new("mk0", [N_META, 512]), new("mk1", [N_META, 512])]
        vs = new("vs", [P, NT, 2, 2, P])
        vb = new("vb", [P, NT, D])
        vb_meta = new("vb_meta", [N_META, D])
        dT_h = at("dT_h", [P, KC, TOK], F32R, top[0])
        qsT = new("qsT", [P, KC, TOK])
        gain_rows = at("gain_rows2", [P, 2, D], F32, top[0])
        qbT = new("qbT", [P, KC, TOK])
        ag = at("ag", [P, NT, D], F32, top[0])
        sT_h = new("sT_h", [P, KC, TOK], F32R)
        sT_l = new("sT_l", [P, KC, TOK], F32R)
        sc = [new("sc0", [P, 2, KEYS]), new("sc1", [P, 2, KEYS])]
        puT = new("puT", [P, 4, P])
        pmT = new("pmT", [N_META, 2, P])
        scratch2 = new("scratch2", [P, 512])

        top[0] = region + NT * D
        g_act = new("g_act", [P, 2, TOK])
        gT_h = new("gT_h", [P, 2, TOK], F32R)
        gT_l = new("gT_l", [P, 2, TOK], F32R)
        gL_h = new("gL_h", [P, 2, TOK], F32R)
        gL_l = new("gL_l", [P, 2, TOK], F32R)

        ps = ctx.enter_context(nc.psum_tensor("ps", [P, 8, BANK], F32))
        acc = [ps[:, 4:6, :].rearrange("p a b -> p (a b)"), ps[:, 6:8, :].rearrange("p a b -> p (a b)")]

        raw_in = [sem(f"raw_in{s}") for s in range(4)]
        split_hi = sem("split_hi")
        split_lo = sem("split_lo")
        blob_used = sem("blob_used")
        x_in = [sem("x_in0"), sem("x_in1")]
        early_in = sem("early_in")
        const_in = sem("const_in")
        first_in = sem("first_in")
        first_hi = sem("first_hi")
        first_lo = sem("first_lo")
        row_in = sem("row_in")
        dve_step = sem("dve_step")
        act_step = sem("act_step")
        pool_step = sem("pool_step")
        init_ok = sem("init_ok")
        out_done = sem("out_done")
        sq_a = sem("sq_a")
        sq_d = sem("sq_d")
        rstd_ok = sem("rstd_ok")
        xn_a = sem("xn_a")
        xn_d = sem("xn_d")
        acc_ok = sem("acc_ok")
        acc_a = sem("acc_a")
        acc_d = sem("acc_d")
        xt_ps = sem("xt_ps")
        xt_hi = sem("xt_hi")
        xt_lo = sem("xt_lo")
        h_ok = sem("h_ok")
        taken_a = sem("taken_a")
        taken_d = sem("taken_d")
        rope_ok = sem("rope_ok")
        q_ps = sem("q_ps")
        q_ok = sem("q_ok")
        sc_ps = sem("sc_ps")
        sc_ok = sem("sc_ok")
        ex_ok = sem("ex_ok")
        pr_ok = sem("pr_ok")
        pt_ps = sem("pt_ps")
        pt_a = sem("pt_a")
        pt_d = sem("pt_d")
        o_ps = sem("o_ps")
        o_hi = sem("o_hi")
        o_lo = sem("o_lo")
        at_ps = sem("at_ps")
        at_ok = sem("at_ok")
        ro_ps = sem("ro_ps")
        rv_ok = sem("rv_ok")
        rr_ok = sem("rr_ok")
        rn_ok = sem("rn_ok")
        rt_ps = sem("rt_ps")
        rt_hi = sem("rt_hi")
        rt_lo = sem("rt_lo")
        e_ok = sem("e_ok")
        mg_ok = sem("mg_ok")
        mg_hi = sem("mg_hi")
        mg_lo = sem("mg_lo")
        ff_relu = sem("ff_relu")
        ff_sq = sem("ff_sq")
        ff_hi = sem("ff_hi")
        ff_lo = sem("ff_lo")

        meta_in = sem("meta_in")
        meta_sq = sem("meta_sq")
        meta_r = sem("meta_r")
        meta_n = sem("meta_n")
        meta_ps = sem("meta_ps")
        meta_g = sem("meta_g")
        meta_hi = sem("meta_hi")
        meta_lo = sem("meta_lo")
        zero2 = sem("zero2")
        mtaken_a = sem("mtaken_a")
        mtaken_d = sem("mtaken_d")
        kt_ps = sem("kt_ps")
        kt_ok = sem("kt_ok")
        sv_ok = sem("sv_ok")
        lam_s = sem("lam_s")
        lam_ok = sem("lam_ok")
        lam_e = sem("lam_e")
        u_sc = sem("u_sc")
        u_max = sem("u_max")
        u_exp = sem("u_exp")
        u_pr = sem("u_pr")
        u_pt = sem("u_pt")
        u_ptd = sem("u_ptd")
        u_ptm = sem("u_ptm")
        u_o = sem("u_o")
        s_hi = sem("s_hi")
        s_lo = sem("s_lo")
        d_o = sem("d_o")
        d_n = sem("d_n")
        d_ps = sem("d_ps")
        d_hi = sem("d_hi")
        d_lo = sem("d_lo")
        rows_in = sem("rows_in")
        gs_ok = sem("gs_ok")
        g_one = sem("g_one")
        g_two = sem("g_two")
        g_hi = sem("g_hi")
        g_lo = sem("g_lo")

        steps = {"act": 0, "dve": 0, "pool": 0}
        chain = {"act": act_step, "dve": dve_step, "pool": pool_step}

        def link(eng, name, ins):
            steps[name] += 1
            ins.then_inc(chain[name], 1)
            eng.wait_ge(chain[name], steps[name])

        TAKERS = "aadd" + "aa" + "dd" + "aaaa" + "dd" + "dd" + "dddd" + "aa" + "ddd" + "aaaa" + "dd" + "dd"

        def wait_pair_free(pe, group):
            if group >= 2:
                who = TAKERS[group - 2]
                pe.wait_ge(taken_a if who == "a" else taken_d, 2 * TAKERS[:group - 1].count(who))

        XT_BANKS = 6

        def xt(t, k):
            per = 4 - 2 * t
            return ps[:, 2 * t + k // per, k % per * P:(k % per + 1) * P]

        def xt_bank(r, t, k):
            return r * XT_BANKS + 2 * t + k // (4 - 2 * t) + 1

        def xt_read(r, t, k):
            per = 4 - 2 * t
            return (2 * r + t) * KC + k // per * per + per

        def product(pe, o, lh, ll, rh, rl, first, last):
            pe.matmul(o, lh, rh, start=first, stop=False)
            pe.matmul(o, lh, rl, start=False, stop=False)
            return pe.matmul(o, ll, rh, start=False, stop=last)

        def multiply_tokens(pe, slot, k0, nk, width, bank0, first, last, xh, xl, chunk_wait=None, part=None,
                            meta_bank=None):
            vh = whi[slot][:].rearrange("p (k c) -> p k c", k=nk)
            vl = wlo[slot][:].rearrange("p (k c) -> p k c", k=nk)
            halves = max(1, width // BANK)
            wd = min(width, BANK)
            for k in range(nk) if part is None else range(part * nk // 2, (part + 1) * nk // 2):
                if chunk_wait is not None:
                    pe.wait_ge(xt_lo, chunk_wait + k0 + k + 1)
                for t in range(NT):
                    for half in range(halves):
                        m = product(pe, ps[:, bank0 + t * halves + half, 0:wd],
                                    xh[:, k0 + k, t * P:(t + 1) * P], xl[:, k0 + k, t * P:(t + 1) * P],
                                    vh[:, k, half * BANK:half * BANK + wd],
                                    vl[:, k, half * BANK:half * BANK + wd],
                                    first and k == 0, last and k == nk - 1)
            if meta_bank is not None:
                for k in range(nk) if part else []:
                    m = product(pe, ps[0:N_META, meta_bank, :], metaT_h[:, k0 + k, :], metaT_l[:, k0 + k, :],
                                vh[:, k, :], vl[:, k, :], first and k == 0, last and k == nk - 1)
            if part != 0:
                m.then_inc(blob_used, 1)

        def multiply_last_two(pe, n, k0, x, made, counts, between=None):
            slots = [slot_of(n), slot_of(n + 1)]
            for t in range(NT):
                for b in range(2):
                    if between is not None and t == 1 and b == 1:
                        between()
                    if t == 0:
                        pe.wait_ge(split_lo, n + b + 1)
                        pe.wait_ge(made, counts[b])
                    vh = whi[slots[b]][:].rearrange("p (k c) -> p k c", k=2)
                    vl = wlo[slots[b]][:].rearrange("p (k c) -> p k c", k=2)
                    xh, xl = x[b]
                    for k in range(2):
                        for half in range(2):
                            m = product(pe, ps[:, 4 + t * 2 + half, :], xh[:, k0[b] + k, t * P:(t + 1) * P],
                                        xl[:, k0[b] + k, t * P:(t + 1) * P], vh[:, k, half * BANK:(half + 1) * BANK],
                                        vl[:, k, half * BANK:(half + 1) * BANK], False, b == 1 and k == 1)
                    if t == 1:
                        m.then_inc(blob_used, 1)
                    elif b == 1:
                        m.then_inc(acc_ok, 1)

        def multiply_features(pe, slot, nk, ntile, bank0, xh, xl, chunk_wait=None, part=None):
            vh = whi[slot][:].rearrange("p (k c) -> p k c", k=nk)
            vl = wlo[slot][:].rearrange("p (k c) -> p k c", k=nk)
            for j in range(ntile) if part is None else range(part * ntile // 2, (part + 1) * ntile // 2):
                o = ps[:, bank0 + j // 2, (j % 2) * TOK:(j % 2 + 1) * TOK]
                for k in range(nk):
                    if chunk_wait is not None and j == 0:
                        pe.wait_ge(xt_lo, chunk_wait + k + 1)
                    m = product(pe, o, vh[:, k, j * P:(j + 1) * P], vl[:, k, j * P:(j + 1) * P],
                                xh[:, k, :], xl[:, k, :], k == 0, k == nk - 1)
            if part != 0:
                m.then_inc(blob_used, 1)

        block = ctx.enter_context(nc.Block())

        @block.sync
        def _(sp):
            def load(n, src, made):
                if made is not None:
                    sp.wait_ge(split_lo, made)
                sp.dma_start(raw[slot_of(n)][:], src).then_inc(raw_in[slot_of(n)], 16)

            for t in range(NT):
                sp.dma_start(h[:, t, :], x[:, t, :]).then_inc(x_in[t], 16)
            sp.dma_start(cst[:, 0:EARLY], consts[:, 0:EARLY]).then_inc(early_in, 16)
            sp.dma_start(col[:], cols).then_inc(early_in, 16)
            sp.dma_start(raw[0][:, 0:BLOB // 2], w[0][:, 0:BLOB // 2]).then_inc(first_in, 16)
            sp.dma_start(raw[0][:, BLOB // 2:BLOB], w[0][:, BLOB // 2:BLOB]).then_inc(raw_in[0], 16)
            for n in range(1, 3):
                load(n, w[n], None)
            sp.dma_start(cst[:, EARLY:NCONST], consts[:, EARLY:NCONST]).then_inc(const_in, 16)
            sp.dma_start(row[:], rows.partition_broadcast(P)).then_inc(const_in, 16)
            load(3, w[3], None)
            with sp.Fori(4, N1 - 4, 4) as i:
                for j in range(4):
                    load(j, w[bass.ds(i + j, 1)].rearrange("a p c -> (a p) c"), i + (j - 3))
            load(N1 - 1, w[N1 - 1], N1 - 1 - 3)
            whole = (NBLOB - N1) // 3 * 3
            with sp.Fori(N1, N1 + whole - 2, 3) as i:
                for j in range(3):
                    load(N1 + j, w[bass.ds(i + j, 1)].rearrange("a p c -> (a p) c"), i + (j - 2))
            for n in range(N1 + whole, NBLOB):
                load(n, w[n], n - 2)

        @block.scalar
        def _(act):
            def hi(n, i=0, per=0):
                s, depth = slot_of(n), depth_of(n)
                act.wait_ge(raw_in[s], i * (16 * per // depth) + 16 * fills(n))
                if n >= 4:
                    act.wait_ge(blob_used, i * per + used_before(n))
                act.activation(whi[s][:], raw[s][:], ACT.Copy).then_inc(split_hi, 1)

            norms = [0]

            def square(t):
                act.activation(xn[:, t, 0:BANK], h[:, t, 0:BANK], ACT.Square, scale=D ** -0.5,
                               accum_out=stat[:, t, 0:1]).then_inc(sq_a, 1)
                norms[0] += 1

            def normalise(t):
                act.wait_ge(rstd_ok, norms[0])
                act.activation(xn[:, t, 0:BANK], h[:, t, 0:BANK], ACT.Copy, scale=stat[:, t, 3:4]).then_inc(xn_a, 1)

            def to_features(r, gain, t):
                for k in range(KC):
                    act.wait_ge(xt_ps, xt_bank(r, t, k))
                    act.activation(xT_h[:, k, t * P:(t + 1) * P], xt(t, k), ACT.Copy,
                                   scale=cl(gain, k)).then_inc(xt_hi, 1)

            def exp_pairs(j):
                act.wait_ge(sc_ok, j + 1)
                st = soft[:, j % 2]
                for u in range(2):
                    act.activation(s1[j % 2][:, u, :], s1[j % 2][:, u, :], ACT.Exp, bias=st[:, 1, u:u + 1],
                                   accum_out=st[:, 3, u:u + 1])
                for u in range(2):
                    act.activation(s0[j % 2][:, u, :], s0[j % 2][:, u, :], ACT.Exp, bias=st[:, 1, 2 + u:3 + u],
                                   accum_out=st[:, 3, 2 + u:3 + u])
                act.activation(st[:, 2, :], st[:, 2, :], ACT.Exp).then_inc(ex_ok, 1)

            def gate(bank, dst, func, scale, bias):
                for b in range(2):
                    for j in range(2):
                        m = act.activation(dst[:, 2 * b + j, :], ps[:, bank + b, j * TOK:(j + 1) * TOK],
                                           func, scale=scale, bias=bias(2 * b + j))
                    m.then_inc(taken_a, 1)

            def merged_hi(count, merged=gate_a):
                act.wait_ge(mg_ok, count + 1)
                i = count % 4
                act.activation(xT_h[:, 2 * i:2 * i + 2, :], merged[:, 2 * i:2 * i + 2, :],
                               ACT.Copy).then_inc(mg_hi, 1)

            for t in range(NT):
                act.wait_ge(x_in[t], 16)
                square(t)
                normalise(t)
            act.wait_ge(early_in, 32)
            act.wait_ge(first_in, 16)
            act.activation(whi[0][:, 0:BLOB // 2], raw[0][:, 0:BLOB // 2], ACT.Copy).then_inc(first_hi, 1)
            for t in range(NT):
                to_features(0, "norm_mix", t)
            act.wait_ge(raw_in[0], 16)
            act.activation(whi[0][:, BLOB // 2:BLOB], raw[0][:, BLOB // 2:BLOB], ACT.Copy).then_inc(split_hi, 1)
            for n in range(1, 3):
                hi(n)

            for n in range(MIX1):
                if n < MIX1 - 1:
                    hi(n + 3)
                if n == 2:
                    act.wait_ge(blob_used, 2)
                    for t in range(NT):
                        act.activation(tok[0][:, t, :], ps[:, t, :], ACT.Copy).then_inc(taken_a, 1)
                if n == 3:
                    act.wait_ge(blob_used, 3)
                    act.wait_ge(init_ok, 3)
                    for t in range(NT):
                        act.activation(ka_tok[:, t, :], ps[:, 2 + t, 0:P], ACT.Copy)
                        act.activation(va[:, t, 0, 0:A_DIM], ps[:, 2 + t, P:P + A_DIM], ACT.Copy)
                        act.activation(va[:, t, 1, A_DIM:P], ps[:, 2 + t, P + A_DIM:2 * P],
                                       ACT.Copy).then_inc(taken_a, 1)
                if n == 4:
                    act.wait_ge(q_ps, 1)
                    for t in range(NT):
                        m = act.activation(qaT[:, :, t * P:(t + 1) * P],
                                           ps[:, 4 + t, :].rearrange("p (j q) -> p j q", j=4), ACT.Copy)
                    m.then_inc(q_ok, 1)
                    act.wait_ge(q_ps, 2)
                    act.activation(kaT[0:A_DIM, 0, :], ps[0:A_DIM, 6, 0:TOK], ACT.Copy)
                    act.activation(kaT[A_DIM:P, 1, :], ps[A_DIM:P, 6, 0:TOK], ACT.Copy).then_inc(q_ok, 1)
                if n in (7, 9):
                    dst, bank = (qrT, 4) if n == 7 else (krT, 6)
                    act.wait_ge(q_ps, 3 if n == 7 else 4)
                    for t in range(NT):
                        m = act.activation(dst[:, :, t * P:(t + 1) * P],
                                           ps[:, bank + t, :].rearrange("p (j q) -> p j q", j=4), ACT.Copy)
                    m.then_inc(q_ok, 1)
                if n in (9, 11):
                    act.wait_ge(blob_used, n)
                    hh = n - 9
                    for t in range(NT):
                        act.activation(vr[:, hh:hh + 2, t, :],
                                       ps[:, (n - 9) + t, :].rearrange("p (a v) -> p a v", a=2),
                                       ACT.Copy).then_inc(taken_a, 1)
                if n in (13, 15):
                    act.wait_ge(blob_used, n)
                    hh = n - 13
                    for t in range(NT):
                        act.activation(gr[:, hh:hh + 2, t, :],
                                       ps[:, (n - 13) + t, :].rearrange("p (a v) -> p a v", a=2),
                                       ACT.Sigmoid).then_inc(e_ok, 1)
                if n in (17, 19, 21, 23):
                    act.wait_ge(blob_used, n)
                    g = (n - 17) // 2
                    gate(2 * (g % 2), (gate_a if g < 2 else gate_r)[:, 4 * (g % 2):4 * (g % 2) + 4, :],
                         ACT.Sigmoid, 1.0, lambda j: cl("b_gates", 4 * g + j))
                if 12 <= n < 16:
                    j = n - 12
                    act.wait_ge(pt_ps, j + 1)
                    act.activation(pT[:, 4:6, :], ps[:, 7, 0:TOK].rearrange("p (a q) -> p a q", a=2),
                                   ACT.Copy).then_inc(pt_a, 1)
                if 13 <= n < 17:
                    j = n - 13
                    act.wait_ge(o_ps, j + 1)
                    act.activation(aT_h[:, j, :], ps[:, 7, TOK:2 * TOK], ACT.Copy).then_inc(o_hi, 1)
                if 10 <= n < 14:
                    exp_pairs(n - 10)
                if 18 <= n < 22:
                    r = n - 18
                    act.wait_ge(rt_ps, r + 1)
                    for j in range(2):
                        act.activation(retT_h[:, 2 * r + j, :], ps[:, 6, j * TOK:(j + 1) * TOK], ACT.Copy,
                                       scale=cl("ret_gn", 2 * r + j)).then_inc(rt_hi, 1)
                if 26 <= n < 30:
                    merged_hi(n - 26)
            for t in range(NT):
                act.wait_ge(h_ok, 2 * t + 1)
                square(t)
                normalise(t)
                to_features(1, "norm_mlp", t)
            hi(MIX1 + 2)

            def hidden_relu(k, used, made=None):
                if made is not None:
                    act.wait_ge(ff_lo, made)
                act.wait_ge(blob_used, used)
                act.activation(f_sq[k][:], ps[:, k, :].rearrange("p (a q) -> p a q", a=2), ACT.Relu).then_inc(ff_relu, 1)

            def hidden_hi(k, count):
                act.wait_ge(ff_sq, count)
                act.activation(fT_h[k][:], f_sq[k][:], ACT.Copy).then_inc(ff_hi, 1)

            act.dma_start(gain_row[:], grow[0].partition_broadcast(P)).then_inc(row_in, 16)
            act.dma_start(meta_tok[:], meta).then_inc(meta_in, 16)
            b = MIX1
            hi(b + 3)
            hi(b + 4)
            hidden_relu(0, b + 1)
            hidden_relu(1, b + 2)
            hidden_hi(0, 1)
            act.wait_ge(meta_in, 16)
            act.activation(xn[0:N_META, 0, :], meta_tok[:], ACT.Square, accum_out=mstat[:, 0:1]).then_inc(meta_sq, 1)
            act.wait_ge(meta_r, 1)
            act.activation(meta_tok[:], meta_tok[:], ACT.Copy, scale=mstat[:, 2:3]).then_inc(meta_n, 1)
            with act.Fori(0, STEP1 - 1) as i:
                b = MIX1 + 2
                hi(b + 3, i, 4)
                hidden_hi(1, i * 2 + 2)
                hi(b + 4, i, 4)
                hidden_relu(0, i * 4 + (b + 1), i * 2 + 1)
                hi(b + 5, i, 4)
                hidden_relu(1, i * 4 + (b + 2), i * 2 + 2)
                hi(b + 6, i, 4)
                hidden_hi(0, i * 2 + 3)
            b = N1 - 2
            act.wait_ge(blob_used, N1 - 2)
            hidden_hi(1, 2 * STEP1)
            hi(b + 3)
            act.wait_ge(meta_g, 1)
            act.activation(metaT_h[:], metaT[:], ACT.Copy).then_inc(meta_hi, 1)

            for t in range(NT):
                act.wait_ge(h_ok, 4 * t + 5)
                square(t)
                act.wait_ge(h_ok, 4 * t + 7)
                square(t)
                normalise(t)
            for t in range(NT):
                to_features(2, "pre_mix", t)
            hi(N1 + 2)

            def copy_halves(dst, variant, bank):
                act.activation(dst[0:DH, variant, :], ps[0:DH, bank, 0:KEYS], ACT.Copy)
                return act.activation(dst[DH:P, variant + 1, :], ps[DH:P, bank, 0:KEYS], ACT.Copy)

            for q in range(2 * OUT2):
                m = q // 2
                if q == 4:
                    act.wait_ge(blob_used, N1 + 2)
                    act.wait_ge(zero2, 1)
                    for u in range(2):
                        for t in range(NT):
                            v = ps[:, t, 256:512].rearrange("p (a u d) -> p a u d", a=2, u=2)
                            act.activation(vs[:, t, :, u, u * DH:(u + 1) * DH], v[:, :, u, :], ACT.Copy)
                        v = ps[0:N_META, 6, 256:512].rearrange("p (a u d) -> p a u d", a=2, u=2)
                        ins = act.activation(vs_meta[:, :, u, u * DH:(u + 1) * DH], v[:, :, u, :], ACT.Copy)
                    ins.then_inc(sv_ok, 1)
                if q in (6, 10, 11, 14, 15):
                    r = (6, 10, 11, 14, 15).index(q)
                    act.wait_ge(kt_ps, r + 1)
                    for cc in range(2):
                        ins = copy_halves(*((ksT, 2 * cc) if r == 0 else (kbT, 4 * (r - 1) + 2 * cc)), 4 + cc)
                    ins.then_inc(kt_ok, 1)
                if q in (18, 30, 34, 38):
                    r = (18, 30, 34, 38).index(q)
                    g = (3, 6, 7, 8)[r]
                    act.wait_ge(q_ps, 5 + r)
                    for t in range(NT):
                        ins = act.activation(
                            (qsT if r < 2 else qbT)[:, 4 * (r % 2):4 * (r % 2) + 4, t * P:(t + 1) * P],
                            ps[:, 2 * (g % 2) + t, :].rearrange("p (j q) -> p j q", j=4), ACT.Copy)
                    ins.then_inc(q_ok, 1)
                if q in (20, 24):
                    half = (q - 20) // 4
                    act.wait_ge(blob_used, N1 + m)
                    for t in range(NT):
                        act.activation(vb[:, t, half * BANK:(half + 1) * BANK], ps[:, 2 * half + t, :],
                                       ACT.Copy).then_inc(taken_a, 1)
                    act.activation(vb_meta[:, half * BANK:(half + 1) * BANK], ps[0:N_META, 7 - half, :],
                                   ACT.Copy).then_inc(mtaken_a, 1)
                U = q - U0 - 3
                if 0 <= U < UNITS:
                    act.wait_ge(u_pt, U + 1)
                    heads = 2 if U < S_UNITS else 1
                    act.activation(pmT[:, 0:heads, :], ps[0:N_META, 7, 32:32 + heads * P].rearrange(
                        "p (a q) -> p a q", a=heads), ACT.Copy).then_inc(u_ptm, 1)
                U = q - U0 - 4
                if 0 <= U < UNITS:
                    act.wait_ge(u_o, U + 1)
                    cc, t = U % S_UNITS // 2, U % 2
                    if U < S_UNITS:
                        act.activation(sT_h[:, cc, t * P:(t + 1) * P], ps[:, 7, 288:288 + P],
                                       ACT.Copy).then_inc(s_hi, 1)
                    else:
                        if U - S_UNITS >= 2:
                            act.wait_ge(d_ps, U - S_UNITS - 1)
                        act.activation(o_junk[:], ps[:, 7, 288:288 + P], ACT.Square,
                                       accum_out=ostat[:, U % 2, 0:1])
                        act.activation(o_tok[U % 2][:], ps[:, 7, 288:288 + P], ACT.Copy).then_inc(d_o, 1)
                V = q - U0 - 6 - S_UNITS
                if 0 <= V < UNITS - S_UNITS:
                    act.wait_ge(d_ps, V + 1)
                    act.wait_ge(u_sc, min(UNITS, q - U0))
                    act.activation(dT_h[:, V // 2, V % 2 * P:(V % 2 + 1) * P], ps[:, 5, P:2 * P], ACT.Copy,
                                   scale=subgain[:]).then_inc(d_hi, 1)
                if q == 2:
                    act.wait_ge(lam_s, 1)
                    act.activation(lam[:, 2:4], lam[:, 0:2], ACT.Exp).then_inc(lam_e, 1)
                U = q - U0 - 1
                if 0 <= U < UNITS:
                    act.wait_ge(u_max, U + 1)
                    st = usoft[:, U % 2]
                    for u in range(2):
                        ins = act.activation(sc[U % 2][:, u, :], sc[U % 2][:, u, :], ACT.Exp,
                                             bias=st[:, 2, u:u + 1], accum_out=st[:, 4, u:u + 1])
                    if U < S_UNITS:
                        ins = act.activation(st[:, 3, :], st[:, 3, :], ACT.Exp)
                    ins.then_inc(u_exp, 1)
                if q in (40, 44, 48, 52):
                    g = (q - 40) // 4
                    act.wait_ge(blob_used, N1 + m)
                    gate(2 * ((g + 1) % 2), (gate_s if g < 2 else gate_d)[:, 4 * (g % 2):4 * (g % 2) + 4, :],
                         ACT.Sigmoid, 1.0, lambda j: cl("b_gate_2", 4 * g + j))
                if q == 2 * OUT2 - 8:
                    act.wait_ge(u_sc, UNITS)
                    act.dma_start(gain_rows[:], grow[1:3].partition_broadcast(P)).then_inc(rows_in, 16)
                if q % 2 == 0 and m:
                    hi(N1 + m + 2)
                if q % 2 == 0 and m > OUT2 - 4:
                    merged_hi(4 + m - (OUT2 - 3), gate_s)
            for m in range(OUT2, MIX2 - 1):
                if m == OUT2:
                    merged_hi(7, gate_s)
                hi(N1 + m + 2)

            def square_acc(t, product, last_blob):
                if t == 0:
                    act.wait_ge(acc_ok, product)
                else:
                    act.wait_ge(blob_used, last_blob)
                act.activation(xn[:, t, 0:BANK], acc[t][:, 0:BANK], ACT.Square, scale=D ** -0.5,
                               accum_out=stat[:, t, 0:1]).then_inc(acc_a, 1)
                act.wait_ge(acc_d, 2 * (product - 3) + t + 1)
                act.activation(xn[:, t, BANK:D], acc[t][:, BANK:D], ACT.Square, scale=D ** -0.5,
                               accum_out=stat[:, t, 1:2]).then_inc(sq_a, 1)
                norms[0] += 1

            for t in range(NT):
                square_acc(t, 3, F2)
                act.wait_ge(h_ok, 2 * t + 13)
                square(t)
                if t == 1:
                    to_features(3, "pre_ffn", 0)
                normalise(t)
            to_features(3, "pre_ffn", 1)
            hi(F2 + 1)
            hi(F2 + 2)

            def silu_one(j, used, i=0):
                act.wait_ge(blob_used, used)
                act.activation(g_act[:], ps[:, 0, :].rearrange("p (a q) -> p a q", a=2),
                               ACT.Sigmoid).then_inc(gs_ok, 1)

            def hidden2_hi(made, dst=gT_h):
                act.wait_ge(g_two, made)
                act.activation(dst[:], g_act[:], ACT.Copy).then_inc(g_hi, 1)

            hi(F2 + 3)
            silu_one(0, F2 + 1)
            hi(F2 + 4)
            hidden2_hi(1)
            with act.Fori(0, STEP2 - 2) as i:
                hi(F2 + 5, i, 3)
                act.wait_ge(g_lo, i + 1)
                silu_one(0, i * 3 + (F2 + 3))
                hi(F2 + 6, i, 3)
                hi(F2 + 7, i, 3)
                hidden2_hi(i + 2)
            hi(NBLOB - 1)
            act.wait_ge(g_lo, STEP2 - 1)
            silu_one(0, F2 + 3 * STEP2 - 3)
            hidden2_hi(STEP2, gL_h)

            for t in range(NT):
                square_acc(t, 4, NBLOB)
            for t in range(NT):
                for half in range(2):
                    a = half * BANK
                    act.wait_ge(h_ok, 17 + 2 * t + half)
                    act.dma_start(out[:, t, a:a + BANK], h[:, t, a:a + BANK]).then_inc(out_done, 16)
            act.wait_ge(out_done, 64)

        @block.gpsimd
        def _(pool):
            def rsqrt(dst, mid, src, scale, rows=P):
                link(pool, "pool", pool.tensor_scalar(mid, src, scale, EPS, ALU.mult, ALU.add))
                return pool.tensor_tensor(dst, mid, c("neghalf")[0:rows, 0:dst.shape[-1]], ALU.pow)

            shares = [0, 0]

            def rms(t, both=True):
                shares[0] += 1
                pool.wait_ge(sq_a, shares[0])
                if both:
                    shares[1] += 1
                    pool.wait_ge(sq_d, shares[1])
                st = stat[:, t]
                link(pool, "pool", pool.tensor_scalar(st[:, 2:3], st[:, 0:1], st[:, 1:2], EPS, ALU.add, ALU.add))
                pool.tensor_tensor(st[:, 3:4], st[:, 2:3], c("neghalf")[:, 0:1], ALU.pow).then_inc(rstd_ok, 1)

            pool.wait_ge(early_in, 32)
            rms(0)
            rms(1)
            pool.wait_ge(const_in, 32)
            for r in range(R_HEADS):
                pool.wait_ge(rv_ok, r + 1)
                rsqrt(gn_r[:, r % 2, :], gn_mid[:, r % 2, :], gn_mv[:, r % 2, :, 1], 1.0).then_inc(rr_ok, 1)
            rms(0)
            rms(1)
            pool.wait_ge(meta_sq, 1)
            rsqrt(mstat[:, 2:3], mstat[:, 1:2], mstat[:, 0:1], 1.0 / D, N_META).then_inc(meta_r, 1)
            for t in range(NT):
                rms(t)
                rms(t)

            pool.wait_ge(blob_used, N1)
            pool.wait_ge(h_ok, 12)
            pool.memset(ksT[:], 0.0)
            pool.memset(vs[:], 0.0)
            pool.memset(vs_meta[:], 0.0)
            pool.memset(kbT[:], 0.0).then_inc(zero2, 1)

            for V in range(UNITS - S_UNITS):
                pool.wait_ge(d_o, V + 1)
                st = ostat[:, V % 2]
                link(pool, "pool", rsqrt(st[:, 2:3], st[:, 1:2], st[:, 0:1], 1.0 / P))
                pool.tensor_scalar(o_tok[V % 2][:], o_tok[V % 2][:], st[:, 2:3], None, ALU.mult).then_inc(d_n, 1)
            for t in range(NT):
                rms(t, False)
                rms(t)
            for t in range(NT):
                rms(t, False)

        @block.tensor
        def _(pe):
            ident = c("ident")

            def features(r, t):
                pe.wait_ge(xn_a, 2 * r + t + 1)
                for k in range(KC):
                    if k == 4:
                        pe.wait_ge(xn_d, 2 * r + t + 1)
                    m = pe.transpose(xt(t, k), xn[:, t, k * P:(k + 1) * P], ident)
                    if k % (4 - 2 * t) == 3 - 2 * t:
                        m.then_inc(xt_ps, 1)

            def keep_warm(times, bank, x=None, columns=BANK):
                for _ in range(times):
                    pe.matmul(ps[:, bank, 0:columns], ident if x is None else x[:, 0:P],
                              cst[:, 0:columns] if x is None else x[:, 0:columns], start=True, stop=True)

            def transpose4(bank, src, signal):
                for t in range(NT):
                    for j in range(4):
                        m = pe.transpose(ps[:, bank + t, j * P:(j + 1) * P], src(t, j), ident)
                m.then_inc(signal, 1)

            pe.wait_ge(early_in, 32)
            for t in range(NT):
                features(0, t)
            for n in range(MIX1):
                if n == 0:
                    pe.wait_ge(first_lo, 1)
                    multiply_tokens(pe, 0, 0, 4, BANK, 0, True, False, xT_h, xT_l, KC, 0)
                    pe.wait_ge(split_lo, 1)
                    multiply_tokens(pe, 0, 0, 4, BANK, 0, True, False, xT_h, xT_l, KC, 1)
                    continue
                if n < MIX1 - 2:
                    pe.wait_ge(split_lo, n + 1)
                if n < 2:
                    multiply_tokens(pe, n % 4, 4 * n, 4, BANK, 0, n == 0, n == 1, xT_h, xT_l, KC)
                elif n == 2:
                    multiply_tokens(pe, n % 4, 0, KC, TOK, 2, True, True, xT_h, xT_l)
                elif n < 15:
                    g = 2 + (n - 3) // 2
                    first = n % 2 == 1
                    if first:
                        wait_pair_free(pe, g)
                    multiply_tokens(pe, n % 4, 0 if first else 4, 4, BANK, 2 * (g % 2), first, not first, xT_h, xT_l)
                elif n < 23:
                    g = 8 + (n - 15) // 2
                    if n % 2 == 1:
                        wait_pair_free(pe, g)
                    multiply_features(pe, n % 4, KC, 2, 2 * (g % 2) + (n - 15) % 2, xT_h, xT_l)
                elif n < 25:
                    g = 12 + n - 23
                    wait_pair_free(pe, g)
                    pe.wait_ge(o_lo, 4)
                    multiply_features(pe, n % 4, 4, 4, 2 * (g % 2), aT_h, aT_l)
                elif n < 29:
                    g = 14 + (n - 25) // 2
                    if n % 2 == 1:
                        wait_pair_free(pe, g)
                    pe.wait_ge(rt_lo, KC)
                    multiply_features(pe, n % 4, KC, 2, 2 * (g % 2) + (n - 25) % 2, retT_h, retT_l)
                elif n < MIX1 - 2:
                    pe.wait_ge(mg_lo, n - 29 + 1)
                    multiply_tokens(pe, n % 4, 2 * (n - 29), 2, D, 4, n == 29, False, xT_h, xT_l)

                if n == 3:
                    pe.wait_ge(rope_ok, 1)
                    transpose4(4, lambda t, j: tok[0][:, t, j * P:(j + 1) * P], q_ps)
                    pe.wait_ge(rope_ok, 2)
                    for t in range(NT):
                        m = pe.transpose(ps[:, 6, t * P:(t + 1) * P], ka_tok[:, t, :], ident)
                    m.then_inc(q_ps, 1)
                if n == 6:
                    pe.wait_ge(rope_ok, 3)
                    pe.wait_ge(q_ok, 1)
                    transpose4(4, lambda t, j: tok[1][:, t, j * P:(j + 1) * P], q_ps)
                if n == 8:
                    pe.wait_ge(rope_ok, 4)
                    pe.wait_ge(q_ok, 2)
                    transpose4(6, lambda t, j: tok[0][:, t, j * P:(j + 1) * P], q_ps)
                if 12 <= n < 16:
                    j = n - 12
                    pe.wait_ge(pt_a, j + 1)
                    pe.wait_ge(pt_d, j + 1)
                    if j >= 1:
                        pe.wait_ge(o_lo, j)
                    for u in range(2):
                        pe.matmul(ps[:, 7, TOK:TOK + P], va[:, 0, u, :], pT[:, 4 + u, :], start=u == 0, stop=u == 1)
                    for u in range(2):
                        for kt in range(NT):
                            m = pe.matmul(ps[:, 7, TOK + P:2 * TOK], va[:, kt, u, :], pT[:, 2 * u + kt, :],
                                          start=u + kt == 0, stop=u + kt == 2)
                    m.then_inc(o_ps, 1)
                if 11 <= n < 15:
                    j = n - 11
                    pe.wait_ge(pr_ok, j + 1)
                    if j == 0:
                        pe.wait_ge(q_ok, 4)
                    else:
                        pe.wait_ge(pt_d, j)
                        pe.wait_ge(pt_a, j)
                    if j >= 2:
                        pe.wait_ge(o_lo, j - 1)
                    for u in range(2):
                        for kt in range(NT):
                            pe.transpose(ps[:, 6, (2 * u + kt) * P:(2 * u + kt + 1) * P],
                                         s1[j % 2][:, u, kt * P:(kt + 1) * P], ident)
                    for u in range(2):
                        m = pe.transpose(ps[:, 7, u * P:(u + 1) * P], s0[j % 2][:, u, :], ident)
                    m.then_inc(pt_ps, 1)
                if 9 <= n < 13:
                    j = n - 9
                    if j == 0:
                        pe.wait_ge(q_ok, 3)
                    else:
                        pe.wait_ge(sc_ok, j)
                    for u in range(2):
                        pe.matmul(ps[:, 4, u * TOK:(u + 1) * TOK], qaT[:, j, P:TOK], kaT[:, u, :], start=True, stop=True)
                        m = pe.matmul(ps[:, 5, u * P:(u + 1) * P], qaT[:, j, 0:P], kaT[:, u, 0:P], start=True, stop=True)
                    m.then_inc(sc_ps, 1)
                if 17 <= n < 21:
                    r = n - 17
                    pe.wait_ge(rn_ok, r + 1)
                    if r == 0:
                        pe.wait_ge(pt_d, 4)
                    else:
                        pe.wait_ge(rt_lo, 2 * r)
                    for j in range(2):
                        for t in range(NT):
                            m = pe.transpose(ps[:, 6, j * TOK + t * P:j * TOK + (t + 1) * P],
                                             gr[:, r, t, j * P:(j + 1) * P], ident)
                    m.then_inc(rt_ps, 1)
                if 15 <= n < 19:
                    r = n - 15
                    pe.wait_ge(at_ok, r + 1)
                    if r == 0:
                        pe.wait_ge(taken_a, 8)
                    else:
                        pe.wait_ge(rn_ok, r)
                    pe.matmul(ps[:, 5, 0:TOK], decayed[:, 0:P], vr[:, r, 0, :], start=True, stop=True)
                    pe.matmul(ps[:, 5, TOK:2 * TOK], decayed[:, P:2 * P], vr[:, r, 0, :], start=True, stop=False)
                    pe.matmul(ps[:, 5, TOK:2 * TOK], decayed[:, 2 * P:3 * P], vr[:, r, 1, :],
                              start=False, stop=True).then_inc(ro_ps, 1)
                if 14 <= n < 18:
                    r = n - 14
                    if r == 0:
                        pe.wait_ge(sc_ok, 4)
                    else:
                        pe.wait_ge(at_ok, r)
                    pe.matmul(ps[:, 4, 0:TOK], krT[:, r, 0:P], qrT[:, r, :], start=True, stop=True)
                    pe.matmul(ps[:, 4, TOK:TOK + P], krT[:, r, P:TOK], qrT[:, r, P:TOK],
                              start=True, stop=True).then_inc(at_ps, 1)

            multiply_last_two(pe, MIX1 - 2, (4, 6), [(xT_h, xT_l)] * 2, mg_lo, (3, 4),
                              lambda: features(1, 0))
            keep_warm(3, 4)
            features(1, 1)

            def hidden(n, k, i=0, last_read=None, chunk_wait=None, per=4):
                pe.wait_ge(split_lo, i * per + n + 1)
                if last_read is not None:
                    pe.wait_ge(ff_relu, last_read)
                multiply_features(pe, slot_of(n), KC, 2, k, xT_h, xT_l, chunk_wait)

            def down(n, k, made, i=0, first=False, last=False, per=4):
                pe.wait_ge(split_lo, i * per + n + 1)
                pe.wait_ge(ff_lo, made)
                multiply_tokens(pe, slot_of(n), 0, 2, D, 4, first, last, fT_h[k], fT_l[k])

            hidden(MIX1, 0, chunk_wait=3 * KC)
            hidden(MIX1 + 1, 1)
            b = MIX1 + 2
            hidden(b, 0, last_read=1)
            hidden(b + 1, 1, last_read=2)
            down(b + 2, 0, 1, first=True)
            pe.wait_ge(meta_n, 1)
            for k in range(KC):
                m = pe.transpose(ps[:, 2, k * N_META:(k + 1) * N_META], meta_tok[:, k * P:(k + 1) * P],
                                 ident[0:N_META, 0:N_META])
            m.then_inc(meta_ps, 1)
            down(b + 3, 1, 2)
            with pe.Fori(1, STEP1 - 1) as i:
                hidden(b, 0, i, i * 2 + 1)
                hidden(b + 1, 1, i, i * 2 + 2)
                down(b + 2, 0, i * 2 + 1, i)
                down(b + 3, 1, i * 2 + 2, i)
            multiply_last_two(pe, N1 - 2, (0, 0), list(zip(fT_h, fT_l)), ff_lo, (2 * STEP1 - 1, 2 * STEP1))

            def first_group(t):
                for b in range(2):
                    n = N1 + b
                    vh = whi[slot_of(n)][:].rearrange("p (k c) -> p k c", k=4)
                    vl = wlo[slot_of(n)][:].rearrange("p (k c) -> p k c", k=4)
                    for k in range(4):
                        kk = 4 * b + k
                        if t is None:
                            m = product(pe, ps[0:N_META, 6, :], metaT_h[:, kk, :], metaT_l[:, kk, :], vh[:, k, :],
                                        vl[:, k, :], kk == 0, kk == KC - 1)
                        else:
                            pe.wait_ge(xt_lo, (4 + t) * KC + max(4, kk + 1) if t == 0 else 5 * KC + kk + 1)
                            m = product(pe, ps[:, t, :], xT_h[:, kk, t * P:(t + 1) * P],
                                        xT_l[:, kk, t * P:(t + 1) * P], vh[:, k, :], vl[:, k, :], kk == 0, kk == KC - 1)
                    if t == 1:
                        m.then_inc(blob_used, 1)

            pe.wait_ge(split_lo, N1 + 2)
            pe.wait_ge(meta_lo, 1)
            pe.wait_ge(h_ok, 10)
            first_group(None)
            for t in range(NT):
                features(2, t)
            for t in range(NT):
                first_group(t)

            def slot(q):
                if q in (5, 9, 10, 13, 14):
                    r = (5, 9, 10, 13, 14).index(q)
                    pe.wait_ge(rope_ok, (5, 6, 6, 7, 7)[r])
                    if r:
                        pe.wait_ge(kt_ok, r)
                    for cc in range(2):
                        if r == 0:
                            src, mt, a = ks_tok, mk[0], cc * P
                        else:
                            src, mt, a = tok2[(r - 1) // 2], mk[(1, 0)[(r - 1) // 2]], ((r - 1) % 2 * 2 + cc) * P
                        for t in range(NT):
                            pe.transpose(ps[:, 4 + cc, t * P:(t + 1) * P], src[:, t, a:a + P], ident)
                        m = pe.transpose(ps[:, 4 + cc, TOK:KEYS], mt[:, a:a + P], ident[0:N_META, 0:N_META])
                    m.then_inc(kt_ps, 1)
                if q in (17, 29, 33, 37):
                    r = (17, 29, 33, 37).index(q)
                    g, buf = (3, 6, 7, 8)[r], tok2[r % 2]
                    pe.wait_ge(rope_ok, 8 + r)
                    transpose4(2 * (g % 2), lambda t, j: buf[:, t, j * P:(j + 1) * P], q_ps)
                U = q - U0 - 3
                if 0 <= U < UNITS:
                    pe.wait_ge(u_ptd, U + 1)
                    pe.wait_ge(u_ptm, U + 1)
                    if 0 < U <= S_UNITS:
                        pe.wait_ge(s_lo, U)
                    elif U > S_UNITS:
                        pe.wait_ge(d_o, U - S_UNITS)
                    cc, o = U % S_UNITS // 2, ps[:, 7, 288:288 + P]
                    if U < S_UNITS:
                        for u in range(2):
                            for kt in range(NT):
                                pe.matmul(o, vs[:, kt, cc // 4, u, :], puT[:, 2 * u + kt, :], start=u + kt == 0,
                                          stop=False)
                            m = pe.matmul(o, vs_meta[:, cc // 4, u, :], pmT[:, u, :], start=False, stop=u == 1)
                    else:
                        for kt in range(NT):
                            pe.matmul(o, puT[:, kt, :], vb[:, kt, cc * P:(cc + 1) * P], start=kt == 0, stop=False)
                        m = pe.matmul(o, pmT[:, 0, :], vb_meta[:, cc * P:(cc + 1) * P], start=False, stop=True)
                    m.then_inc(u_o, 1)
                U = q - U0 - 2
                if 0 <= U < UNITS:
                    pe.wait_ge(u_pr, U + 1)
                    if U == 0:
                        pe.wait_ge(mtaken_a, 2)
                    else:
                        pe.wait_ge(u_ptd, U)
                        pe.wait_ge(u_ptm, U)
                    heads = 2 if U < S_UNITS else 1
                    for u in range(heads):
                        for kt in range(NT):
                            pe.transpose(ps[:, 6, (2 * u + kt) * P:(2 * u + kt + 1) * P],
                                         sc[U % 2][:, u, kt * P:(kt + 1) * P], ident)
                    for u in range(heads):
                        m = pe.transpose(ps[0:N_META, 7, 32 + u * P:32 + (u + 1) * P], sc[U % 2][:, u, TOK:KEYS],
                                         ident)
                    m.then_inc(u_pt, 1)
                V = q - U0 - 5 - S_UNITS
                if 0 <= V < UNITS - S_UNITS:
                    pe.wait_ge(d_n, V + 1)
                    pe.wait_ge(u_max, min(UNITS, q - U0))
                    if V:
                        pe.wait_ge(d_lo, V)
                    pe.transpose(ps[:, 5, P:2 * P], o_tok[V % 2][:], ident).then_inc(d_ps, 1)
                U = q - U0
                if 0 <= U < UNITS:
                    cc, t = U % S_UNITS // 2, U % 2
                    pe.wait_ge(q_ok, 5 + U // 8)
                    if U == 0:
                        pe.wait_ge(kt_ok, 5)
                    else:
                        pe.wait_ge(u_max, U)
                    if q - U0 - 6 - S_UNITS >= 0:
                        pe.wait_ge(d_lo, q - U0 - 5 - S_UNITS)
                    qT = qsT if U < S_UNITS else qbT
                    for u in range(2):
                        kT = ksT[:, 2 * (cc // 4) + u, :] if U < S_UNITS else kbT[:, 2 * cc + u, :]
                        pe.matmul(ps[:, 4, u * TOK:(u + 1) * TOK], qT[:, cc, t * P:(t + 1) * P], kT[:, 0:TOK],
                                  start=True, stop=True)
                        m = pe.matmul(ps[:, 5, u * N_META:(u + 1) * N_META], qT[:, cc, t * P:(t + 1) * P],
                                      kT[:, TOK:KEYS], start=True, stop=True)
                    m.then_inc(u_sc, 1)

            for m2 in range(OUT2):
                n = N1 + m2
                pe.wait_ge(split_lo, n + 1)
                for part in range(2):
                    if m2 < 2:
                        pass
                    elif m2 < 18:
                        g, first = m2 // 2, m2 % 2 == 0
                        meta_bank = {1: 7, 2: 6, 4: 7, 5: 6}.get(g)
                        if first and part == 0:
                            if g >= 2:
                                wait_pair_free(pe, 16 + g)
                            if g - 2 in (3, 6, 7, 8):
                                pe.wait_ge(q_ok, 5 + (3, 6, 7, 8).index(g - 2))
                        if first and part == 1 and g in (2, 4, 5):
                            pe.wait_ge(mtaken_d, {2: 1, 4: 2, 5: 3}[g])
                        multiply_tokens(pe, slot_of(n), 0 if first else 4, 4, BANK, 2 * (g % 2), first, not first,
                                        xT_h, xT_l, None, part, meta_bank)
                    else:
                        g = 9 + (m2 - 18) // 2
                        if m2 % 2 == 0 and part == 0:
                            wait_pair_free(pe, 16 + g)
                            if g - 2 in (7, 8):
                                pe.wait_ge(q_ok, g - 2)
                            if m2 == 26:
                                pe.wait_ge(s_lo, S_UNITS)
                            if m2 == 30:
                                pe.wait_ge(d_lo, UNITS - S_UNITS)
                        xh, xl = (xT_h, xT_l) if m2 < 26 else (sT_h, sT_l) if m2 < 30 else (dT_h, dT_l)
                        multiply_features(pe, slot_of(n), KC, 2, 2 * (g % 2) + m2 % 2, xh, xl, None, part)
                    slot(2 * m2 + part)
            for i in range(2):
                n = N1 + OUT2 + i
                pe.wait_ge(split_lo, n + 1)
                pe.wait_ge(mg_lo, 4 + i + 1)
                multiply_tokens(pe, slot_of(n), 2 * i, 2, D, 4, i == 0, False, xT_h, xT_l)
            multiply_last_two(pe, F2 - 2, (4, 6), [(xT_h, xT_l)] * 2, mg_lo, (7, 8))

            features(3, 0)
            keep_warm(4, 5)
            features(3, 1)

            def hidden2(n, bank, signal, read, i=0, chunk_wait=None):
                pe.wait_ge(split_lo, i * 3 + n + 1)
                if signal is not None:
                    pe.wait_ge(signal, read)
                multiply_features(pe, slot_of(n), KC, 2, bank, xT_h, xT_l, chunk_wait)

            def down2(n, made, i=0, first=False, last=False):
                pe.wait_ge(split_lo, i * 3 + n + 1)
                pe.wait_ge(g_lo, made)
                multiply_tokens(pe, slot_of(n), 0, 2, D, 4, first, last, gT_h, gT_l)

            hidden2(F2, 0, None, 0, chunk_wait=7 * KC)
            hidden2(F2 + 1, 1, None, 0)
            hidden2(F2 + 2, 0, g_one, 1)
            hidden2(F2 + 3, 1, g_two, 1)
            down2(F2 + 4, 1, first=True)
            with pe.Fori(0, STEP2 - 3) as i:
                hidden2(F2 + 5, 0, g_one, i + 2, i)
                hidden2(F2 + 6, 1, g_two, i + 2, i)
                down2(F2 + 7, i + 2, i)
            hidden2(NBLOB - 4, 0, g_one, STEP2 - 1)
            hidden2(NBLOB - 3, 1, g_two, STEP2 - 1)
            multiply_last_two(pe, NBLOB - 2, (0, 0), [(gT_h, gT_l), (gL_h, gL_l)], g_lo, (STEP2 - 1, STEP2))

        @block.vector
        def _(dve):
            freed, mfreed, rotated = [0], [0], [0]

            def free(ins):
                freed[0] += 1
                ins.then_inc(taken_d, 1)
                dve.wait_ge(taken_d, freed[0])

            def lo(n, i=0, per=0):
                s = slot_of(n)
                dve.wait_ge(split_hi, i * per + n + 1)
                dve.tensor_tensor(wlo[s][:], raw[s][:], whi[s][:], ALU.subtract).then_inc(split_lo, 1)

            norms = [0]

            def square(t):
                dve.tensor_tensor_reduce(out=xn[:, t, BANK:D], in0=h[:, t, BANK:D], in1=h[:, t, BANK:D],
                                         scale=1.0 / D, scalar=0.0, op0=ALU.mult, op1=ALU.add,
                                         accum_out=stat[:, t, 1:2]).then_inc(sq_d, 1)
                norms[0] += 1

            def normalise(t):
                dve.wait_ge(rstd_ok, norms[0])
                dve.tensor_scalar(xn[:, t, BANK:D], h[:, t, BANK:D], stat[:, t, 3:4], None, ALU.mult).then_inc(xn_d, 1)

            def to_features(r, gain, t):
                for k in range(KC):
                    dve.wait_ge(xt_hi, xt_read(r, t, k))
                    dve.scalar_tensor_tensor(out=xT_l[:, k, t * P:(t + 1) * P], in0=xt(t, k), scalar=cl(gain, k),
                                             in1=xT_h[:, k, t * P:(t + 1) * P], op0=ALU.mult,
                                             op1=ALU.subtract).then_inc(xt_lo, 1)

            added = [0]

            def add_product(t, product, last_blob):
                if t == 0:
                    dve.wait_ge(acc_ok, product)
                else:
                    dve.wait_ge(blob_used, last_blob)
                for half in range(2):
                    v = h[:, t, half * BANK:(half + 1) * BANK]
                    dve.tensor_tensor(v, acc[t][:, half * BANK:(half + 1) * BANK], v, ALU.add).then_inc(h_ok, 1)
                added[0] += 2
                dve.wait_ge(h_ok, added[0])

            def rope_window(buf, heads, t, signal):
                v = buf.rearrange("p (a d) -> p a d", d=A_DIM)
                cs = c("a_cos")[:, t * A_ROPE:(t + 1) * A_ROPE].unsqueeze(1).to_broadcast([P, heads, A_ROPE])
                sn = c("a_sin")[:, t * A_ROPE:(t + 1) * A_ROPE]
                half = A_ROPE // 2
                tmp = scratch[:, 0:heads * A_ROPE].rearrange("p (a d) -> p a d", a=heads)
                dve.tensor_tensor(tmp[:, :, 0:half], v[:, :, half:A_ROPE],
                                  sn[:, 0:half].unsqueeze(1).to_broadcast([P, heads, half]), ALU.mult)
                link(dve, "dve", dve.tensor_tensor(
                    tmp[:, :, half:A_ROPE], v[:, :, 0:half],
                    sn[:, half:A_ROPE].unsqueeze(1).to_broadcast([P, heads, half]), ALU.mult))
                link(dve, "dve", dve.tensor_tensor(v[:, :, 0:A_ROPE], v[:, :, 0:A_ROPE], cs, ALU.mult))
                m = dve.tensor_tensor(v[:, :, 0:A_ROPE], v[:, :, 0:A_ROPE], tmp, ALU.add)
                if signal is None:
                    link(dve, "dve", m)
                else:
                    m.then_inc(signal, 1)
                    rotated[0] += 1
                    dve.wait_ge(signal, rotated[0])

            def rope_whole(dst, bank, heads, d, cs, sn, signal, spare=scratch, rows=P):
                v = ps[0:rows, bank, 0:heads * d].rearrange("p (a d) -> p a d", a=heads)
                o = dst.rearrange("p (a d) -> p a d", a=heads)
                tmp = spare[0:rows, 0:heads * d].rearrange("p (a d) -> p a d", a=heads)
                half = d // 2
                dve.tensor_tensor(tmp[:, :, 0:half], v[:, :, half:d],
                                  sn[:, 0:half].unsqueeze(1).to_broadcast([rows, heads, half]), ALU.mult)
                dve.tensor_tensor(tmp[:, :, half:d], v[:, :, 0:half],
                                  sn[:, half:d].unsqueeze(1).to_broadcast([rows, heads, half]), ALU.mult)
                m = dve.tensor_tensor(o, v, cs.unsqueeze(1).to_broadcast([rows, heads, d]), ALU.mult)
                if rows == P:
                    free(m)
                else:
                    mfreed[0] += 1
                    m.then_inc(mtaken_d, 1)
                    dve.wait_ge(mtaken_d, mfreed[0])
                m = dve.tensor_tensor(o, o, tmp, ALU.add)
                if signal is None:
                    link(dve, "dve", m)
                else:
                    m.then_inc(signal, 1)
                    rotated[0] += 1
                    dve.wait_ge(signal, rotated[0])

            def merge(i, n, first=gate_a, second=gate_r, spare=scratch, bank=0, before=0):
                a = first[:, 2 * i:2 * i + 2, :].rearrange("p a q -> p (a q)")
                r = second[:, 2 * i:2 * i + 2, :].rearrange("p a q -> p (a q)")
                dve.wait_ge(blob_used, n)
                free(dve.tensor_tensor(spare[:], ps[:, (bank + i) % 4, :], r, ALU.mult))
                dve.tensor_tensor(a, spare[:], a, ALU.add).then_inc(mg_ok, 1)
                dve.wait_ge(mg_hi, before + i + 1)
                dve.tensor_tensor(xT_l[:, 2 * i:2 * i + 2, :], first[:, 2 * i:2 * i + 2, :],
                                  xT_h[:, 2 * i:2 * i + 2, :], ALU.subtract).then_inc(mg_lo, 1)

            def softmax_front(j):
                dve.wait_ge(sc_ps, j + 1)
                if j >= 2:
                    dve.wait_ge(pt_ps, j - 1)
                st = soft[:, j % 2]
                m1 = cst[:, CONST["gt"][0]:CONST["gt"][0] + 2 * P]
                dve.scalar_tensor_tensor(out=s1[j % 2][:], in0=ps[:, 4, :].rearrange("p (a k) -> p a k", a=2),
                                         scalar=A_DIM ** -0.5, in1=m1.unsqueeze(1).to_broadcast([P, 2, 2 * P]),
                                         op0=ALU.mult, op1=ALU.add)
                link(dve, "dve", dve.scalar_tensor_tensor(
                    out=s0[j % 2][:], in0=ps[:, 5, 0:TOK].rearrange("p (a k) -> p a k", a=2), scalar=A_DIM ** -0.5,
                    in1=c("diag1").unsqueeze(1).to_broadcast([P, 2, P]), op0=ALU.mult, op1=ALU.add))
                dve.tensor_reduce(st[:, 0, 0:2], s1[j % 2][:], AX.X, ALU.max)
                link(dve, "dve", dve.tensor_reduce(st[:, 0, 2:4], s0[j % 2][:], AX.X, ALU.max))
                link(dve, "dve", dve.scalar_tensor_tensor(out=st[:, 1, :], in0=st[:, 0, :], scalar=-1.0,
                                                          in1=negsink[:, 4 * j:4 * j + 4], op0=ALU.mult, op1=ALU.min))
                dve.tensor_tensor(st[:, 2, :], st[:, 1, :], negsink[:, 4 * j:4 * j + 4],
                                  ALU.subtract).then_inc(sc_ok, 1)

            def softmax_back(j):
                dve.wait_ge(ex_ok, j + 1)
                st = soft[:, j % 2]
                link(dve, "dve", dve.tensor_tensor(st[:, 3, :], st[:, 3, :], st[:, 2, :], ALU.add))
                link(dve, "dve", dve.reciprocal(st[:, 4, :], st[:, 3, :]))
                for u in range(2):
                    dve.tensor_scalar(s1[j % 2][:, u, :], s1[j % 2][:, u, :], st[:, 4, u:u + 1], None, ALU.mult)
                for u in range(2):
                    m = dve.tensor_scalar(s0[j % 2][:, u, :], s0[j % 2][:, u, :], st[:, 4, 2 + u:3 + u], None, ALU.mult)
                m.then_inc(pr_ok, 1)

            def step_lambda():
                a = ROWS["lambdas"][0]
                for v in range(2):
                    m = dve.tensor_tensor_reduce(
                        out=scratch2[:, v * DH:(v + 1) * DH], in0=row[:, a + 2 * v * DH:a + (2 * v + 1) * DH],
                        in1=row[:, a + (2 * v + 1) * DH:a + (2 * v + 2) * DH], scale=1.0, scalar=0.0, op0=ALU.mult,
                        op1=ALU.add, accum_out=lam[:, v:v + 1])
                m.then_inc(lam_s, 1)
                dve.tensor_scalar(subgain[:], cl("subln"), 1.0 - LAMBDA, None, ALU.mult)
                dve.wait_ge(lam_e, 1)
                dve.scalar_tensor_tensor(out=neglam[:], in0=lam[:, 3:4], scalar=-LAMBDA, in1=lam[:, 2:3],
                                         op0=ALU.add, op1=ALU.subtract).then_inc(lam_ok, 1)

            def unit_front(U):
                dve.wait_ge(u_sc, U + 1)
                if U >= 2:
                    dve.wait_ge(u_pt, U - 1)
                st, s = usoft[:, U % 2], sc[U % 2]
                if U < S_UNITS:
                    a = CONST["ge" if U % 2 else "zero"][0]
                    mask = cst[:, a:a + TOK]
                else:
                    mask = None
                for u in range(2):
                    for part, (src, a, b) in enumerate(((ps[:, 4, u * TOK:(u + 1) * TOK], 0, TOK),
                                                        (ps[:, 5, u * N_META:(u + 1) * N_META], TOK, KEYS))):
                        if part == 0 and mask is not None:
                            add = mask
                        elif part == 0:
                            add = c("zero").unsqueeze(1).to_broadcast([P, 2, P])
                            src = src.rearrange("p (a k) -> p a k", a=2)
                        else:
                            add = c("zero")[:, 0:N_META]
                        o = s[:, u, a:b]
                        if part == 0 and mask is None:
                            o = o.rearrange("p (a k) -> p a k", a=2)
                        m = dve.tensor_tensor_reduce(out=o, in0=src, in1=add, scale=DH ** -0.5, scalar=NEG,
                                                     op0=ALU.add, op1=ALU.max, accum_out=st[:, part, u:u + 1])
                link(dve, "dve", m)
                link(dve, "dve", dve.tensor_tensor(st[:, 0, :], st[:, 0, :], st[:, 1, :], ALU.max))
                if U < S_UNITS:
                    sink = negsink[:, 2 * A_HEADS + U // 2 * 2:2 * A_HEADS + U // 2 * 2 + 2]
                    link(dve, "dve", dve.scalar_tensor_tensor(out=st[:, 2, :], in0=st[:, 0, :], scalar=-1.0, in1=sink,
                                                              op0=ALU.mult, op1=ALU.min))
                    dve.tensor_tensor(st[:, 3, :], st[:, 2, :], sink, ALU.subtract).then_inc(u_max, 1)
                else:
                    dve.tensor_scalar(st[:, 2, :], st[:, 0, :], -1.0, None, ALU.mult).then_inc(u_max, 1)

            def unit_back(U):
                dve.wait_ge(u_exp, U + 1)
                st, s = usoft[:, U % 2], sc[U % 2]
                if U < S_UNITS:
                    link(dve, "dve", dve.tensor_tensor(st[:, 4, :], st[:, 4, :], st[:, 3, :], ALU.add))
                link(dve, "dve", dve.reciprocal(st[:, 5, :], st[:, 4, :]))
                if U < S_UNITS:
                    for u in range(2):
                        ins = dve.tensor_scalar(s[:, u, :], s[:, u, :], st[:, 5, u:u + 1], None, ALU.mult)
                else:
                    dve.tensor_tensor(st[:, 5, 1:2], st[:, 5, 1:2], neglam[:], ALU.mult)
                    link(dve, "dve", dve.tensor_scalar(s[:, 0, :], s[:, 0, :], st[:, 5, 0:1], None, ALU.mult))
                    ins = dve.scalar_tensor_tensor(out=s[:, 0, :], in0=s[:, 1, :], scalar=st[:, 5, 1:2],
                                                   in1=s[:, 0, :], op0=ALU.mult, op1=ALU.add)
                ins.then_inc(u_pr, 1)

            dve.memset(kaT[:], 0.0).then_inc(init_ok, 1)
            dve.memset(va[:], 0.0).then_inc(init_ok, 1)
            for t in range(NT):
                dve.wait_ge(x_in[t], 16)
                square(t)
                normalise(t)
            dve.wait_ge(early_in, 32)
            dve.wait_ge(first_hi, 1)
            dve.tensor_tensor(wlo[0][:, 0:BLOB // 2], raw[0][:, 0:BLOB // 2], whi[0][:, 0:BLOB // 2],
                              ALU.subtract).then_inc(first_lo, 1)
            for t in range(NT):
                to_features(0, "norm_mix", t)
            dve.wait_ge(split_hi, 1)
            dve.tensor_tensor(wlo[0][:, BLOB // 2:BLOB], raw[0][:, BLOB // 2:BLOB], whi[0][:, BLOB // 2:BLOB],
                              ALU.subtract).then_inc(split_lo, 1)
            dve.wait_ge(const_in, 32)
            dve.tensor_scalar(negsink[:], row[:, 0:2 * A_HEADS + S_HEADS], -1.0, None, ALU.mult).then_inc(init_ok, 1)
            for n in range(1, 3):
                lo(n)

            for n in range(MIX1):
                if n < MIX1 - 1:
                    lo(n + 3)
                if n == 2:
                    dve.wait_ge(taken_a, 2)
                    rope_window(tok[0][:, 0, :], A_HEADS, 0, None)
                    rope_window(tok[0][:, 1, :], A_HEADS, 1, rope_ok)
                if n == 3:
                    dve.wait_ge(taken_a, 4)
                    rope_window(ka_tok[:, 0, :], 2, 0, None)
                    rope_window(ka_tok[:, 1, :], 2, 1, rope_ok)
                if n in (5, 7):
                    dve.wait_ge(blob_used, n)
                    if n == 7:
                        dve.wait_ge(q_ps, 1)
                    for t in range(NT):
                        rope_whole(tok[1 if n == 5 else 0][:, t, :], (n - 5) + t, R_HEADS, R_KEY,
                                   c("ret_cos")[:, t * P:(t + 1) * P], c("ret_sin")[:, t * P:(t + 1) * P],
                                   rope_ok if t == 1 else None)
                if n in (13, 15):
                    hh = n - 13
                    v = gr[:, hh:hh + 2]
                    for t in range(NT):
                        dve.wait_ge(e_ok, 2 * (hh // 2) + t + 1)
                        free(dve.tensor_tensor(v[:, :, t, :], ps[:, (n - 13) + t, :].rearrange("p (a v) -> p a v", a=2),
                                               v[:, :, t, :], ALU.mult))
                if 12 <= n < 16:
                    j = n - 12
                    dve.wait_ge(pt_ps, j + 1)
                    dve.tensor_copy(pT[:, 0:4, :], ps[:, 6, :].rearrange("p (a q) -> p a q", a=4)).then_inc(pt_d, 1)
                if 13 <= n < 17:
                    j = n - 13
                    dve.wait_ge(o_hi, j + 1)
                    dve.wait_ge(pt_a, min(4, j + 2))
                    dve.tensor_tensor(aT_l[:, j, :], ps[:, 7, TOK:2 * TOK], aT_h[:, j, :],
                                      ALU.subtract).then_inc(o_lo, 1)
                if 11 <= n < 15:
                    softmax_back(n - 11)
                if 10 <= n < 14:
                    softmax_front(n - 10)
                if 18 <= n < 22:
                    r = n - 18
                    dve.wait_ge(rt_hi, 2 * r + 2)
                    for j in range(2):
                        dve.scalar_tensor_tensor(out=retT_l[:, 2 * r + j, :], in0=ps[:, 6, j * TOK:(j + 1) * TOK],
                                                 scalar=cl("ret_gn", 2 * r + j), in1=retT_h[:, 2 * r + j, :],
                                                 op0=ALU.mult, op1=ALU.subtract).then_inc(rt_lo, 1)
                if 16 <= n < 20:
                    r = n - 16
                    b = r % 2
                    dve.wait_ge(ro_ps, r + 1)
                    for t in range(NT):
                        m = dve.bn_stats(gn_stat[:, b, t, :], ps[:, 5, t * TOK:(t + 1) * TOK])
                    link(dve, "dve", m)
                    for t in range(NT):
                        m = dve.bn_aggr(gn_mv[:, b, t, :], gn_stat[:, b, t, :])
                    m.then_inc(rv_ok, 1)
                    dve.wait_ge(rv_ok, r + 1)
                    for t in range(NT):
                        m = dve.scalar_tensor_tensor(out=gr[:, r, t, :], in0=ps[:, 5, t * TOK:(t + 1) * TOK],
                                                     scalar=gn_mv[:, b, t, 0:1], in1=gr[:, r, t, :],
                                                     op0=ALU.subtract, op1=ALU.mult)
                    link(dve, "dve", m)
                    dve.wait_ge(rr_ok, r + 1)
                    for t in range(NT):
                        m = dve.tensor_scalar(gr[:, r, t, :], gr[:, r, t, :], gn_r[:, b, t:t + 1], None, ALU.mult)
                    m.then_inc(rn_ok, 1)
                if 15 <= n < 19:
                    r = n - 15
                    dve.wait_ge(at_ps, r + 1)
                    if r:
                        dve.wait_ge(ro_ps, r)
                    dve.tensor_tensor(decayed[:], ps[:, 4, 0:3 * P], c("decay")[:, r * 3 * P:(r + 1) * 3 * P],
                                      ALU.mult).then_inc(at_ok, 1)
                if n in (24, 25):
                    v = gate_a[:, 4 * (n - 24):4 * (n - 24) + 4, :].rearrange("p a q -> p (a q)")
                    dve.wait_ge(blob_used, n)
                    for b in range(2):
                        free(dve.tensor_tensor(v[:, b * BANK:(b + 1) * BANK], ps[:, 2 * (n - 24) + b, :],
                                               v[:, b * BANK:(b + 1) * BANK], ALU.mult))
                if 26 <= n < 30:
                    merge(n - 26, n)
            for t in range(NT):
                add_product(t, 1, MIX1)
                square(t)
                normalise(t)
                to_features(1, "norm_mlp", t)
            lo(MIX1 + 2)

            def hidden_square(k, count):
                dve.wait_ge(ff_relu, count)
                dve.tensor_tensor(f_sq[k][:], f_sq[k][:], f_sq[k][:], ALU.mult).then_inc(ff_sq, 1)

            def hidden_lo(k, count):
                dve.wait_ge(ff_hi, count)
                dve.tensor_tensor(fT_l[k][:], f_sq[k][:], fT_h[k][:], ALU.subtract).then_inc(ff_lo, 1)

            b = MIX1
            lo(b + 3)
            lo(b + 4)
            hidden_square(0, 1)
            hidden_square(1, 2)
            hidden_lo(0, 1)
            with dve.Fori(0, STEP1 - 1) as i:
                b = MIX1 + 2
                lo(b + 3, i, 4)
                hidden_lo(1, i * 2 + 2)
                lo(b + 4, i, 4)
                hidden_square(0, i * 2 + 3)
                lo(b + 5, i, 4)
                hidden_square(1, i * 2 + 4)
                lo(b + 6, i, 4)
                hidden_lo(0, i * 2 + 3)
            b = N1 - 2
            hidden_lo(1, 2 * STEP1)
            lo(b + 3)
            dve.wait_ge(meta_ps, 1)
            dve.tensor_tensor(metaT[:], ps[:, 2, 0:KC * N_META].rearrange("p (a q) -> p a q", a=KC),
                              cl("pre_mix", 0, KC).unsqueeze(2).to_broadcast([P, KC, N_META]),
                              ALU.mult).then_inc(meta_g, 1)
            dve.wait_ge(meta_hi, 1)
            dve.tensor_tensor(metaT_l[:], metaT[:], metaT_h[:], ALU.subtract).then_inc(meta_lo, 1)
            dve.wait_ge(row_in, 16)
            for t in range(NT):
                add_product(t, 2, N1)
                square(t)
                dve.wait_ge(rstd_ok, norms[0])
                for half in range(2):
                    v = h[:, t, half * BANK:(half + 1) * BANK]
                    dve.scalar_tensor_tensor(out=v, in0=v, scalar=stat[:, t, 3:4],
                                             in1=gain_row[:, half * BANK:(half + 1) * BANK], op0=ALU.mult,
                                             op1=ALU.mult).then_inc(h_ok, 1)
                added[0] += 2
                dve.wait_ge(h_ok, added[0])
                square(t)
                normalise(t)
            for t in range(NT):
                to_features(2, "pre_mix", t)
            lo(N1 + 2)

            for q in range(2 * OUT2):
                m2 = q // 2
                if q == 1:
                    step_lambda()
                U = q - U0 - 3
                if 0 <= U < UNITS:
                    dve.wait_ge(u_pt, U + 1)
                    if U:
                        dve.wait_ge(u_o, U)
                    n = 4 if U < S_UNITS else 2
                    dve.tensor_copy(puT[:, 0:n, :], ps[:, 6, 0:n * P].rearrange("p (a q) -> p a q", a=n)).then_inc(
                        u_ptd, 1)
                U = q - U0 - 4
                if 0 <= U < S_UNITS:
                    cc, t = U // 2, U % 2
                    dve.wait_ge(s_hi, U + 1)
                    dve.tensor_tensor(sT_l[:, cc, t * P:(t + 1) * P], ps[:, 7, 288:288 + P],
                                      sT_h[:, cc, t * P:(t + 1) * P], ALU.subtract).then_inc(s_lo, 1)
                V = q - U0 - 6 - S_UNITS
                if 0 <= V < UNITS - S_UNITS:
                    cc, t = V // 2, V % 2
                    dve.wait_ge(d_hi, V + 1)
                    dve.scalar_tensor_tensor(out=dT_l[:, cc, t * P:(t + 1) * P], in0=ps[:, 5, P:2 * P],
                                             scalar=subgain[:], in1=dT_h[:, cc, t * P:(t + 1) * P], op0=ALU.mult,
                                             op1=ALU.subtract).then_inc(d_lo, 1)
                U = q - U0 - 1
                if 0 <= U < UNITS:
                    unit_front(U)
                if q % 2 == 1 and 1 <= m2 and m2 < OUT2:
                    lo(N1 + m2 + 2)
                if 0 <= U < UNITS:
                    unit_back(U)
                if q in (4, 8, 12, 16, 28, 32, 36):
                    r = (4, 8, 12, 16, 28, 32, 36).index(q)
                    g = (0, 1, 2, 3, 6, 7, 8)[r]
                    dve.wait_ge(blob_used, N1 + m2)
                    if r == 0:
                        dve.wait_ge(sv_ok, 1)
                        dst, heads = ks_tok, S_KV
                    else:
                        dst, heads = tok2[(0, 1, 0, 1, 0, 1)[r - 1]], F_HEADS
                    if r in (2, 3, 4):
                        dve.wait_ge(kt_ps, {2: 1, 3: 3, 4: 5}[r])
                    if r in (5, 6):
                        dve.wait_ge(q_ps, r)
                    for t in range(NT + 1 if r < 3 else NT):
                        cs, sn = (c(name)[:, t * DH:(t + 1) * DH] for name in ("h_cos", "h_sin"))
                        if t < NT:
                            last = t == NT - 1 and r >= 3
                            rope_whole(dst[:, t, :], 2 * (g % 2) + t, heads, DH, cs, sn, rope_ok if last else None,
                                       scratch2)
                        else:
                            rope_whole(mk[r % 2][:, 0:heads * DH], 6 + r % 2, heads, DH, cs[0:N_META],
                                       sn[0:N_META], rope_ok, scratch2, N_META)
                if q in (56, 60):
                    g = (q - 56) // 4
                    dve.wait_ge(blob_used, N1 + m2)
                    for b in range(2):
                        v = gate_s[:, 4 * g + 2 * b:4 * g + 2 * b + 2, :].rearrange("p a q -> p (a q)")
                        free(dve.tensor_tensor(v, ps[:, (2 + 2 * g + b) % 4, :], v, ALU.mult))
                if q % 2 == 0 and m2 > OUT2 - 4:
                    merge(m2 - (OUT2 - 3), N1 + m2, gate_s, gate_d, scratch2, 2, 4)
            for m2 in range(OUT2, MIX2 - 1):
                if m2 == OUT2:
                    merge(3, N1 + OUT2, gate_s, gate_d, scratch2, 2, 4)
                lo(N1 + m2 + 2)

            def add_normalised(t, product, last_blob, k):
                if t == 0:
                    dve.wait_ge(acc_ok, product)
                else:
                    dve.wait_ge(blob_used, last_blob)
                for half in (1, 0):
                    a = half * BANK
                    if half == 0:
                        dve.wait_ge(acc_a, 2 * k + t + 1)
                    m = dve.tensor_tensor(ag[:, t, a:a + BANK], acc[t][:, a:a + BANK], gain_rows[:, k, a:a + BANK],
                                          ALU.mult)
                    if half == 1:
                        m.then_inc(acc_d, 1)
                link(dve, "dve", m)
                norms[0] += 1
                dve.wait_ge(rstd_ok, norms[0])
                for half in range(2):
                    v = h[:, t, half * BANK:(half + 1) * BANK]
                    dve.scalar_tensor_tensor(out=v, in0=ag[:, t, half * BANK:(half + 1) * BANK],
                                             scalar=stat[:, t, 3:4], in1=v, op0=ALU.mult,
                                             op1=ALU.add).then_inc(h_ok, 1)
                added[0] += 2
                dve.wait_ge(h_ok, added[0])

            dve.wait_ge(rows_in, 16)
            for t in range(NT):
                add_normalised(t, 3, F2, 0)
                square(t)
                if t == 1:
                    to_features(3, "pre_ffn", 0)
                normalise(t)
            to_features(3, "pre_ffn", 1)
            lo(F2 + 1)
            lo(F2 + 2)

            def gate_product(made):
                dve.wait_ge(gs_ok, made)
                v = g_act[:].rearrange("p a q -> p (a q)")
                dve.tensor_tensor(v, ps[:, 0, :], v, ALU.mult).then_inc(g_one, 1)

            def up_product(made, used):
                dve.wait_ge(g_one, made)
                dve.wait_ge(blob_used, used)
                v = g_act[:].rearrange("p a q -> p (a q)")
                dve.tensor_tensor(v, ps[:, 1, :], v, ALU.mult).then_inc(g_two, 1)

            def hidden2_lo(made, low=gT_l, high=gT_h):
                dve.wait_ge(g_hi, made)
                dve.tensor_tensor(low[:], g_act[:], high[:], ALU.subtract).then_inc(g_lo, 1)

            lo(F2 + 3)
            gate_product(1)
            up_product(1, F2 + 2)
            lo(F2 + 4)
            hidden2_lo(1)
            with dve.Fori(0, STEP2 - 2) as i:
                lo(F2 + 5, i, 3)
                gate_product(i + 2)
                lo(F2 + 6, i, 3)
                up_product(i + 2, i * 3 + (F2 + 4))
                lo(F2 + 7, i, 3)
                hidden2_lo(i + 2)
            lo(NBLOB - 1)
            gate_product(STEP2)
            up_product(STEP2, F2 + 3 * STEP2 - 2)
            hidden2_lo(STEP2, gL_l, gL_h)
            for t in range(NT):
                add_normalised(t, 4, NBLOB, 1)



def blob_tokens(w, c0, width=BANK):
    nk = BLOB // width
    v = w[:, c0:c0 + width].reshape(-1, nk, P, width)
    return [v[i].transpose(1, 0, 2).reshape(P, BLOB) for i in range(v.shape[0])]


def head_pairs(w, first, axis):
    n = w.shape[axis] // DH
    order = [8 * p + 4 * u + a for p in range(n // 8) for a in range(4) for u in range(2)]
    v = np.moveaxis(w, axis, 0).reshape((n, DH) + tuple(np.delete(w.shape, axis)))
    return np.moveaxis(v[order].reshape((n * DH,) + v.shape[2:]), 0, axis)


def weight_stream(i):
    w = np.asarray(i["w_in"])[0]
    at = np.cumsum([0, 512, 128, 128, 512, 512, 1024, 1024, 1024, 1024])
    out = []
    out += blob_tokens(head_pairs(w[:, 0:512], 0, 1), 0)
    out += blob_tokens(w, at[1], 256)
    for a in range(3, 5):
        out += blob_tokens(w, at[a])
    for a in range(5, 7):
        out += blob_tokens(w, at[a]) + blob_tokens(w, at[a] + BANK)
    for a in range(7, 9):
        for q in range(4):
            out += blob_tokens(w, at[a] + 256 * q, 256)
    att = head_pairs(np.asarray(i["w_att_up"])[0], 0, 0)
    out += blob_tokens(att, 0) + blob_tokens(att, BANK)
    up = np.asarray(i["w_ret_up"])[0]
    for q in range(4):
        out += blob_tokens(up, 256 * q, 256)
    out += blob_tokens(np.asarray(i["w_out"])[0], 0, D)
    ff1, ff2 = np.asarray(i["w_ff1"])[0], np.asarray(i["w_ff2"])[0]
    down = blob_tokens(ff2, 0, D)
    for j in range(STEP1):
        out += blob_tokens(ff1, 512 * j, 256) + blob_tokens(ff1, 512 * j + 256, 256)
        if j:
            out += down[2 * j - 2:2 * j]
    out += down[-2:]
    assert len(out) == N1

    w = np.asarray(i["w_in_2"])[0]
    at = np.cumsum([0, 1024, 256, 256, 1024, 1024, 1024])
    qa = head_pairs(w[:, 0:1024], 0, 1)
    out += blob_tokens(w, at[1])
    out += blob_tokens(w, at[4]) + blob_tokens(w, at[4] + BANK)
    out += blob_tokens(qa, 0)
    out += blob_tokens(w, at[5]) + blob_tokens(w, at[5] + BANK)
    out += blob_tokens(qa, BANK)
    out += blob_tokens(w, at[3]) + blob_tokens(w, at[3] + BANK)
    for q in range(8):
        out += blob_tokens(w, at[6] + 256 * q, 256)
    for up in (head_pairs(np.asarray(i["w_branch_swa_2"])[0], 0, 0), np.asarray(i["w_branch_diff_2"])[0]):
        for q in range(4):
            out += blob_tokens(up, 256 * q, 256)
    out += blob_tokens(np.asarray(i["w_out_2"])[0], 0, D)
    assert len(out) == F2
    up, down = np.asarray(i["w_ffn_in_2"])[0], blob_tokens(np.asarray(i["w_ffn_out_2"])[0], 0, D)
    for j in range(STEP2):
        out += blob_tokens(up, 256 * j, 256) + blob_tokens(up, FF2 + 256 * j, 256)
        if j:
            out += down[j - 1:j]
    out += down[-1:]
    assert len(out) == NBLOB
    return out


def constants():
    out = np.zeros((P, NCONST), np.float32)

    def put(name, v):
        a, n = CONST[name]
        out[:v.shape[0], a:a + n] = v.reshape(v.shape[0], n)

    f = np.float32
    q, k = np.arange(P)[:, None], np.arange(P)[None, :]
    put("ident", np.eye(P, dtype=f))
    put("gt", np.where(k > q, 0, NEG))
    put("diag1", np.where(k <= q, 0, NEG))
    put("ge", np.where(k >= q, 0, NEG))
    put("diag2", np.where(k <= q, 0, NEG))
    lg = np.log1p(-np.exp2(-5.0 - np.arange(R_HEADS)))
    dec = np.zeros((P, R_HEADS, 3, P))
    kk, qq = np.arange(P)[:, None], np.arange(P)[None, :]
    for r in range(R_HEADS):
        dec[:, r, 0] = np.where(qq >= kk, np.exp(np.maximum(qq - kk, 0) * lg[r]), 0)
        dec[:, r, 1] = np.exp((P + qq - kk) * lg[r])
        dec[:, r, 2] = dec[:, r, 0]
    put("decay", dec * R_KEY ** -0.5)

    def rope(pos, dim, theta):
        inv = f(theta) ** (-np.arange(0, dim, 2, dtype=f) / f(dim))
        ang = pos.astype(f)[:, None] * inv[None, :].astype(f)
        cs, sn = np.cos(ang.astype(np.float64)), np.sin(ang.astype(np.float64))
        return np.concatenate([cs, cs], 1), np.concatenate([-sn, sn], 1)

    for name, dim, theta in (("a", A_ROPE, 500000.0), ("ret", R_KEY, 10000.0)):
        for part, v in zip(("_cos", "_sin"), rope(np.arange(TOK), dim, theta)):
            put(name + part, v.reshape(NT, P, dim).transpose(1, 0, 2).copy())
    for part, v in zip(("_cos", "_sin"), rope(np.arange(KEYS), DH, 10000.0)):
        a, n = CONST["h" + part]
        t = out[:, a:a + n].reshape(P, NT + 1, DH)
        t[:, 0:NT] = v[N_META:].reshape(NT, P, DH).transpose(1, 0, 2)
        t[:N_META, NT] = v[:N_META]
        out[:, a:a + n] = t.reshape(P, n)
    put("neghalf", np.full((P, 2), -0.5))
    return out


def kernel(**inputs):
    import concourse.bacc as bacc
    from concourse.bass_utils import run_bass_kernel_spmd

    i = {k: np.asarray(v) for k, v in inputs.items()}
    x = i["x"][0].reshape(NT, P, D).transpose(1, 0, 2)
    cols = np.zeros((P, NCOLS), np.float32)
    for name, key in (("norm_mix", "norm_mix_gain"), ("norm_mlp", "norm_mlp_gain"), ("ret_gn", "ret_gn_gain"),
                      ("b_gates", "b_gates"), ("pre_mix", "pre_mix_gain_2"), ("b_gate_2", "b_gate_2"),
                      ("pre_ffn", "pre_ffn_gain_2"), ("subln", "diff_subln_gain_2")):
        a, n = COLS[name]
        cols[:, a:a + n] = i[key].reshape(n, P).T
    s = i["attn_sinks"][0]
    s2 = i["attn_sink_2"][0]
    rows = np.concatenate(
        [np.concatenate([s[[j, j + 4, j, j + 4]] for j in range(4)]),
         s2[[8 * p + 4 * u + a for p in range(2) for a in range(4) for u in range(2)]],
         i["lambda_q1_2"][0], i["lambda_k1_2"][0], i["lambda_q2_2"][0], i["lambda_k2_2"][0]])
    grow = np.stack([i["norm_final_gain"], i["post_mix_gain_2"][0], i["post_ffn_gain_2"][0]])
    arrays = {
        "weights": np.stack(weight_stream(i)),
        "x_tiles": x,
        "meta": i["meta_tokens_2"],
        "consts": constants(),
        "cols": cols,
        "rows": rows,
        "gain_rows": grow,
    }
    arrays = {k: np.ascontiguousarray(v) for k, v in arrays.items()}
    nc = bacc.Bacc("TRN2", target_bir_lowering=False, num_devices=1)
    args = [nc.dram_tensor(k, v.shape, mybir.dt.from_np(v.dtype), kind="ExternalInput").ap() for k, v in arrays.items()]
    y = nc.dram_tensor("y", (P, NT, D), F32, kind="ExternalOutput").ap()
    build(nc, *args, y)
    r = run_bass_kernel_spmd(nc, [arrays], core_ids=[0])
    return r.results[0]["y"].transpose(1, 0, 2).reshape(1, TOK, D)
```

```python
from contextlib import ExitStack

import numpy as np

import concourse.bass as bass
from concourse import mybir

F32 = mybir.dt.float32
F32R = mybir.dt.float32r
ALU = mybir.AluOpType
ACT = mybir.ActivationFunctionType
AX = mybir.AxisListType

P = 128
D = 1024
TOK = 256
NT = TOK // P
KC = D // P
BANK = 512
BLOB = 2048
EPS = 1e-6
NEG = -1e30

A_HEADS, A_DIM, A_ROPE, A_WINDOW = 8, 64, 16, 128
R_HEADS, R_KEY, R_VAL = 4, 128, 256
FF1 = 4096
N_META = 16
S_HEADS, S_KV, DH = 16, 4, 64
F_HEADS = 8
FF2 = 2816
LAMBDA = 0.8 - 0.6
KEYS = TOK + N_META

MIX1 = 2 + 1 + 2 + 2 + 4 + 4 + 4 + 4 + 2 + 4 + 4
STEP1 = FF1 // 512
N1 = MIX1 + 4 * STEP1
OUT2 = 34
U0, S_UNITS, UNITS = 22, 16, 32
MIX2 = 2 + 4 + 4 + 4 + 4 + 4 + 4 + 4 + 4 + 4
STEP2 = FF2 // 256
F2 = N1 + MIX2
NBLOB = F2 + 3 * STEP2

CONST = {}
for _name, _width in (("ident", P), ("neghalf", 2), ("a_cos", NT * A_ROPE), ("a_sin", NT * A_ROPE),
                      ("ge", P), ("zero", P), ("diag2", P), ("pad", 6),
                      ("h_cos", (NT + 1) * DH), ("h_sin", (NT + 1) * DH),
                      ("gt", P), ("diag1", P), ("ret_cos", NT * P), ("ret_sin", NT * P),
                      ("decay", R_HEADS * 3 * P)):
    CONST[_name] = (sum(w for _, w in CONST.values()), _width)
NCONST = sum(w for _, w in CONST.values())
EARLY = P + 2

COLS = {}
for _name, _width in (("norm_mix", KC), ("norm_mlp", KC), ("ret_gn", KC), ("b_gates", 2 * KC),
                      ("pre_mix", KC), ("b_gate_2", 2 * KC), ("pre_ffn", KC), ("subln", 1)):
    COLS[_name] = (sum(w for _, w in COLS.values()), _width)
NCOLS = sum(w for _, w in COLS.values())

ROWS = {}
for _name, _width in (("sinks", A_HEADS * 2), ("sinks_2", S_HEADS), ("lambdas", 4 * DH)):
    ROWS[_name] = (sum(w for _, w in ROWS.values()), _width)
NROWS = sum(w for _, w in ROWS.values())


def slot_of(n):
    return n % 4 if n < N1 else 1 + (n - N1) % 3


def depth_of(n):
    return 4 if n < N1 else 3


def used_before(n):
    return n - 3 if n < N1 + 3 else n - 2


def fills(n):
    if n < N1:
        return n // 4 + 1
    return (N1 - 1) // 4 + 1 + (n - N1) // 3


def build(nc, w, x, meta, consts, cols, rows, grow, out):
    with ExitStack() as ctx:
        def sem(name):
            return ctx.enter_context(nc.semaphore(name))

        base = (nc.sbuf_base + 127) // 128 * 128
        top = [0]

        def at(name, shape, dt, offset):
            return nc.alloc_sbuf_tensor_at(name, shape, dt, offset=base + 4 * offset)

        def new(name, shape, dt=F32):
            size = (int(np.prod(shape[1:])) + 7) // 8 * 8
            top[0] += size
            assert base + 4 * top[0] <= nc.sbuf_usable_end, (name, top[0])
            return at(name, shape, dt, top[0] - size)

        raw, whi, wlo = [None] * 4, [None] * 4, [None] * 4
        for s in range(4):
            raw[s] = new(f"raw{s}", [P, BLOB])
            whi[s] = new(f"whi{s}", [P, BLOB], F32R)
            wlo[s] = new(f"wlo{s}", [P, BLOB], F32R)
        xT_h = new("xT_h", [P, KC, TOK], F32R)
        xT_l = new("xT_l", [P, KC, TOK], F32R)
        h = new("h", [P, NT, D])
        cst_at = top[0]
        cst = new("cst", [P, NCONST])
        col = new("col", [P, NCOLS])
        row = new("row", [P, NROWS])
        stat = new("stat", [P, NT, 4])
        soft = new("soft", [P, 2, 5, 4])
        gn_stat = new("gn_stat", [P, 2, NT, 6])
        gn_mv = new("gn_mv", [P, 2, NT, 2])
        gn_mid = new("gn_mid", [P, 2, NT])
        gn_r = new("gn_r", [P, 2, NT])
        metaT_hl = new("metaT_hl", [P, KC, 3 * N_META], F32R)
        metaT = new("metaT", [P, KC, N_META])
        mstat = new("mstat", [N_META, 4])
        usoft = new("usoft", [P, 4, 6, 2])
        halfb = new("halfb", [P, 2 * KC])
        lam = new("lam", [P, 4])
        neglam = new("neglam", [P, 1])
        subgain = new("subgain", [P, 1])
        ostat = new("ostat", [P, 3, 3])
        negsink = new("negsink", [P, 2 * A_HEADS + S_HEADS])
        region = top[0]

        def c(name):
            a, n = CONST[name]
            return cst[:, a:a + n]

        def cl(name, i=0, n=1):
            a = COLS[name][0] + i
            return col[:, a:a + n]

        xn = at("xn", [P, NT, D], F32, region)

        tok = [new("tok0", [P, NT, 512]), new("tok1", [P, NT, 512])]
        ka_tok = new("ka_tok", [P, NT, P])
        qaT = new("qaT", [P, 4, TOK])
        kaT = new("kaT", [P, 2, TOK])
        va = new("va", [P, NT, 2, P])
        qrT = new("qrT", [P, R_HEADS, TOK])
        krT = new("krT", [P, R_HEADS, TOK])
        vr_at = top[0]
        vr = new("vr", [P, R_HEADS, NT, R_VAL])
        gr_at = top[0]
        gr = new("gr", [P, R_HEADS, NT, R_VAL])
        gate_a = new("gate_a", [P, KC, TOK])
        gate_r = at("gate_r", [P, KC, TOK], F32, region)
        retT_h = at("retT_h", [P, KC, TOK], F32R, vr_at)
        retT_l = at("retT_l", [P, KC, TOK], F32R, gr_at)
        aT_h = new("aT_h", [P, 4, TOK], F32R)
        aT_l = new("aT_l", [P, 4, TOK], F32R)
        s1 = [new("s1a", [P, 2, TOK]), new("s1b", [P, 2, TOK])]
        s0 = [new("s0a", [P, 2, P]), new("s0b", [P, 2, P])]
        pT = new("pT", [P, 6, P])
        decayed_at = top[0]
        decayed = new("decayed", [P, 3 * P])
        scratch = new("scratch", [P, 512])
        end1 = top[0]

        top[0] = region + NT * D
        f_sq = [new("f_sq0", [P, 2, TOK]), new("f_sq1", [P, 2, TOK])]
        fT_h = [new("fT_h0", [P, 2, TOK], F32R), new("fT_h1", [P, 2, TOK], F32R)]
        fT_l = [new("fT_l0", [P, 2, TOK], F32R), new("fT_l1", [P, 2, TOK], F32R)]

        gain_row = new("gain_row", [P, D])
        meta_tok = new("meta_tok", [N_META, D])

        dead = cst_at + CONST["gt"][0]
        gate_s = at("gate_s", [P, KC, TOK], F32, dead)
        top[0] = 0
        kbT = new("kbT", [P, 2 * F_HEADS, KEYS])
        ksT = new("ksT", [P, S_KV, KEYS])
        vs_meta = new("vs_meta", [N_META, S_KV * DH])
        o_junk = new("o_junk", [P, P])
        assert top[0] <= 3 * BLOB
        top[0] = region
        gate_d = at("gate_d", [P, KC, TOK], F32, region)
        tok2 = [new("tok2a", [P, NT, 512]), new("tok2b", [P, NT, 512])]
        dT_l = at("dT_l", [P, KC, TOK], F32R, top[0])
        ks_tok = new("ks_tok", [P, NT, 256])
        mk = [new("mk0", [N_META, 512]), new("mk1", [N_META, 512])]
        vs = new("vs", [P, NT, S_KV * DH])
        vb = new("vb", [P, NT, D])
        vb_meta = new("vb_meta", [N_META, D])
        dT_h = at("dT_h", [P, KC, TOK], F32R, top[0])
        qsT = new("qsT", [P, KC, TOK])
        gain_rows = at("gain_rows2", [P, 2, D], F32, top[0])
        qbT = new("qbT", [P, KC, TOK])
        ag = at("ag", [P, NT, D], F32, top[0])
        sT_h = new("sT_h", [P, KC, TOK], F32R)
        sT_l = new("sT_l", [P, KC, TOK], F32R)
        sc = [new("sc0", [P, 2, KEYS]), new("sc1", [P, 2, KEYS])]
        mlow = at("mlow", [N_META, 512], F32, top[0])
        puT = new("puT", [P, 4, P])
        pmT = new("pmT", [N_META, 2, P])
        scratch2 = new("scratch2", [P, 512])
        o_tok = [at("o_tok0", [P, P], F32, dead + KC * TOK), new("o_tok1", [P, P]), new("o_tok2", [P, P])]

        top[0] = region + NT * D
        g_act = new("g_act", [P, 2, TOK])
        gT_h = new("gT_h", [P, 2, TOK], F32R)
        gT_l = new("gT_l", [P, 2, TOK], F32R)
        gL_h = new("gL_h", [P, 2, TOK], F32R)
        gL_l = new("gL_l", [P, 2, TOK], F32R)

        ps = ctx.enter_context(nc.psum_tensor("ps", [P, 8, BANK], F32))
        acc = [ps[:, 4:6, :].rearrange("p a b -> p (a b)"), ps[:, 6:8, :].rearrange("p a b -> p (a b)")]

        raw_in = [sem(f"raw_in{s}") for s in range(4)]
        split_hi = sem("split_hi")
        split_lo = sem("split_lo")
        blob_used = sem("blob_used")
        x_in = [sem("x_in0"), sem("x_in1")]
        early_in = sem("early_in")
        col_in = sem("col_in")
        const_in = sem("const_in")
        first_in = sem("first_in")
        first_hi = sem("first_hi")
        first_lo = sem("first_lo")
        row_in = sem("row_in")
        dve_step = sem("dve_step")
        act_step = sem("act_step")
        pool_step = sem("pool_step")
        init_ok = sem("init_ok")
        out_done = sem("out_done")
        sq_a = sem("sq_a")
        sq_d = sem("sq_d")
        rstd_ok = sem("rstd_ok")
        xn_a = sem("xn_a")
        xn_d = sem("xn_d")
        acc_ok = sem("acc_ok")
        acc_a = sem("acc_a")
        xt_ps = sem("xt_ps")
        xt_hi = sem("xt_hi")
        xt_lo = sem("xt_lo")
        h_ok = sem("h_ok")
        taken_a = sem("taken_a")
        taken_d = sem("taken_d")
        rope_ok = sem("rope_ok")
        q_ps = sem("q_ps")
        q_ok = sem("q_ok")
        sc_ps = sem("sc_ps")
        sc_ok = sem("sc_ok")
        ex_ok = sem("ex_ok")
        pr_ok = sem("pr_ok")
        pt_ps = sem("pt_ps")
        pt_a = sem("pt_a")
        pt_d = sem("pt_d")
        o_ps = sem("o_ps")
        o_hi = sem("o_hi")
        o_lo = sem("o_lo")
        at_ps = sem("at_ps")
        at_ok = sem("at_ok")
        ro_ps = sem("ro_ps")
        rv_ok = sem("rv_ok")
        rr_ok = sem("rr_ok")
        rn_ok = sem("rn_ok")
        rt_ps = sem("rt_ps")
        rt_hi = sem("rt_hi")
        rt_lo = sem("rt_lo")
        e_ok = sem("e_ok")
        mg_ok = sem("mg_ok")
        mg_hi = sem("mg_hi")
        mg_lo = sem("mg_lo")
        ff_relu = sem("ff_relu")
        ff_sq = sem("ff_sq")
        ff_hi = sem("ff_hi")
        ff_lo = sem("ff_lo")

        meta_in = sem("meta_in")
        meta_sq = sem("meta_sq")
        meta_r = sem("meta_r")
        meta_n = sem("meta_n")
        meta_ps = sem("meta_ps")
        meta_g = sem("meta_g")
        meta_hi = sem("meta_hi")
        meta_lo = sem("meta_lo")
        zero2 = sem("zero2")
        mlow_ok = sem("mlow_ok")
        mtaken_d = sem("mtaken_d")
        kt_ps = sem("kt_ps")
        kt_ok = sem("kt_ok")
        sv_ok = sem("sv_ok")
        lam_s = sem("lam_s")
        lam_ok = sem("lam_ok")
        lam_e = sem("lam_e")
        u_sc = sem("u_sc")
        u_max = sem("u_max")
        u_exp = sem("u_exp")
        u_pr = sem("u_pr")
        u_pt = sem("u_pt")
        u_ptd = sem("u_ptd")
        u_ptm = sem("u_ptm")
        u_o = sem("u_o")
        d_o = sem("d_o")
        d_n = sem("d_n")
        d_ps = sem("d_ps")
        d_hi = sem("d_hi")
        d_lo = sem("d_lo")
        rows_in = sem("rows_in")
        gs_ok = sem("gs_ok")
        g_one = sem("g_one")
        g_two = sem("g_two")
        g_hi = sem("g_hi")
        g_lo = sem("g_lo")

        steps = {"act": 0, "dve": 0, "pool": 0}
        chain = {"act": act_step, "dve": dve_step, "pool": pool_step}

        def link(eng, name, ins):
            steps[name] += 1
            ins.then_inc(chain[name], 1)
            eng.wait_ge(chain[name], steps[name])

        TAKERS = "aadd" + "aa" + "dd" + "aaaa" + "dd" + "dd" + "dddd" + "aa" + "ddd" + "aaaa" + "dd" + "dd"

        def wait_pair_free(pe, group):
            if group >= 2:
                who = TAKERS[group - 2]
                pe.wait_ge(taken_a if who == "a" else taken_d, 2 * TAKERS[:group - 1].count(who))

        XT_BANKS = 6

        def xt(t, k):
            per = 4 - 2 * t
            return ps[:, 2 * t + k // per, k % per * P:(k % per + 1) * P]

        def xt_bank(r, t, k):
            return r * XT_BANKS + 2 * t + k // (4 - 2 * t) + 1

        def xt_read(r, t, k):
            per = 4 - 2 * t
            return (2 * r + t) * KC + k // per * per + per

        def product(pe, o, lh, ll, rh, rl, first, last):
            pe.matmul(o, lh, rh, start=first, stop=False)
            pe.matmul(o, lh, rl, start=False, stop=False)
            return pe.matmul(o, ll, rh, start=False, stop=last)

        def product_meta(pe, bank, k, rh, rl, first, last):
            if first:
                pe.matmul(ps[0:3 * N_META, bank, :], metaT_hl[:, k, :], rh, start=True, stop=False)
            m = pe.matmul(ps[0:N_META, bank, :], metaT_hl[:, k, 0:N_META], rl, start=False, stop=False)
            if not first:
                m = pe.matmul(ps[0:3 * N_META, bank, :], metaT_hl[:, k, :], rh, start=False, stop=last)
            return m

        def multiply_tokens(pe, slot, k0, nk, width, bank0, first, last, xh, xl, chunk_wait=None, part=None,
                            meta_bank=None):
            vh = whi[slot][:].rearrange("p (k c) -> p k c", k=nk)
            vl = wlo[slot][:].rearrange("p (k c) -> p k c", k=nk)
            halves = max(1, width // BANK)
            wd = min(width, BANK)
            for k in range(nk) if part is None else range(part * nk // 2, (part + 1) * nk // 2):
                if chunk_wait is not None:
                    pe.wait_ge(xt_lo, chunk_wait + k0 + k + 1)
                for t in range(NT):
                    for half in range(halves):
                        m = product(pe, ps[:, bank0 + t * halves + half, 0:wd],
                                    xh[:, k0 + k, t * P:(t + 1) * P], xl[:, k0 + k, t * P:(t + 1) * P],
                                    vh[:, k, half * BANK:half * BANK + wd],
                                    vl[:, k, half * BANK:half * BANK + wd],
                                    first and k == 0, last and k == nk - 1)
            if meta_bank is not None:
                for k in range(nk) if part else []:
                    m = product_meta(pe, meta_bank, k0 + k, vh[:, k, :], vl[:, k, :], first and k == 0,
                                     last and k == nk - 1)
            if part != 0:
                m.then_inc(blob_used, 1)

        def multiply_last_two(pe, n, k0, x, made, counts, between=None):
            for t, halves in ((0, (0, 1)), (1, (0,)), (1, (1,))):
                for b in range(2):
                    if t == 0:
                        pe.wait_ge(split_lo, n + b + 1)
                        pe.wait_ge(made, counts[b])
                    slot = slot_of(n + b)
                    vh = whi[slot][:].rearrange("p (k c) -> p k c", k=2)
                    vl = wlo[slot][:].rearrange("p (k c) -> p k c", k=2)
                    xh, xl = x[b]
                    if between is not None and (halves, b) == ((1,), 1):
                        between()
                    for k in range(2):
                        for half in halves:
                            m = product(pe, ps[:, 4 + t * 2 + half, :], xh[:, k0[b] + k, t * P:(t + 1) * P],
                                        xl[:, k0[b] + k, t * P:(t + 1) * P], vh[:, k, half * BANK:(half + 1) * BANK],
                                        vl[:, k, half * BANK:(half + 1) * BANK], False, b == 1 and k == 1)
                    if halves == (1,):
                        m.then_inc(blob_used, 1)
                    elif b == 1:
                        m.then_inc(acc_ok, 1)

        def multiply_features(pe, slot, nk, ntile, bank0, xh, xl, chunk_wait=None, part=None):
            vh = whi[slot][:].rearrange("p (k c) -> p k c", k=nk)
            vl = wlo[slot][:].rearrange("p (k c) -> p k c", k=nk)
            for j in range(ntile) if part is None else range(part * ntile // 2, (part + 1) * ntile // 2):
                o = ps[:, bank0 + j // 2, (j % 2) * TOK:(j % 2 + 1) * TOK]
                for k in range(nk):
                    if chunk_wait is not None and j == 0:
                        pe.wait_ge(xt_lo, chunk_wait + k + 1)
                    m = product(pe, o, vh[:, k, j * P:(j + 1) * P], vl[:, k, j * P:(j + 1) * P],
                                xh[:, k, :], xl[:, k, :], k == 0, k == nk - 1)
            if part != 0:
                m.then_inc(blob_used, 1)

        block = ctx.enter_context(nc.Block())

        @block.sync
        def _(sp):
            def load(n, src, made):
                if made is not None:
                    sp.wait_ge(split_lo, made)
                sp.dma_start(raw[slot_of(n)][:], src).then_inc(raw_in[slot_of(n)], 16)

            sp.dma_start(cst[:, 0:EARLY], consts[:, 0:EARLY]).then_inc(early_in, 16)
            for t in range(NT):
                sp.dma_start(h[:, t, :], x[:, t, :]).then_inc(x_in[t], 16)
            sp.dma_start(col[:], cols).then_inc(col_in, 16)
            sp.dma_start(raw[0][:, 0:BLOB // 2], w[0][:, 0:BLOB // 2]).then_inc(first_in, 16)
            sp.dma_start(raw[0][:, BLOB // 2:BLOB], w[0][:, BLOB // 2:BLOB]).then_inc(raw_in[0], 16)
            for n in range(1, 3):
                load(n, w[n], None)
            sp.dma_start(cst[:, EARLY:NCONST], consts[:, EARLY:NCONST]).then_inc(const_in, 16)
            sp.dma_start(row[:], rows.partition_broadcast(P)).then_inc(const_in, 16)
            load(3, w[3], None)
            with sp.Fori(4, N1 - 4, 4) as i:
                for j in range(4):
                    load(j, w[bass.ds(i + j, 1)].rearrange("a p c -> (a p) c"), i + (j - 3))
            load(N1 - 1, w[N1 - 1], N1 - 1 - 3)
            whole = (NBLOB - N1) // 3 * 3
            with sp.Fori(N1, N1 + whole - 2, 3) as i:
                for j in range(3):
                    load(N1 + j, w[bass.ds(i + j, 1)].rearrange("a p c -> (a p) c"), i + (j - 2))
            for n in range(N1 + whole, NBLOB):
                load(n, w[n], n - 2)

        @block.scalar
        def _(act):
            def hi(n, i=0, per=0):
                s, depth = slot_of(n), depth_of(n)
                act.wait_ge(raw_in[s], i * (16 * per // depth) + 16 * fills(n))
                if n >= 4:
                    act.wait_ge(blob_used, i * per + used_before(n))
                act.activation(whi[s][:], raw[s][:], ACT.Copy).then_inc(split_hi, 1)

            norms = [0]

            def square(t):
                act.activation(xn[:, t, 0:BANK], h[:, t, 0:BANK], ACT.Square, scale=D ** -0.5,
                               accum_out=stat[:, t, 0:1]).then_inc(sq_a, 1)
                norms[0] += 1

            def normalise(t, since=0):
                act.wait_ge(rstd_ok, norms[0] - since)
                act.activation(xn[:, t, 0:BANK], h[:, t, 0:BANK], ACT.Copy, scale=stat[:, t, 3:4]).then_inc(xn_a, 1)

            def to_features(r, gain, t):
                for k in range(KC):
                    act.wait_ge(xt_ps, xt_bank(r, t, k))
                    act.activation(xT_h[:, k, t * P:(t + 1) * P], xt(t, k), ACT.Copy,
                                   scale=cl(gain, k)).then_inc(xt_hi, 1)

            def exp_pairs(j):
                act.wait_ge(sc_ok, j + 1)
                st = soft[:, j % 2]
                for u in range(2):
                    act.activation(s1[j % 2][:, u, :], s1[j % 2][:, u, :], ACT.Exp, bias=st[:, 1, u:u + 1],
                                   accum_out=st[:, 3, u:u + 1])
                for u in range(2):
                    act.activation(s0[j % 2][:, u, :], s0[j % 2][:, u, :], ACT.Exp, bias=st[:, 1, 2 + u:3 + u],
                                   accum_out=st[:, 3, 2 + u:3 + u])
                act.activation(st[:, 2, :], st[:, 2, :], ACT.Exp).then_inc(ex_ok, 1)

            def gate(bank, dst, func, scale, bias):
                for b in range(2):
                    for j in range(2):
                        m = act.activation(dst[:, 2 * b + j, :], ps[:, bank + b, j * TOK:(j + 1) * TOK],
                                           func, scale=scale, bias=bias(2 * b + j))
                    m.then_inc(taken_a, 1)

            def merged_hi(count, merged=gate_a, scale=1.0):
                act.wait_ge(mg_ok, count + 1)
                i = count % 4
                act.activation(xT_h[:, 2 * i:2 * i + 2, :], merged[:, 2 * i:2 * i + 2, :],
                               ACT.Copy, scale=scale).then_inc(mg_hi, 1)

            for t in range(NT):
                act.wait_ge(x_in[t], 16)
                square(t)
                normalise(t)
            act.wait_ge(col_in, 16)
            act.wait_ge(first_in, 16)
            act.activation(whi[0][:, 0:BLOB // 2], raw[0][:, 0:BLOB // 2], ACT.Copy).then_inc(first_hi, 1)
            for t in range(NT):
                to_features(0, "norm_mix", t)
            act.wait_ge(raw_in[0], 16)
            act.activation(whi[0][:, BLOB // 2:BLOB], raw[0][:, BLOB // 2:BLOB], ACT.Copy).then_inc(split_hi, 1)
            for n in range(1, 3):
                hi(n)

            for n in range(MIX1):
                if n == 2:
                    act.wait_ge(blob_used, 2)
                    for t in range(NT):
                        act.activation(tok[0][:, t, :], ps[:, t, :], ACT.Copy).then_inc(taken_a, 1)
                if n == 3:
                    act.wait_ge(blob_used, 3)
                    act.wait_ge(init_ok, 2)
                    for t in range(NT):
                        act.activation(ka_tok[:, t, :], ps[:, 2 + t, 0:P], ACT.Copy)
                        act.activation(va[:, t, 0, 0:A_DIM], ps[:, 2 + t, P:P + A_DIM], ACT.Copy)
                        act.activation(va[:, t, 1, A_DIM:P], ps[:, 2 + t, P + A_DIM:2 * P],
                                       ACT.Copy).then_inc(taken_a, 1)
                if n == 4:
                    act.wait_ge(q_ps, 1)
                    for t in range(NT):
                        m = act.activation(qaT[:, :, t * P:(t + 1) * P],
                                           ps[:, 4 + t, :].rearrange("p (j q) -> p j q", j=4), ACT.Copy)
                    m.then_inc(q_ok, 1)
                    act.wait_ge(q_ps, 2)
                    act.activation(kaT[0:A_DIM, 0, :], ps[0:A_DIM, 6, 0:TOK], ACT.Copy)
                    act.activation(kaT[A_DIM:P, 1, :], ps[A_DIM:P, 6, 0:TOK], ACT.Copy).then_inc(q_ok, 1)
                if n in (7, 9):
                    dst, bank = (qrT, 4) if n == 7 else (krT, 6)
                    act.wait_ge(q_ps, 3 if n == 7 else 4)
                    for t in range(NT):
                        m = act.activation(dst[:, :, t * P:(t + 1) * P],
                                           ps[:, bank + t, :].rearrange("p (j q) -> p j q", j=4), ACT.Copy)
                    m.then_inc(q_ok, 1)
                if 12 <= n < 16:
                    j = n - 12
                    act.wait_ge(pt_ps, j + 1)
                    act.activation(pT[:, 4:6, :], ps[:, 7, 0:TOK].rearrange("p (a q) -> p a q", a=2),
                                   ACT.Copy).then_inc(pt_a, 1)
                if 13 <= n < 17:
                    j = n - 13
                    act.wait_ge(o_ps, j + 1)
                    act.activation(aT_h[:, j, :], ps[:, 7, TOK:2 * TOK], ACT.Copy).then_inc(o_hi, 1)
                if 10 <= n < 14:
                    hi(n + 3)
                    exp_pairs(n - 10)
                if n in (9, 11):
                    act.wait_ge(blob_used, n)
                    hh = n - 9
                    for t in range(NT):
                        act.activation(vr[:, hh:hh + 2, t, :],
                                       ps[:, (n - 9) + t, :].rearrange("p (a v) -> p a v", a=2),
                                       ACT.Copy).then_inc(taken_a, 1)
                if n in (13, 15):
                    act.wait_ge(blob_used, n)
                    hh = n - 13
                    for t in range(NT):
                        act.activation(gr[:, hh:hh + 2, t, :],
                                       ps[:, (n - 13) + t, :].rearrange("p (a v) -> p a v", a=2),
                                       ACT.Sigmoid).then_inc(e_ok, 1)
                if n in (17, 19, 21, 23):
                    act.wait_ge(blob_used, n)
                    g = (n - 17) // 2
                    gate(2 * (g % 2), (gate_a if g < 2 else gate_r)[:, 4 * (g % 2):4 * (g % 2) + 4, :],
                         ACT.Sigmoid, 1.0, lambda j: cl("b_gates", 4 * g + j))
                if 18 <= n < 22:
                    r = n - 18
                    act.wait_ge(rt_ps, r + 1)
                    for j in range(2):
                        act.activation(retT_h[:, 2 * r + j, :], ps[:, 6, j * TOK:(j + 1) * TOK], ACT.Copy,
                                       scale=cl("ret_gn", 2 * r + j)).then_inc(rt_hi, 1)
                if 26 <= n < 30:
                    merged_hi(n - 26)
                if n < MIX1 - 1 and not 10 <= n < 14:
                    hi(n + 3)
            act.wait_ge(h_ok, 1)
            square(0)
            normalise(0)
            act.wait_ge(h_ok, 3)
            square(1)
            to_features(1, "norm_mlp", 0)
            normalise(1)
            to_features(1, "norm_mlp", 1)
            hi(MIX1 + 2)

            def hidden_relu(k, used, made=None):
                if made is not None:
                    act.wait_ge(ff_lo, made)
                act.wait_ge(blob_used, used)
                act.activation(f_sq[k][:], ps[:, k, :].rearrange("p (a q) -> p a q", a=2), ACT.Relu).then_inc(ff_relu, 1)

            def hidden_hi(k, count):
                act.wait_ge(ff_sq, count)
                act.activation(fT_h[k][:], f_sq[k][:], ACT.Copy).then_inc(ff_hi, 1)

            act.dma_start(gain_row[:], grow[0].partition_broadcast(P)).then_inc(row_in, 16)
            act.dma_start(meta_tok[:], meta).then_inc(meta_in, 16)
            b = MIX1
            hi(b + 3)
            hi(b + 4)
            hidden_relu(0, b + 1)
            hidden_relu(1, b + 2)
            hidden_hi(0, 1)
            act.wait_ge(meta_in, 16)
            act.activation(xn[0:N_META, 0, :], meta_tok[:], ACT.Square, accum_out=mstat[:, 0:1]).then_inc(meta_sq, 1)
            act.wait_ge(meta_r, 1)
            act.activation(meta_tok[:], meta_tok[:], ACT.Copy, scale=mstat[:, 2:3]).then_inc(meta_n, 1)
            with act.Fori(0, STEP1 - 1) as i:
                b = MIX1 + 2
                hi(b + 3, i, 4)
                hidden_hi(1, i * 2 + 2)
                hi(b + 4, i, 4)
                hidden_relu(0, i * 4 + (b + 1), i * 2 + 1)
                hi(b + 5, i, 4)
                hidden_relu(1, i * 4 + (b + 2), i * 2 + 2)
                hi(b + 6, i, 4)
                hidden_hi(0, i * 2 + 3)
            b = N1 - 2
            act.wait_ge(blob_used, N1 - 2)
            hidden_hi(1, 2 * STEP1)
            hi(b + 3)
            act.wait_ge(meta_g, 1)
            for i in range(2):
                m = act.activation(metaT_hl[:, :, i * N_META:(i + 1) * N_META], metaT[:], ACT.Copy)
            m.then_inc(meta_hi, 1)

            for t in range(NT):
                act.wait_ge(h_ok, 4 * t + 5)
                square(t)
                act.wait_ge(h_ok, 4 * t + 7)
                square(t)
                normalise(t)
            for t in range(NT):
                to_features(2, "pre_mix", t)
            hi(N1 + 2)

            def copy_halves(dst, variant, bank):
                act.activation(dst[0:DH, variant, :], ps[0:DH, bank, 0:KEYS], ACT.Copy)
                return act.activation(dst[DH:P, variant + 1, :], ps[DH:P, bank, 0:KEYS], ACT.Copy)

            for q in range(2 * OUT2):
                m = q // 2
                if q == 4:
                    act.wait_ge(blob_used, N1 + 2)
                    for t in range(NT):
                        ins = act.activation(vs[:, t, :], ps[:, t, 256:512], ACT.Copy)
                    ins.then_inc(sv_ok, 1)
                if q == 6:
                    act.wait_ge(zero2, 1)
                if q in (6, 11, 12, 15, 16):
                    r = (6, 11, 12, 15, 16).index(q)
                    act.wait_ge(kt_ps, r + 1)
                    for cc in range(2):
                        ins = copy_halves(*((ksT, 2 * cc) if r == 0 else (kbT, 4 * (r - 1) + 2 * cc)), 4 + cc)
                    ins.then_inc(kt_ok, 1)
                if q in (18, 30, 34, 38):
                    r = (18, 30, 34, 38).index(q)
                    g = (3, 6, 7, 8)[r]
                    act.wait_ge(q_ps, 5 + r)
                    for t in range(NT):
                        ins = act.activation(
                            (qsT if r < 2 else qbT)[:, 4 * (r % 2):4 * (r % 2) + 4, t * P:(t + 1) * P],
                            ps[:, 2 * (g % 2) + t, :].rearrange("p (j q) -> p j q", j=4), ACT.Copy)
                    ins.then_inc(q_ok, 1)
                if q in (20, 24):
                    half = (q - 20) // 4
                    act.wait_ge(blob_used, N1 + m)
                    for t in range(NT):
                        act.activation(vb[:, t, half * BANK:(half + 1) * BANK], ps[:, 2 * half + t, :],
                                       ACT.Copy).then_inc(taken_a, 1)
                if q in (4, 8, 12, 20, 24):
                    r = (4, 8, 12, 20, 24).index(q)
                    act.wait_ge(blob_used, N1 + m)
                    if r == 4:
                        act.wait_ge(mtaken_d, 4)
                    elif r:
                        act.wait_ge(rope_ok, 4 + r)
                    act.activation(mlow[:], ps[2 * N_META:3 * N_META, (6, 7, 6, 7, 6)[r], :],
                                   ACT.Copy).then_inc(mlow_ok, 1)
                U = q - U0 - 3
                if 0 <= U < UNITS:
                    act.wait_ge(u_pt, U + 1)
                    heads = 2 if U < S_UNITS else 1
                    act.activation(pmT[:, 0:heads, :], ps[0:N_META, 7, 32:32 + heads * P].rearrange(
                        "p (a q) -> p a q", a=heads), ACT.Copy).then_inc(u_ptm, 1)
                U = q - U0 - 4
                if 0 <= U < UNITS:
                    act.wait_ge(u_o, U + 1)
                    if U >= 3:
                        act.wait_ge(d_ps, U - 2)
                    if U < S_UNITS:
                        act.wait_ge(u_pr, U + 1)
                        for u in range(2):
                            ins = act.activation(o_tok[U % 3][:, u * DH:(u + 1) * DH],
                                                 ps[:, 7, 288 + u * DH:288 + (u + 1) * DH], ACT.Copy,
                                                 scale=usoft[:, U % 4, 5, u:u + 1])
                    else:
                        act.activation(o_junk[:], ps[:, 7, 288:288 + P], ACT.Square,
                                       accum_out=ostat[:, U % 3, 0:1])
                        ins = act.activation(o_tok[U % 3][:], ps[:, 7, 288:288 + P], ACT.Copy)
                    ins.then_inc(d_o, 1)
                U = q - U0 - 7
                if 0 <= U < UNITS:
                    act.wait_ge(d_ps, U + 1)
                    act.wait_ge(u_sc, min(UNITS, q - U0))
                    act.activation((sT_h if U < S_UNITS else dT_h)[:, U % S_UNITS // 2, U % 2 * P:(U % 2 + 1) * P],
                                   ps[:, 5, P:2 * P], ACT.Copy,
                                   scale=1.0 if U < S_UNITS else subgain[:]).then_inc(d_hi, 1)
                if q == 2:
                    act.wait_ge(lam_s, 1)
                    act.activation(lam[:, 2:4], lam[:, 0:2], ACT.Exp).then_inc(lam_e, 1)
                U = q - U0 - 1
                if 0 <= U < UNITS:
                    act.wait_ge(u_max, U + 1)
                    st = usoft[:, U % 4]
                    for u in range(2):
                        ins = act.activation(sc[U % 2][:, u, :], sc[U % 2][:, u, :], ACT.Exp,
                                             bias=st[:, 2, u:u + 1], accum_out=st[:, 4, u:u + 1])
                    if U < S_UNITS:
                        ins = act.activation(st[:, 3, :], st[:, 3, :], ACT.Exp)
                    ins.then_inc(u_exp, 1)
                if q in (41, 45, 49, 53):
                    g = (q - 41) // 4
                    act.wait_ge(blob_used, N1 + m)
                    gate(2 * ((g + 1) % 2), (gate_s if g < 2 else gate_d)[:, 4 * (g % 2):4 * (g % 2) + 4, :],
                         ACT.Tanh, 0.5, lambda j: halfb[:, 4 * g + j:4 * g + j + 1])
                if q == 2 * OUT2 - 8:
                    act.wait_ge(u_sc, UNITS)
                    act.dma_start(gain_rows[:], grow[1:3].partition_broadcast(P)).then_inc(rows_in, 16)
                if q % 2 == 0 and m:
                    hi(N1 + m + 2)
                if q % 2 == 0 and m > OUT2 - 4:
                    merged_hi(4 + m - (OUT2 - 3), gate_s, 0.5)
            for m in range(OUT2, MIX2 - 1):
                if m == OUT2:
                    merged_hi(7, gate_s, 0.5)
                hi(N1 + m + 2)

            def square_acc(t, product, last_blob):
                for half in range(2):
                    if (t, half) == (1, 1):
                        act.wait_ge(blob_used, last_blob)
                    else:
                        act.wait_ge(acc_ok, 2 * product - 1 + t)
                    a = half * BANK
                    act.activation(xn[:, t, a:a + BANK], acc[t][:, a:a + BANK], ACT.Square, scale=D ** -0.5,
                                   accum_out=stat[:, t, half:half + 1]).then_inc(acc_a, 1)
                norms[0] += 1

            square_acc(0, 3, F2)
            act.wait_ge(h_ok, 13)
            square(0)
            square_acc(1, 3, F2)
            normalise(0, 1)
            act.wait_ge(h_ok, 15)
            square(1)
            to_features(3, "pre_ffn", 0)
            normalise(1)
            to_features(3, "pre_ffn", 1)
            hi(F2 + 1)
            hi(F2 + 2)

            def silu_one(j, used, i=0):
                act.wait_ge(blob_used, used)
                act.activation(g_act[:], ps[:, 0, :].rearrange("p (a q) -> p a q", a=2),
                               ACT.Sigmoid).then_inc(gs_ok, 1)

            def hidden2_hi(made, dst=gT_h):
                act.wait_ge(g_two, made)
                act.activation(dst[:], g_act[:], ACT.Copy).then_inc(g_hi, 1)

            hi(F2 + 3)
            silu_one(0, F2 + 1)
            hi(F2 + 4)
            hidden2_hi(1)
            with act.Fori(0, STEP2 - 2) as i:
                hi(F2 + 5, i, 3)
                act.wait_ge(g_lo, i + 1)
                silu_one(0, i * 3 + (F2 + 3))
                hi(F2 + 6, i, 3)
                hi(F2 + 7, i, 3)
                hidden2_hi(i + 2)
            hi(NBLOB - 1)
            act.wait_ge(g_lo, STEP2 - 1)
            silu_one(0, F2 + 3 * STEP2 - 3)
            hidden2_hi(STEP2, gL_h)

            for t in range(NT):
                square_acc(t, 4, NBLOB)
            for t in range(NT):
                for half in range(2):
                    a = half * BANK
                    act.wait_ge(h_ok, 17 + 2 * t + half)
                    act.dma_start(out[:, t, a:a + BANK], h[:, t, a:a + BANK]).then_inc(out_done, 16)
            act.wait_ge(out_done, 64)

        @block.gpsimd
        def _(pool):
            def rsqrt(dst, mid, src, scale, rows=P):
                link(pool, "pool", pool.tensor_scalar(mid, src, scale, EPS, ALU.mult, ALU.add))
                return pool.tensor_tensor(dst, mid, c("neghalf")[0:rows, 0:dst.shape[-1]], ALU.pow)

            shares = [0, 0]

            def rms(t, product=False):
                if product:
                    shares[1] += 1
                    pool.wait_ge(acc_a, 2 * shares[1])
                else:
                    shares[0] += 1
                    pool.wait_ge(sq_a, shares[0])
                    pool.wait_ge(sq_d, shares[0])
                st = stat[:, t]
                link(pool, "pool", pool.tensor_scalar(st[:, 2:3], st[:, 0:1], st[:, 1:2], EPS, ALU.add, ALU.add))
                pool.tensor_tensor(st[:, 3:4], st[:, 2:3], c("neghalf")[:, 0:1], ALU.pow).then_inc(rstd_ok, 1)

            pool.wait_ge(early_in, 16)
            rms(0)
            rms(1)
            pool.wait_ge(const_in, 32)
            for r in range(R_HEADS):
                pool.wait_ge(rv_ok, r + 1)
                rsqrt(gn_r[:, r % 2, :], gn_mid[:, r % 2, :], gn_mv[:, r % 2, :, 1], 1.0).then_inc(rr_ok, 1)
            rms(0)
            rms(1)
            pool.wait_ge(meta_sq, 1)
            rsqrt(mstat[:, 2:3], mstat[:, 1:2], mstat[:, 0:1], 1.0 / D, N_META).then_inc(meta_r, 1)
            for t in range(NT):
                rms(t)
                rms(t)

            pool.wait_ge(blob_used, N1)
            pool.wait_ge(h_ok, 12)
            pool.memset(ksT[:], 0.0)
            pool.memset(kbT[:], 0.0).then_inc(zero2, 1)

            for U in range(S_UNITS, UNITS):
                pool.wait_ge(d_o, U + 1)
                st = ostat[:, U % 3]
                link(pool, "pool", rsqrt(st[:, 2:3], st[:, 1:2], st[:, 0:1], 1.0 / P))
                pool.tensor_scalar(o_tok[U % 3][:], o_tok[U % 3][:], st[:, 2:3], None, ALU.mult).then_inc(d_n, 1)
            for t in range(NT):
                rms(t, True)
                rms(t)
            for t in range(NT):
                rms(t, True)

        @block.tensor
        def _(pe):
            ident = c("ident")

            def features(r, t):
                pe.wait_ge(xn_a, 2 * r + t + 1)
                for k in range(KC):
                    if k == 4:
                        pe.wait_ge(xn_d, 2 * r + t + 1)
                    m = pe.transpose(xt(t, k), xn[:, t, k * P:(k + 1) * P], ident)
                    if k % (4 - 2 * t) == 3 - 2 * t:
                        m.then_inc(xt_ps, 1)

            def keep_warm(times, bank, x=None, columns=BANK):
                for _ in range(times):
                    pe.matmul(ps[:, bank, 0:columns], ident if x is None else x[:, 0:P],
                              cst[:, 0:columns] if x is None else x[:, 0:columns], start=True, stop=True)

            def transpose4(bank, src, signal):
                for t in range(NT):
                    for j in range(4):
                        m = pe.transpose(ps[:, bank + t, j * P:(j + 1) * P], src(t, j), ident)
                m.then_inc(signal, 1)

            pe.wait_ge(init_ok, 1)
            keep_warm(3, 7, kaT[:].rearrange("p a k -> p (a k)"))
            pe.wait_ge(early_in, 16)
            for t in range(NT):
                features(0, t)
            for n in range(MIX1):
                if n == 0:
                    pe.wait_ge(first_lo, 1)
                    multiply_tokens(pe, 0, 0, 4, BANK, 0, True, False, xT_h, xT_l, KC, 0)
                    pe.wait_ge(split_lo, 1)
                    multiply_tokens(pe, 0, 0, 4, BANK, 0, True, False, xT_h, xT_l, KC, 1)
                    continue
                if n < MIX1 - 2:
                    pe.wait_ge(split_lo, n + 1)
                if n < 2:
                    multiply_tokens(pe, n % 4, 4 * n, 4, BANK, 0, n == 0, n == 1, xT_h, xT_l, KC)
                elif n == 2:
                    multiply_tokens(pe, n % 4, 0, KC, TOK, 2, True, True, xT_h, xT_l)
                elif n < 15:
                    g = 2 + (n - 3) // 2
                    first = n % 2 == 1
                    if first:
                        wait_pair_free(pe, g)
                    multiply_tokens(pe, n % 4, 0 if first else 4, 4, BANK, 2 * (g % 2), first, not first, xT_h, xT_l)
                elif n < 23:
                    g = 8 + (n - 15) // 2
                    if n % 2 == 1:
                        wait_pair_free(pe, g)
                    multiply_features(pe, n % 4, KC, 2, 2 * (g % 2) + (n - 15) % 2, xT_h, xT_l)
                elif n < 25:
                    g = 12 + n - 23
                    wait_pair_free(pe, g)
                    pe.wait_ge(o_lo, 4)
                    multiply_features(pe, n % 4, 4, 4, 2 * (g % 2), aT_h, aT_l)
                elif n < 29:
                    g = 14 + (n - 25) // 2
                    if n % 2 == 1:
                        wait_pair_free(pe, g)
                    pe.wait_ge(rt_lo, KC)
                    multiply_features(pe, n % 4, KC, 2, 2 * (g % 2) + (n - 25) % 2, retT_h, retT_l)
                elif n < MIX1 - 2:
                    pe.wait_ge(mg_lo, n - 29 + 1)
                    multiply_tokens(pe, n % 4, 2 * (n - 29), 2, D, 4, n == 29, False, xT_h, xT_l)

                if n == 3:
                    pe.wait_ge(rope_ok, 1)
                    transpose4(4, lambda t, j: tok[0][:, t, j * P:(j + 1) * P], q_ps)
                    pe.wait_ge(rope_ok, 2)
                    for t in range(NT):
                        m = pe.transpose(ps[:, 6, t * P:(t + 1) * P], ka_tok[:, t, :], ident)
                    m.then_inc(q_ps, 1)
                if n == 6:
                    pe.wait_ge(rope_ok, 3)
                    pe.wait_ge(q_ok, 1)
                    transpose4(4, lambda t, j: tok[1][:, t, j * P:(j + 1) * P], q_ps)
                if n == 8:
                    pe.wait_ge(rope_ok, 4)
                    pe.wait_ge(q_ok, 2)
                    transpose4(6, lambda t, j: tok[0][:, t, j * P:(j + 1) * P], q_ps)
                if 12 <= n < 16:
                    j = n - 12
                    pe.wait_ge(pt_a, j + 1)
                    pe.wait_ge(pt_d, j + 1)
                    if j >= 1:
                        pe.wait_ge(o_lo, j)
                    for u in range(2):
                        pe.matmul(ps[:, 7, TOK:TOK + P], va[:, 0, u, :], pT[:, 4 + u, :], start=u == 0, stop=u == 1)
                    for u in range(2):
                        for kt in range(NT):
                            m = pe.matmul(ps[:, 7, TOK + P:2 * TOK], va[:, kt, u, :], pT[:, 2 * u + kt, :],
                                          start=u + kt == 0, stop=u + kt == 2)
                    m.then_inc(o_ps, 1)
                if 11 <= n < 15:
                    j = n - 11
                    pe.wait_ge(pr_ok, j + 1)
                    if j == 0:
                        pe.wait_ge(q_ok, 4)
                    else:
                        pe.wait_ge(pt_d, j)
                        pe.wait_ge(pt_a, j)
                    if j >= 2:
                        pe.wait_ge(o_lo, j - 1)
                    for u in range(2):
                        for kt in range(NT):
                            pe.transpose(ps[:, 6, (2 * u + kt) * P:(2 * u + kt + 1) * P],
                                         s1[j % 2][:, u, kt * P:(kt + 1) * P], ident)
                    for u in range(2):
                        m = pe.transpose(ps[:, 7, u * P:(u + 1) * P], s0[j % 2][:, u, :], ident)
                    m.then_inc(pt_ps, 1)
                if 9 <= n < 13:
                    j = n - 9
                    if j == 0:
                        pe.wait_ge(q_ok, 3)
                    else:
                        pe.wait_ge(sc_ok, j)
                    for u in range(2):
                        pe.matmul(ps[:, 4, u * TOK:(u + 1) * TOK], qaT[:, j, P:TOK], kaT[:, u, :], start=True, stop=True)
                        m = pe.matmul(ps[:, 5, u * P:(u + 1) * P], qaT[:, j, 0:P], kaT[:, u, 0:P], start=True, stop=True)
                    m.then_inc(sc_ps, 1)
                if 17 <= n < 21:
                    r = n - 17
                    pe.wait_ge(rn_ok, r + 1)
                    if r == 0:
                        pe.wait_ge(pt_d, 4)
                    else:
                        pe.wait_ge(rt_lo, 2 * r)
                    for j in range(2):
                        for t in range(NT):
                            m = pe.transpose(ps[:, 6, j * TOK + t * P:j * TOK + (t + 1) * P],
                                             gr[:, r, t, j * P:(j + 1) * P], ident)
                    m.then_inc(rt_ps, 1)
                if 15 <= n < 19:
                    r = n - 15
                    pe.wait_ge(at_ok, r + 1)
                    if r == 0:
                        pe.wait_ge(taken_a, 8)
                    else:
                        pe.wait_ge(rn_ok, r)
                    pe.matmul(ps[:, 5, 0:TOK], decayed[:, 0:P], vr[:, r, 0, :], start=True, stop=True)
                    pe.matmul(ps[:, 5, TOK:2 * TOK], decayed[:, P:2 * P], vr[:, r, 0, :], start=True, stop=False)
                    pe.matmul(ps[:, 5, TOK:2 * TOK], decayed[:, 2 * P:3 * P], vr[:, r, 1, :],
                              start=False, stop=True).then_inc(ro_ps, 1)
                if 14 <= n < 18:
                    r = n - 14
                    if r == 0:
                        pe.wait_ge(sc_ok, 4)
                    else:
                        pe.wait_ge(at_ok, r)
                    pe.matmul(ps[:, 4, 0:TOK], krT[:, r, 0:P], qrT[:, r, :], start=True, stop=True)
                    pe.matmul(ps[:, 4, TOK:TOK + P], krT[:, r, P:TOK], qrT[:, r, P:TOK],
                              start=True, stop=True).then_inc(at_ps, 1)

            multiply_last_two(pe, MIX1 - 2, (4, 6), [(xT_h, xT_l)] * 2, mg_lo, (3, 4),
                              lambda: features(1, 0))
            keep_warm(3, 4)
            features(1, 1)

            def hidden(n, k, i=0, last_read=None, chunk_wait=None, per=4):
                pe.wait_ge(split_lo, i * per + n + 1)
                if last_read is not None:
                    pe.wait_ge(ff_relu, last_read)
                multiply_features(pe, slot_of(n), KC, 2, k, xT_h, xT_l, chunk_wait)

            def down(n, k, made, i=0, first=False, last=False, per=4):
                pe.wait_ge(split_lo, i * per + n + 1)
                pe.wait_ge(ff_lo, made)
                multiply_tokens(pe, slot_of(n), 0, 2, D, 4, first, last, fT_h[k], fT_l[k])

            hidden(MIX1, 0, chunk_wait=3 * KC)
            hidden(MIX1 + 1, 1)
            b = MIX1 + 2
            hidden(b, 0, last_read=1)
            hidden(b + 1, 1, last_read=2)
            down(b + 2, 0, 1, first=True)
            pe.wait_ge(meta_n, 1)
            for k in range(KC):
                m = pe.transpose(ps[:, 2, k * N_META:(k + 1) * N_META], meta_tok[:, k * P:(k + 1) * P],
                                 ident[0:N_META, 0:N_META])
            m.then_inc(meta_ps, 1)
            down(b + 3, 1, 2)
            with pe.Fori(1, STEP1 - 1) as i:
                hidden(b, 0, i, i * 2 + 1)
                hidden(b + 1, 1, i, i * 2 + 2)
                down(b + 2, 0, i * 2 + 1, i)
                down(b + 3, 1, i * 2 + 2, i)
            multiply_last_two(pe, N1 - 2, (0, 0), list(zip(fT_h, fT_l)), ff_lo, (2 * STEP1 - 1, 2 * STEP1))

            def first_group(t):
                for b in range(2):
                    n = N1 + b
                    vh = whi[slot_of(n)][:].rearrange("p (k c) -> p k c", k=4)
                    vl = wlo[slot_of(n)][:].rearrange("p (k c) -> p k c", k=4)
                    for k in range(4):
                        kk = 4 * b + k
                        if t is None:
                            m = product_meta(pe, 6, kk, vh[:, k, :], vl[:, k, :], kk == 0, kk == KC - 1)
                        else:
                            pe.wait_ge(xt_lo, (4 + t) * KC + max(4, kk + 1) if t == 0 else 5 * KC + kk + 1)
                            m = product(pe, ps[:, t, :], xT_h[:, kk, t * P:(t + 1) * P],
                                        xT_l[:, kk, t * P:(t + 1) * P], vh[:, k, :], vl[:, k, :], kk == 0, kk == KC - 1)
                    if t == 1:
                        m.then_inc(blob_used, 1)

            pe.wait_ge(split_lo, N1 + 2)
            pe.wait_ge(meta_lo, 1)
            pe.wait_ge(h_ok, 10)
            features(2, 0)
            first_group(None)
            features(2, 1)
            for t in range(NT):
                first_group(t)

            def slot(q):
                if q in (5, 10, 11, 14, 15):
                    r = (5, 10, 11, 14, 15).index(q)
                    pe.wait_ge(rope_ok, (5, 6, 6, 7, 7)[r])
                    if r:
                        pe.wait_ge(kt_ok, r)
                    for cc in range(2):
                        if r == 0:
                            src, mt, a = ks_tok, mk[0], cc * P
                        else:
                            src, mt, a = tok2[(r - 1) // 2], mk[(1, 0)[(r - 1) // 2]], ((r - 1) % 2 * 2 + cc) * P
                        for t in range(NT):
                            pe.transpose(ps[:, 4 + cc, t * P:(t + 1) * P], src[:, t, a:a + P], ident)
                        m = pe.transpose(ps[:, 4 + cc, TOK:KEYS], mt[:, a:a + P], ident[0:N_META, 0:N_META])
                    m.then_inc(kt_ps, 1)
                if q in (17, 29, 33, 37):
                    r = (17, 29, 33, 37).index(q)
                    g, buf = (3, 6, 7, 8)[r], tok2[r % 2]
                    pe.wait_ge(rope_ok, 8 + r)
                    transpose4(2 * (g % 2), lambda t, j: buf[:, t, j * P:(j + 1) * P], q_ps)
                U = q - U0 - 3
                if 0 <= U < UNITS:
                    pe.wait_ge(u_ptd, U + 1)
                    pe.wait_ge(u_ptm, U + 1)
                    if U:
                        pe.wait_ge(d_o, U)
                    cc, o = U % S_UNITS // 2, ps[:, 7, 288:288 + P]
                    if U < S_UNITS:
                        for u in range(2):
                            a = (2 * (cc // 4) + u) * DH
                            for kt in range(NT):
                                pe.matmul(o[:, u * DH:(u + 1) * DH], puT[:, 2 * u + kt, :], vs[:, kt, a:a + DH],
                                          start=kt == 0, stop=False)
                            m = pe.matmul(o[:, u * DH:(u + 1) * DH], pmT[:, u, :], vs_meta[:, a:a + DH],
                                          start=False, stop=True)
                    else:
                        for kt in range(NT):
                            pe.matmul(o, puT[:, kt, :], vb[:, kt, cc * P:(cc + 1) * P], start=kt == 0, stop=False)
                        m = pe.matmul(o, pmT[:, 0, :], vb_meta[:, cc * P:(cc + 1) * P], start=False, stop=True)
                    m.then_inc(u_o, 1)
                U = q - U0 - 2
                if 0 <= U < UNITS:
                    pe.wait_ge(u_exp if U < S_UNITS else u_pr, U + 1)
                    if U == 0:
                        pe.wait_ge(mtaken_d, 5)
                    else:
                        pe.wait_ge(u_ptd, U)
                        pe.wait_ge(u_ptm, U)
                    heads = 2 if U < S_UNITS else 1
                    for u in range(heads):
                        for kt in range(NT):
                            pe.transpose(ps[:, 6, (2 * u + kt) * P:(2 * u + kt + 1) * P],
                                         sc[U % 2][:, u, kt * P:(kt + 1) * P], ident)
                    for u in range(heads):
                        m = pe.transpose(ps[0:N_META, 7, 32 + u * P:32 + (u + 1) * P], sc[U % 2][:, u, TOK:KEYS],
                                         ident)
                    m.then_inc(u_pt, 1)
                U = q - U0 - 6
                if 0 <= U < UNITS:
                    if U < S_UNITS:
                        pe.wait_ge(d_o, U + 1)
                    else:
                        pe.wait_ge(d_n, U - S_UNITS + 1)
                    pe.wait_ge(u_max, min(UNITS, q - U0))
                    if U:
                        pe.wait_ge(d_lo, U)
                    pe.transpose(ps[:, 5, P:2 * P], o_tok[U % 3][:], ident).then_inc(d_ps, 1)
                U = q - U0
                if 0 <= U < UNITS:
                    cc, t = U % S_UNITS // 2, U % 2
                    pe.wait_ge(q_ok, 5 + U // 8)
                    if U == 0:
                        pe.wait_ge(kt_ok, 5)
                    else:
                        pe.wait_ge(u_max, U)
                    if U > 6:
                        pe.wait_ge(d_lo, U - 6)
                    qT = qsT if U < S_UNITS else qbT
                    for u in range(2):
                        kT = ksT[:, 2 * (cc // 4) + u, :] if U < S_UNITS else kbT[:, 2 * cc + u, :]
                        pe.matmul(ps[:, 4, u * TOK:(u + 1) * TOK], qT[:, cc, t * P:(t + 1) * P], kT[:, 0:TOK],
                                  start=True, stop=True)
                        m = pe.matmul(ps[:, 5, u * N_META:(u + 1) * N_META], qT[:, cc, t * P:(t + 1) * P],
                                      kT[:, TOK:KEYS], start=True, stop=True)
                    m.then_inc(u_sc, 1)

            for m2 in range(OUT2):
                n = N1 + m2
                pe.wait_ge(split_lo, n + 1)
                for part in range(2):
                    if m2 < 2:
                        pass
                    elif m2 < 18:
                        g, first = m2 // 2, m2 % 2 == 0
                        meta_bank = {1: 7, 2: 6, 4: 7, 5: 6}.get(g)
                        if first and part == 0:
                            if g >= 2:
                                wait_pair_free(pe, 16 + g)
                            if g - 2 in (3, 6, 7, 8):
                                pe.wait_ge(q_ok, 5 + (3, 6, 7, 8).index(g - 2))
                        if first and part == 1 and g in (2, 4, 5):
                            pe.wait_ge(mtaken_d, {2: 1, 4: 2, 5: 3}[g])
                        multiply_tokens(pe, slot_of(n), 0 if first else 4, 4, BANK, 2 * (g % 2), first, not first,
                                        xT_h, xT_l, None, part, meta_bank)
                    else:
                        g = 9 + (m2 - 18) // 2
                        if m2 % 2 == 0 and part == 0:
                            wait_pair_free(pe, 16 + g)
                            if g - 2 in (7, 8):
                                pe.wait_ge(q_ok, g - 2)
                            if m2 == 26:
                                pe.wait_ge(d_lo, S_UNITS)
                            if m2 == 30:
                                pe.wait_ge(d_lo, UNITS)
                        xh, xl = (xT_h, xT_l) if m2 < 26 else (sT_h, sT_l) if m2 < 30 else (dT_h, dT_l)
                        multiply_features(pe, slot_of(n), KC, 2, 2 * (g % 2) + m2 % 2, xh, xl, None, part)
                    slot(2 * m2 + part)
            for i in range(2):
                n = N1 + OUT2 + i
                pe.wait_ge(split_lo, n + 1)
                pe.wait_ge(mg_lo, 4 + i + 1)
                multiply_tokens(pe, slot_of(n), 2 * i, 2, D, 4, i == 0, False, xT_h, xT_l)
            multiply_last_two(pe, F2 - 2, (4, 6), [(xT_h, xT_l)] * 2, mg_lo, (7, 8))

            features(3, 0)
            keep_warm(2, 5)
            features(3, 1)

            def hidden2(n, bank, signal, read, i=0, chunk_wait=None):
                pe.wait_ge(split_lo, i * 3 + n + 1)
                if signal is not None:
                    pe.wait_ge(signal, read)
                multiply_features(pe, slot_of(n), KC, 2, bank, xT_h, xT_l, chunk_wait)

            def down2(n, made, i=0, first=False, last=False):
                pe.wait_ge(split_lo, i * 3 + n + 1)
                pe.wait_ge(g_lo, made)
                multiply_tokens(pe, slot_of(n), 0, 2, D, 4, first, last, gT_h, gT_l)

            hidden2(F2, 0, None, 0, chunk_wait=7 * KC)
            hidden2(F2 + 1, 1, None, 0)
            hidden2(F2 + 2, 0, g_one, 1)
            hidden2(F2 + 3, 1, g_two, 1)
            down2(F2 + 4, 1, first=True)
            with pe.Fori(0, STEP2 - 3) as i:
                hidden2(F2 + 5, 0, g_one, i + 2, i)
                hidden2(F2 + 6, 1, g_two, i + 2, i)
                down2(F2 + 7, i + 2, i)
            hidden2(NBLOB - 4, 0, g_one, STEP2 - 1)
            hidden2(NBLOB - 3, 1, g_two, STEP2 - 1)
            multiply_last_two(pe, NBLOB - 2, (0, 0), [(gT_h, gT_l), (gL_h, gL_l)], g_lo, (STEP2 - 1, STEP2))

        @block.vector
        def _(dve):
            freed, mfreed, rotated = [0], [0], [0]

            def free(ins):
                freed[0] += 1
                ins.then_inc(taken_d, 1)
                dve.wait_ge(taken_d, freed[0])

            def lo(n, i=0, per=0):
                s = slot_of(n)
                dve.wait_ge(split_hi, i * per + n + 1)
                dve.tensor_tensor(wlo[s][:], raw[s][:], whi[s][:], ALU.subtract).then_inc(split_lo, 1)

            norms = [0]

            def square(t):
                dve.tensor_tensor_reduce(out=xn[:, t, BANK:D], in0=h[:, t, BANK:D], in1=h[:, t, BANK:D],
                                         scale=1.0 / D, scalar=0.0, op0=ALU.mult, op1=ALU.add,
                                         accum_out=stat[:, t, 1:2]).then_inc(sq_d, 1)
                norms[0] += 1

            def normalise(t):
                dve.wait_ge(rstd_ok, norms[0])
                dve.tensor_scalar(xn[:, t, BANK:D], h[:, t, BANK:D], stat[:, t, 3:4], None, ALU.mult).then_inc(xn_d, 1)

            def to_features(r, gain, t, chunks=range(KC)):
                for k in chunks:
                    dve.wait_ge(xt_hi, xt_read(r, t, k))
                    dve.scalar_tensor_tensor(out=xT_l[:, k, t * P:(t + 1) * P], in0=xt(t, k), scalar=cl(gain, k),
                                             in1=xT_h[:, k, t * P:(t + 1) * P], op0=ALU.mult,
                                             op1=ALU.subtract).then_inc(xt_lo, 1)

            added = [0]

            def add_product(t, product, last_blob, halves=(0, 1)):
                for half in halves:
                    if (t, half) == (1, 1):
                        dve.wait_ge(blob_used, last_blob)
                    else:
                        dve.wait_ge(acc_ok, 2 * product - 1 + t)
                    v = h[:, t, half * BANK:(half + 1) * BANK]
                    dve.tensor_tensor(v, acc[t][:, half * BANK:(half + 1) * BANK], v, ALU.add).then_inc(h_ok, 1)
                added[0] += len(halves)
                dve.wait_ge(h_ok, added[0])

            def rope_window(buf, heads, t, signal):
                v = buf.rearrange("p (a d) -> p a d", d=A_DIM)
                cs = c("a_cos")[:, t * A_ROPE:(t + 1) * A_ROPE].unsqueeze(1).to_broadcast([P, heads, A_ROPE])
                sn = c("a_sin")[:, t * A_ROPE:(t + 1) * A_ROPE]
                half = A_ROPE // 2
                tmp = scratch[:, 0:heads * A_ROPE].rearrange("p (a d) -> p a d", a=heads)
                dve.tensor_tensor(tmp[:, :, 0:half], v[:, :, half:A_ROPE],
                                  sn[:, 0:half].unsqueeze(1).to_broadcast([P, heads, half]), ALU.mult)
                link(dve, "dve", dve.tensor_tensor(
                    tmp[:, :, half:A_ROPE], v[:, :, 0:half],
                    sn[:, half:A_ROPE].unsqueeze(1).to_broadcast([P, heads, half]), ALU.mult))
                link(dve, "dve", dve.tensor_tensor(v[:, :, 0:A_ROPE], v[:, :, 0:A_ROPE], cs, ALU.mult))
                m = dve.tensor_tensor(v[:, :, 0:A_ROPE], v[:, :, 0:A_ROPE], tmp, ALU.add)
                if signal is None:
                    link(dve, "dve", m)
                else:
                    m.then_inc(signal, 1)
                    rotated[0] += 1
                    dve.wait_ge(signal, rotated[0])

            def rope_whole(dst, bank, heads, d, cs, sn, signal, spare=scratch, rows=P):
                if rows == P:
                    v = ps[:, bank, 0:heads * d].rearrange("p (a d) -> p a d", a=heads)
                else:
                    v = mlow[:, 0:heads * d].rearrange("p (a d) -> p a d", a=heads)
                o = dst.rearrange("p (a d) -> p a d", a=heads)
                tmp = spare[0:rows, 0:heads * d].rearrange("p (a d) -> p a d", a=heads)
                half = d // 2
                dve.tensor_tensor(tmp[:, :, 0:half], v[:, :, half:d],
                                  sn[:, 0:half].unsqueeze(1).to_broadcast([rows, heads, half]), ALU.mult)
                dve.tensor_tensor(tmp[:, :, half:d], v[:, :, 0:half],
                                  sn[:, half:d].unsqueeze(1).to_broadcast([rows, heads, half]), ALU.mult)
                m = dve.tensor_tensor(o, v, cs.unsqueeze(1).to_broadcast([rows, heads, d]), ALU.mult)
                if rows == P:
                    free(m)
                else:
                    link(dve, "dve", m)
                m = dve.tensor_tensor(o, o, tmp, ALU.add)
                if signal is None:
                    link(dve, "dve", m)
                else:
                    m.then_inc(signal, 1)
                    rotated[0] += 1
                    dve.wait_ge(signal, rotated[0])

            def meta_sum(dst, bank, a, b):
                return dve.tensor_tensor(dst, ps[0:N_META, bank, a:b], mlow[:, a:b], ALU.add)

            def meta_free(ins):
                mfreed[0] += 1
                ins.then_inc(mtaken_d, 1)
                dve.wait_ge(mtaken_d, mfreed[0])

            def merge(i, n, first=gate_a, second=gate_r, spare=scratch, bank=0, before=0):
                a = first[:, 2 * i:2 * i + 2, :].rearrange("p a q -> p (a q)")
                r = second[:, 2 * i:2 * i + 2, :].rearrange("p a q -> p (a q)")
                dve.wait_ge(blob_used, n)
                if before:
                    free(dve.scalar_tensor_tensor(out=spare[:], in0=r, scalar=1.0, in1=ps[:, (bank + i) % 4, :],
                                                  op0=ALU.add, op1=ALU.mult))
                else:
                    free(dve.tensor_tensor(spare[:], ps[:, (bank + i) % 4, :], r, ALU.mult))
                dve.tensor_tensor(a, spare[:], a, ALU.add).then_inc(mg_ok, 1)
                dve.wait_ge(mg_hi, before + i + 1)
                dve.scalar_tensor_tensor(out=xT_l[:, 2 * i:2 * i + 2, :], in0=first[:, 2 * i:2 * i + 2, :],
                                         scalar=0.5 if before else 1.0, in1=xT_h[:, 2 * i:2 * i + 2, :],
                                         op0=ALU.mult, op1=ALU.subtract).then_inc(mg_lo, 1)

            def softmax_front(j):
                dve.wait_ge(sc_ps, j + 1)
                if j >= 2:
                    dve.wait_ge(pt_ps, j - 1)
                st = soft[:, j % 2]
                m1 = cst[:, CONST["gt"][0]:CONST["gt"][0] + 2 * P]
                for u in range(2):
                    dve.tensor_tensor_reduce(out=s1[j % 2][:, u, :], in0=ps[:, 4, u * TOK:(u + 1) * TOK], in1=m1,
                                             scale=A_DIM ** -0.5, scalar=NEG, op0=ALU.add, op1=ALU.max,
                                             accum_out=st[:, 0, u:u + 1])
                for u in range(2):
                    m = dve.tensor_tensor_reduce(out=s0[j % 2][:, u, :], in0=ps[:, 5, u * P:(u + 1) * P],
                                                 in1=c("diag1"), scale=A_DIM ** -0.5, scalar=NEG, op0=ALU.add,
                                                 op1=ALU.max, accum_out=st[:, 0, 2 + u:3 + u])
                link(dve, "dve", m)
                link(dve, "dve", dve.scalar_tensor_tensor(out=st[:, 1, :], in0=st[:, 0, :], scalar=-1.0,
                                                          in1=negsink[:, 4 * j:4 * j + 4], op0=ALU.mult, op1=ALU.min))
                dve.tensor_tensor(st[:, 2, :], st[:, 1, :], negsink[:, 4 * j:4 * j + 4],
                                  ALU.subtract).then_inc(sc_ok, 1)

            def softmax_back(j):
                dve.wait_ge(ex_ok, j + 1)
                st = soft[:, j % 2]
                link(dve, "dve", dve.tensor_tensor(st[:, 3, :], st[:, 3, :], st[:, 2, :], ALU.add))
                link(dve, "dve", dve.reciprocal(st[:, 4, :], st[:, 3, :]))
                for u in range(2):
                    dve.tensor_scalar(s1[j % 2][:, u, :], s1[j % 2][:, u, :], st[:, 4, u:u + 1], None, ALU.mult)
                for u in range(2):
                    m = dve.tensor_scalar(s0[j % 2][:, u, :], s0[j % 2][:, u, :], st[:, 4, 2 + u:3 + u], None, ALU.mult)
                m.then_inc(pr_ok, 1)

            def step_lambda():
                a = ROWS["lambdas"][0]
                for v in range(2):
                    m = dve.tensor_tensor_reduce(
                        out=scratch2[:, v * DH:(v + 1) * DH], in0=row[:, a + 2 * v * DH:a + (2 * v + 1) * DH],
                        in1=row[:, a + (2 * v + 1) * DH:a + (2 * v + 2) * DH], scale=1.0, scalar=0.0, op0=ALU.mult,
                        op1=ALU.add, accum_out=lam[:, v:v + 1])
                m.then_inc(lam_s, 1)
                dve.tensor_scalar(subgain[:], cl("subln"), 1.0 - LAMBDA, None, ALU.mult)
                dve.tensor_scalar(halfb[:], cl("b_gate_2", 0, 2 * KC), 0.5, None, ALU.mult)
                dve.wait_ge(lam_e, 1)
                dve.scalar_tensor_tensor(out=neglam[:], in0=lam[:, 3:4], scalar=-LAMBDA, in1=lam[:, 2:3],
                                         op0=ALU.add, op1=ALU.subtract).then_inc(lam_ok, 1)

            def unit_front(U):
                dve.wait_ge(u_sc, U + 1)
                if U >= 2:
                    dve.wait_ge(u_pt, U - 1)
                st, s = usoft[:, U % 4], sc[U % 2]
                if U < S_UNITS:
                    a = CONST["ge" if U % 2 else "zero"][0]
                    mask = cst[:, a:a + TOK]
                else:
                    mask = None
                for u in range(2):
                    for part, (src, a, b) in enumerate(((ps[:, 4, u * TOK:(u + 1) * TOK], 0, TOK),
                                                        (ps[:, 5, u * N_META:(u + 1) * N_META], TOK, KEYS))):
                        if part == 0 and mask is not None:
                            add = mask
                        elif part == 0:
                            add = c("zero").unsqueeze(1).to_broadcast([P, 2, P])
                            src = src.rearrange("p (a k) -> p a k", a=2)
                        else:
                            add = c("zero")[:, 0:N_META]
                        o = s[:, u, a:b]
                        if part == 0 and mask is None:
                            o = o.rearrange("p (a k) -> p a k", a=2)
                        m = dve.tensor_tensor_reduce(out=o, in0=src, in1=add, scale=DH ** -0.5, scalar=NEG,
                                                     op0=ALU.add, op1=ALU.max, accum_out=st[:, part, u:u + 1])
                link(dve, "dve", m)
                link(dve, "dve", dve.tensor_tensor(st[:, 0, :], st[:, 0, :], st[:, 1, :], ALU.max))
                if U < S_UNITS:
                    sink = negsink[:, 2 * A_HEADS + U // 2 * 2:2 * A_HEADS + U // 2 * 2 + 2]
                    link(dve, "dve", dve.scalar_tensor_tensor(out=st[:, 2, :], in0=st[:, 0, :], scalar=-1.0, in1=sink,
                                                              op0=ALU.mult, op1=ALU.min))
                    dve.tensor_tensor(st[:, 3, :], st[:, 2, :], sink, ALU.subtract).then_inc(u_max, 1)
                else:
                    dve.tensor_scalar(st[:, 2, :], st[:, 0, :], -1.0, None, ALU.mult).then_inc(u_max, 1)

            def unit_back(U):
                dve.wait_ge(u_exp, U + 1)
                st, s = usoft[:, U % 4], sc[U % 2]
                if U < S_UNITS:
                    link(dve, "dve", dve.tensor_tensor(st[:, 4, :], st[:, 4, :], st[:, 3, :], ALU.add))
                ins = dve.reciprocal(st[:, 5, :], st[:, 4, :])
                if U >= S_UNITS:
                    link(dve, "dve", ins)
                    dve.tensor_tensor(st[:, 5, 1:2], st[:, 5, 1:2], neglam[:], ALU.mult)
                    link(dve, "dve", dve.tensor_scalar(s[:, 0, :], s[:, 0, :], st[:, 5, 0:1], None, ALU.mult))
                    ins = dve.scalar_tensor_tensor(out=s[:, 0, :], in0=s[:, 1, :], scalar=st[:, 5, 1:2],
                                                   in1=s[:, 0, :], op0=ALU.mult, op1=ALU.add)
                ins.then_inc(u_pr, 1)

            dve.memset(kaT[:], 0.0).then_inc(init_ok, 1)
            dve.memset(va[:], 0.0).then_inc(init_ok, 1)
            for t in range(NT):
                dve.wait_ge(x_in[t], 16)
                square(t)
                normalise(t)
            dve.wait_ge(col_in, 16)
            dve.wait_ge(first_hi, 1)
            dve.tensor_tensor(wlo[0][:, 0:BLOB // 2], raw[0][:, 0:BLOB // 2], whi[0][:, 0:BLOB // 2],
                              ALU.subtract).then_inc(first_lo, 1)
            for t in range(NT):
                to_features(0, "norm_mix", t)
            dve.wait_ge(split_hi, 1)
            dve.tensor_tensor(wlo[0][:, BLOB // 2:BLOB], raw[0][:, BLOB // 2:BLOB], whi[0][:, BLOB // 2:BLOB],
                              ALU.subtract).then_inc(split_lo, 1)
            for n in range(1, 3):
                lo(n)

            for n in range(MIX1):
                if n == 2:
                    dve.wait_ge(const_in, 32)
                    dve.tensor_scalar(negsink[:], row[:, 0:2 * A_HEADS + S_HEADS], -1.0, None, ALU.mult)
                    dve.wait_ge(taken_a, 2)
                    rope_window(tok[0][:, 0, :], A_HEADS, 0, None)
                    rope_window(tok[0][:, 1, :], A_HEADS, 1, rope_ok)
                if n == 3:
                    dve.wait_ge(taken_a, 4)
                    rope_window(ka_tok[:, 0, :], 2, 0, None)
                    rope_window(ka_tok[:, 1, :], 2, 1, rope_ok)
                if n in (5, 7):
                    dve.wait_ge(blob_used, n)
                    if n == 7:
                        dve.wait_ge(q_ps, 1)
                    for t in range(NT):
                        rope_whole(tok[1 if n == 5 else 0][:, t, :], (n - 5) + t, R_HEADS, R_KEY,
                                   c("ret_cos")[:, t * P:(t + 1) * P], c("ret_sin")[:, t * P:(t + 1) * P],
                                   rope_ok if t == 1 else None)
                if 12 <= n < 16:
                    j = n - 12
                    dve.wait_ge(pt_ps, j + 1)
                    dve.tensor_copy(pT[:, 0:4, :], ps[:, 6, :].rearrange("p (a q) -> p a q", a=4)).then_inc(pt_d, 1)
                if 13 <= n < 17:
                    j = n - 13
                    dve.wait_ge(o_hi, j + 1)
                    dve.wait_ge(pt_a, min(4, j + 2))
                    dve.tensor_tensor(aT_l[:, j, :], ps[:, 7, TOK:2 * TOK], aT_h[:, j, :],
                                      ALU.subtract).then_inc(o_lo, 1)
                if 11 <= n < 15:
                    softmax_back(n - 11)
                if 10 <= n < 14:
                    softmax_front(n - 10)
                if n in (13, 15):
                    hh = n - 13
                    v = gr[:, hh:hh + 2]
                    for t in range(NT):
                        dve.wait_ge(e_ok, 2 * (hh // 2) + t + 1)
                        free(dve.tensor_tensor(v[:, :, t, :], ps[:, (n - 13) + t, :].rearrange("p (a v) -> p a v", a=2),
                                               v[:, :, t, :], ALU.mult))
                if 18 <= n < 22:
                    r = n - 18
                    dve.wait_ge(rt_hi, 2 * r + 2)
                    for j in range(2):
                        dve.scalar_tensor_tensor(out=retT_l[:, 2 * r + j, :], in0=ps[:, 6, j * TOK:(j + 1) * TOK],
                                                 scalar=cl("ret_gn", 2 * r + j), in1=retT_h[:, 2 * r + j, :],
                                                 op0=ALU.mult, op1=ALU.subtract).then_inc(rt_lo, 1)
                if 16 <= n < 20:
                    r = n - 16
                    b = r % 2
                    dve.wait_ge(ro_ps, r + 1)
                    for t in range(NT):
                        m = dve.bn_stats(gn_stat[:, b, t, :], ps[:, 5, t * TOK:(t + 1) * TOK])
                    link(dve, "dve", m)
                    for t in range(NT):
                        m = dve.bn_aggr(gn_mv[:, b, t, :], gn_stat[:, b, t, :])
                    m.then_inc(rv_ok, 1)
                    dve.wait_ge(rv_ok, r + 1)
                    for t in range(NT):
                        m = dve.scalar_tensor_tensor(out=gr[:, r, t, :], in0=ps[:, 5, t * TOK:(t + 1) * TOK],
                                                     scalar=gn_mv[:, b, t, 0:1], in1=gr[:, r, t, :],
                                                     op0=ALU.subtract, op1=ALU.mult)
                    link(dve, "dve", m)
                    dve.wait_ge(rr_ok, r + 1)
                    for t in range(NT):
                        m = dve.tensor_scalar(gr[:, r, t, :], gr[:, r, t, :], gn_r[:, b, t:t + 1], None, ALU.mult)
                    m.then_inc(rn_ok, 1)
                if 15 <= n < 19:
                    r = n - 15
                    dve.wait_ge(at_ps, r + 1)
                    if r:
                        dve.wait_ge(ro_ps, r)
                    dve.tensor_tensor(decayed[:], ps[:, 4, 0:3 * P], c("decay")[:, r * 3 * P:(r + 1) * 3 * P],
                                      ALU.mult).then_inc(at_ok, 1)
                if n in (24, 25):
                    v = gate_a[:, 4 * (n - 24):4 * (n - 24) + 4, :].rearrange("p a q -> p (a q)")
                    dve.wait_ge(blob_used, n)
                    for b in range(2):
                        free(dve.tensor_tensor(v[:, b * BANK:(b + 1) * BANK], ps[:, 2 * (n - 24) + b, :],
                                               v[:, b * BANK:(b + 1) * BANK], ALU.mult))
                if 26 <= n < 30:
                    merge(n - 26, n)
                if n < MIX1 - 1:
                    lo(n + 3)
            add_product(0, 1, MIX1)
            square(0)
            normalise(0)
            add_product(1, 1, MIX1, (0,))
            to_features(1, "norm_mlp", 0, range(0, 4))
            add_product(1, 1, MIX1, (1,))
            square(1)
            to_features(1, "norm_mlp", 0, range(4, KC))
            normalise(1)
            to_features(1, "norm_mlp", 1)
            lo(MIX1 + 2)

            def hidden_square(k, count):
                dve.wait_ge(ff_relu, count)
                dve.tensor_tensor(f_sq[k][:], f_sq[k][:], f_sq[k][:], ALU.mult).then_inc(ff_sq, 1)

            def hidden_lo(k, count):
                dve.wait_ge(ff_hi, count)
                dve.tensor_tensor(fT_l[k][:], f_sq[k][:], fT_h[k][:], ALU.subtract).then_inc(ff_lo, 1)

            b = MIX1
            lo(b + 3)
            lo(b + 4)
            hidden_square(0, 1)
            hidden_square(1, 2)
            hidden_lo(0, 1)
            with dve.Fori(0, STEP1 - 1) as i:
                b = MIX1 + 2
                lo(b + 3, i, 4)
                hidden_lo(1, i * 2 + 2)
                lo(b + 4, i, 4)
                hidden_square(0, i * 2 + 3)
                lo(b + 5, i, 4)
                hidden_square(1, i * 2 + 4)
                lo(b + 6, i, 4)
                hidden_lo(0, i * 2 + 3)
            b = N1 - 2
            hidden_lo(1, 2 * STEP1)
            lo(b + 3)
            dve.wait_ge(meta_ps, 1)
            dve.tensor_tensor(metaT[:], ps[:, 2, 0:KC * N_META].rearrange("p (a q) -> p a q", a=KC),
                              cl("pre_mix", 0, KC).unsqueeze(2).to_broadcast([P, KC, N_META]),
                              ALU.mult).then_inc(meta_g, 1)
            dve.wait_ge(meta_hi, 1)
            dve.tensor_tensor(metaT_hl[:, :, 2 * N_META:3 * N_META], metaT[:], metaT_hl[:, :, 0:N_META],
                              ALU.subtract).then_inc(meta_lo, 1)
            dve.wait_ge(row_in, 16)
            for t in range(NT):
                if t == 0:
                    add_product(0, 2, N1)
                square(t)
                dve.wait_ge(rstd_ok, norms[0])
                for half in range(2):
                    v = h[:, t, half * BANK:(half + 1) * BANK]
                    dve.scalar_tensor_tensor(out=v, in0=v, scalar=stat[:, t, 3:4],
                                             in1=gain_row[:, half * BANK:(half + 1) * BANK], op0=ALU.mult,
                                             op1=ALU.mult).then_inc(h_ok, 1)
                added[0] += 2
                dve.wait_ge(h_ok, added[0])
                square(t)
                if t == 0:
                    add_product(1, 2, N1)
                normalise(t)
            for t in range(NT):
                to_features(2, "pre_mix", t)
            lo(N1 + 2)

            for q in range(2 * OUT2):
                m2 = q // 2
                if q == 1:
                    step_lambda()
                if q in (20, 24):
                    half = (q - 20) // 4
                    dve.wait_ge(mlow_ok, 4 + half)
                    meta_free(meta_sum(vb_meta[:, half * BANK:(half + 1) * BANK], 7 - half, 0, BANK))
                U = q - U0 - 3
                if 0 <= U < UNITS:
                    dve.wait_ge(u_pt, U + 1)
                    if U:
                        dve.wait_ge(u_o, U)
                    n = 4 if U < S_UNITS else 2
                    dve.tensor_copy(puT[:, 0:n, :], ps[:, 6, 0:n * P].rearrange("p (a q) -> p a q", a=n)).then_inc(
                        u_ptd, 1)
                U = q - U0 - 7
                if 0 <= U < UNITS:
                    cc, t = U % S_UNITS // 2, U % 2
                    dve.wait_ge(d_hi, U + 1)
                    if U < S_UNITS:
                        dve.tensor_tensor(sT_l[:, cc, t * P:(t + 1) * P], ps[:, 5, P:2 * P],
                                          sT_h[:, cc, t * P:(t + 1) * P], ALU.subtract).then_inc(d_lo, 1)
                    else:
                        dve.scalar_tensor_tensor(out=dT_l[:, cc, t * P:(t + 1) * P], in0=ps[:, 5, P:2 * P],
                                                 scalar=subgain[:], in1=dT_h[:, cc, t * P:(t + 1) * P],
                                                 op0=ALU.mult, op1=ALU.subtract).then_inc(d_lo, 1)
                U = q - U0 - 1
                if 0 <= U < UNITS:
                    unit_front(U)
                if q % 2 == 1 and 1 <= m2 and m2 < OUT2:
                    lo(N1 + m2 + 2)
                if 0 <= U < UNITS:
                    unit_back(U)
                if q in (4, 8, 12, 16, 28, 32, 36):
                    r = (4, 8, 12, 16, 28, 32, 36).index(q)
                    g = (0, 1, 2, 3, 6, 7, 8)[r]
                    dve.wait_ge(blob_used, N1 + m2)
                    if r == 0:
                        dve.wait_ge(sv_ok, 1)
                        dst, heads = ks_tok, S_KV
                    else:
                        dst, heads = tok2[(0, 1, 0, 1, 0, 1)[r - 1]], F_HEADS
                    if r in (2, 3, 4):
                        dve.wait_ge(kt_ps, {2: 1, 3: 3, 4: 5}[r])
                    if r in (5, 6):
                        dve.wait_ge(q_ps, r)
                    for t in range(NT + 1 if r < 3 else NT):
                        cs, sn = (c(name)[:, t * DH:(t + 1) * DH] for name in ("h_cos", "h_sin"))
                        if t < NT:
                            last = t == NT - 1 and r >= 3
                            rope_whole(dst[:, t, :], 2 * (g % 2) + t, heads, DH, cs, sn, rope_ok if last else None,
                                       scratch2)
                        else:
                            dve.wait_ge(mlow_ok, r + 1)
                            if r == 0:
                                meta_sum(vs_meta[:], 6, 256, 512)
                            meta_free(meta_sum(mlow[:, 0:heads * DH], 6 + r % 2, 0, heads * DH))
                            rope_whole(mk[r % 2][:, 0:heads * DH], 6 + r % 2, heads, DH, cs[0:N_META],
                                       sn[0:N_META], rope_ok, scratch2, N_META)
                if q in (56, 60):
                    g = (q - 56) // 4
                    dve.wait_ge(blob_used, N1 + m2)
                    for b in range(2):
                        v = gate_s[:, 4 * g + 2 * b:4 * g + 2 * b + 2, :].rearrange("p a q -> p (a q)")
                        free(dve.scalar_tensor_tensor(out=v, in0=v, scalar=1.0, in1=ps[:, (2 + 2 * g + b) % 4, :],
                                                      op0=ALU.add, op1=ALU.mult))
                if q % 2 == 0 and m2 > OUT2 - 4:
                    merge(m2 - (OUT2 - 3), N1 + m2, gate_s, gate_d, scratch2, 2, 4)
            for m2 in range(OUT2, MIX2 - 1):
                if m2 == OUT2:
                    merge(3, N1 + OUT2, gate_s, gate_d, scratch2, 2, 4)
                lo(N1 + m2 + 2)

            squared = [0]

            def times_gain(t, k):
                for half in range(2):
                    a = half * BANK
                    squared[0] += 1
                    dve.wait_ge(acc_a, squared[0])
                    m = dve.tensor_tensor(ag[:, t, a:a + BANK], acc[t][:, a:a + BANK], gain_rows[:, k, a:a + BANK],
                                          ALU.mult)
                link(dve, "dve", m)

            def add_normalised(t):
                norms[0] += 1
                dve.wait_ge(rstd_ok, norms[0])
                for half in range(2):
                    v = h[:, t, half * BANK:(half + 1) * BANK]
                    dve.scalar_tensor_tensor(out=v, in0=ag[:, t, half * BANK:(half + 1) * BANK],
                                             scalar=stat[:, t, 3:4], in1=v, op0=ALU.mult,
                                             op1=ALU.add).then_inc(h_ok, 1)
                added[0] += 2
                dve.wait_ge(h_ok, added[0])

            dve.wait_ge(rows_in, 16)
            for t in range(NT):
                if t == 0:
                    times_gain(0, 0)
                add_normalised(t)
                square(t)
                if t == 0:
                    times_gain(1, 0)
                normalise(t)
            for t in range(NT):
                to_features(3, "pre_ffn", t)
            lo(F2 + 1)
            lo(F2 + 2)

            def gate_product(made):
                dve.wait_ge(gs_ok, made)
                v = g_act[:].rearrange("p a q -> p (a q)")
                dve.tensor_tensor(v, ps[:, 0, :], v, ALU.mult).then_inc(g_one, 1)

            def up_product(made, used):
                dve.wait_ge(g_one, made)
                dve.wait_ge(blob_used, used)
                v = g_act[:].rearrange("p a q -> p (a q)")
                dve.tensor_tensor(v, ps[:, 1, :], v, ALU.mult).then_inc(g_two, 1)

            def hidden2_lo(made, low=gT_l, high=gT_h):
                dve.wait_ge(g_hi, made)
                dve.tensor_tensor(low[:], g_act[:], high[:], ALU.subtract).then_inc(g_lo, 1)

            lo(F2 + 3)
            gate_product(1)
            up_product(1, F2 + 2)
            lo(F2 + 4)
            hidden2_lo(1)
            with dve.Fori(0, STEP2 - 2) as i:
                lo(F2 + 5, i, 3)
                gate_product(i + 2)
                lo(F2 + 6, i, 3)
                up_product(i + 2, i * 3 + (F2 + 4))
                lo(F2 + 7, i, 3)
                hidden2_lo(i + 2)
            lo(NBLOB - 1)
            gate_product(STEP2)
            up_product(STEP2, F2 + 3 * STEP2 - 2)
            hidden2_lo(STEP2, gL_l, gL_h)
            for t in range(NT):
                times_gain(t, 1)
                add_normalised(t)



def blob_tokens(w, c0, width=BANK):
    nk = BLOB // width
    v = w[:, c0:c0 + width].reshape(-1, nk, P, width)
    return [v[i].transpose(1, 0, 2).reshape(P, BLOB) for i in range(v.shape[0])]


def head_pairs(w, first, axis):
    n = w.shape[axis] // DH
    order = [8 * p + 4 * u + a for p in range(n // 8) for a in range(4) for u in range(2)]
    v = np.moveaxis(w, axis, 0).reshape((n, DH) + tuple(np.delete(w.shape, axis)))
    return np.moveaxis(v[order].reshape((n * DH,) + v.shape[2:]), 0, axis)


def weight_stream(i):
    w = np.asarray(i["w_in"])[0]
    at = np.cumsum([0, 512, 128, 128, 512, 512, 1024, 1024, 1024, 1024])
    out = []
    out += blob_tokens(head_pairs(w[:, 0:512], 0, 1), 0)
    out += blob_tokens(w, at[1], 256)
    for a in range(3, 5):
        out += blob_tokens(w, at[a])
    for a in range(5, 7):
        out += blob_tokens(w, at[a]) + blob_tokens(w, at[a] + BANK)
    for a in range(7, 9):
        for q in range(4):
            out += blob_tokens(w, at[a] + 256 * q, 256)
    att = head_pairs(np.asarray(i["w_att_up"])[0], 0, 0)
    out += blob_tokens(att, 0) + blob_tokens(att, BANK)
    up = np.asarray(i["w_ret_up"])[0]
    for q in range(4):
        out += blob_tokens(up, 256 * q, 256)
    out += blob_tokens(np.asarray(i["w_out"])[0], 0, D)
    ff1, ff2 = np.asarray(i["w_ff1"])[0], np.asarray(i["w_ff2"])[0]
    down = blob_tokens(ff2, 0, D)
    for j in range(STEP1):
        out += blob_tokens(ff1, 512 * j, 256) + blob_tokens(ff1, 512 * j + 256, 256)
        if j:
            out += down[2 * j - 2:2 * j]
    out += down[-2:]
    assert len(out) == N1

    w = np.asarray(i["w_in_2"])[0]
    at = np.cumsum([0, 1024, 256, 256, 1024, 1024, 1024])
    qa = head_pairs(w[:, 0:1024], 0, 1)
    out += blob_tokens(w, at[1])
    out += blob_tokens(w, at[4]) + blob_tokens(w, at[4] + BANK)
    out += blob_tokens(qa, 0)
    out += blob_tokens(w, at[5]) + blob_tokens(w, at[5] + BANK)
    out += blob_tokens(qa, BANK)
    out += blob_tokens(w, at[3]) + blob_tokens(w, at[3] + BANK)
    for q in range(8):
        out += blob_tokens(w, at[6] + 256 * q, 256)
    for up in (head_pairs(np.asarray(i["w_branch_swa_2"])[0], 0, 0), np.asarray(i["w_branch_diff_2"])[0]):
        for q in range(4):
            out += blob_tokens(up, 256 * q, 256)
    out += blob_tokens(np.asarray(i["w_out_2"])[0], 0, D)
    assert len(out) == F2
    up, down = np.asarray(i["w_ffn_in_2"])[0], blob_tokens(np.asarray(i["w_ffn_out_2"])[0], 0, D)
    for j in range(STEP2):
        out += blob_tokens(up, 256 * j, 256) + blob_tokens(up, FF2 + 256 * j, 256)
        if j:
            out += down[j - 1:j]
    out += down[-1:]
    assert len(out) == NBLOB
    return out


def constants():
    out = np.zeros((P, NCONST), np.float32)

    def put(name, v):
        a, n = CONST[name]
        out[:v.shape[0], a:a + n] = v.reshape(v.shape[0], n)

    f = np.float32
    q, k = np.arange(P)[:, None], np.arange(P)[None, :]
    put("ident", np.eye(P, dtype=f))
    put("gt", np.where(k > q, 0, NEG))
    put("diag1", np.where(k <= q, 0, NEG))
    put("ge", np.where(k >= q, 0, NEG))
    put("diag2", np.where(k <= q, 0, NEG))
    lg = np.log1p(-np.exp2(-5.0 - np.arange(R_HEADS)))
    dec = np.zeros((P, R_HEADS, 3, P))
    kk, qq = np.arange(P)[:, None], np.arange(P)[None, :]
    for r in range(R_HEADS):
        dec[:, r, 0] = np.where(qq >= kk, np.exp(np.maximum(qq - kk, 0) * lg[r]), 0)
        dec[:, r, 1] = np.exp((P + qq - kk) * lg[r])
        dec[:, r, 2] = dec[:, r, 0]
    put("decay", dec * R_KEY ** -0.5)

    def rope(pos, dim, theta):
        inv = f(theta) ** (-np.arange(0, dim, 2, dtype=f) / f(dim))
        ang = pos.astype(f)[:, None] * inv[None, :].astype(f)
        cs, sn = np.cos(ang.astype(np.float64)), np.sin(ang.astype(np.float64))
        return np.concatenate([cs, cs], 1), np.concatenate([-sn, sn], 1)

    for name, dim, theta in (("a", A_ROPE, 500000.0), ("ret", R_KEY, 10000.0)):
        for part, v in zip(("_cos", "_sin"), rope(np.arange(TOK), dim, theta)):
            put(name + part, v.reshape(NT, P, dim).transpose(1, 0, 2).copy())
    for part, v in zip(("_cos", "_sin"), rope(np.arange(KEYS), DH, 10000.0)):
        a, n = CONST["h" + part]
        t = out[:, a:a + n].reshape(P, NT + 1, DH)
        t[:, 0:NT] = v[N_META:].reshape(NT, P, DH).transpose(1, 0, 2)
        t[:N_META, NT] = v[:N_META]
        out[:, a:a + n] = t.reshape(P, n)
    put("neghalf", np.full((P, 2), -0.5))
    return out


def kernel(**inputs):
    import concourse.bacc as bacc
    from concourse.bass_utils import run_bass_kernel_spmd

    i = {k: np.asarray(v) for k, v in inputs.items()}
    x = i["x"][0].reshape(NT, P, D).transpose(1, 0, 2)
    cols = np.zeros((P, NCOLS), np.float32)
    for name, key in (("norm_mix", "norm_mix_gain"), ("norm_mlp", "norm_mlp_gain"), ("ret_gn", "ret_gn_gain"),
                      ("b_gates", "b_gates"), ("pre_mix", "pre_mix_gain_2"), ("b_gate_2", "b_gate_2"),
                      ("pre_ffn", "pre_ffn_gain_2"), ("subln", "diff_subln_gain_2")):
        a, n = COLS[name]
        cols[:, a:a + n] = i[key].reshape(n, P).T
    s = i["attn_sinks"][0]
    s2 = i["attn_sink_2"][0]
    rows = np.concatenate(
        [np.concatenate([s[[j, j + 4, j, j + 4]] for j in range(4)]),
         s2[[8 * p + 4 * u + a for p in range(2) for a in range(4) for u in range(2)]],
         i["lambda_q1_2"][0], i["lambda_k1_2"][0], i["lambda_q2_2"][0], i["lambda_k2_2"][0]])
    grow = np.stack([i["norm_final_gain"], i["post_mix_gain_2"][0], i["post_ffn_gain_2"][0]])
    arrays = {
        "weights": np.stack(weight_stream(i)),
        "x_tiles": x,
        "meta": i["meta_tokens_2"],
        "consts": constants(),
        "cols": cols,
        "rows": rows,
        "gain_rows": grow,
    }
    arrays = {k: np.ascontiguousarray(v) for k, v in arrays.items()}
    nc = bacc.Bacc("TRN2", target_bir_lowering=False, num_devices=1)
    args = [nc.dram_tensor(k, v.shape, mybir.dt.from_np(v.dtype), kind="ExternalInput").ap() for k, v in arrays.items()]
    y = nc.dram_tensor("y", (P, NT, D), F32, kind="ExternalOutput").ap()
    build(nc, *args, y)
    r = run_bass_kernel_spmd(nc, [arrays], core_ids=[0])
    return r.results[0]["y"].transpose(1, 0, 2).reshape(1, TOK, D)
```
